# Optimizing a Trainium2 kernel written in Bass

```python
import math, functools
import jax, jax.numpy as jnp
from jax import lax
import numpy as np

D_MODEL = 1024
BATCH = 1
SEQ = 128
DEPTH = 2
DEC_BATCH = 1
DEC_SEQ = 512
PAST_LEN = 128

GRID_W = 64
MIX_WIDTH = D_MODEL
CONV_CH = D_MODEL // 4
HYENA_CH = D_MODEL // 4
FOURIER_CH = D_MODEL // 4
HEAD_DIM = 64
N_Q_HEADS = (D_MODEL // 4) // HEAD_DIM
N_KV_HEADS = N_Q_HEADS // 2
Q_PER_KV = N_Q_HEADS // N_KV_HEADS
ATT_CH = N_Q_HEADS * HEAD_DIM
IN_COLS = 2 * CONV_CH + 3 * HYENA_CH + FOURIER_CH + (N_Q_HEADS + 2 * N_KV_HEADS) * HEAD_DIM
CONV_WIDTH = 31
SHORT_WIDTH = 3
HYENA_ORDER = 2
HYENA_EMB = 33
HYENA_FFN = 64
HYENA_DECAY_TARGET = 1e-2
HYENA_FAST_PCT = 0.3
HYENA_SLOW_PCT = 1.5
HYENA_SHIFT = 0.05
WINDOW = 128
ATT_BLOCK = 128
ROPE_BASE = 10000.0
N_GROUPS = 4
EXPERTS_PER_GROUP = 8
N_EXPERTS = N_GROUPS * EXPERTS_PER_GROUP
TOP_K = 2
D_EXPERT = 256
MOE_BLOCK = 256
N_MOD = 6
EPS = 1e-6
NEG_INF = -1e30

kernel_name = "hybrid_prefix_diffusion_trunk_step"

def rmsnorm(x, g):
    xf = x.astype(jnp.float32)
    y = xf * lax.rsqrt(jnp.mean(xf * xf, axis=-1, keepdims=True) + EPS)
    return (y * g.astype(jnp.float32)).astype(x.dtype)

def adaln(cvec, w, b):
    m = jax.nn.silu(cvec) @ w + b
    return [part[:, None, :] for part in jnp.split(m, N_MOD, axis=-1)]

def depthwise_conv(x, w, b):
    K, C = w.shape
    p = (K - 1) // 2
    y = lax.conv_general_dilated(x, w[:, None, :].astype(x.dtype), (1,), [(p, p)],
                                 dimension_numbers=('NWC', 'WIO', 'NWC'), feature_group_count=C)
    return y + b.astype(x.dtype)

def axial_rope_tables(L):
    rows = L // GRID_W
    row_pos = jnp.repeat(jnp.arange(rows, dtype=jnp.float32), GRID_W)
    col_pos = jnp.tile(jnp.arange(GRID_W, dtype=jnp.float32), rows)
    n_freq = HEAD_DIM // 4
    inv = ROPE_BASE ** (-jnp.arange(n_freq, dtype=jnp.float32) / n_freq)
    ang = jnp.concatenate([row_pos[:, None] * inv, col_pos[:, None] * inv], axis=-1)
    return jnp.cos(ang), jnp.sin(ang)

def apply_rope(x, cos, sin):
    x1, x2 = jnp.split(x, 2, axis=-1)
    c = cos[None, :, None, :].astype(x.dtype)
    s = sin[None, :, None, :].astype(x.dtype)
    return jnp.concatenate([x1 * c - x2 * s, x1 * s + x2 * c], axis=-1)

def conformer_conv(u, dw_w, dw_b, ln_g, ln_b):
    a, g = jnp.split(u, 2, axis=-1)
    z = depthwise_conv(a * jax.nn.sigmoid(g), dw_w, dw_b).astype(jnp.float32)
    mu = jnp.mean(z, axis=-1, keepdims=True)
    var = jnp.mean(jnp.square(z - mu), axis=-1, keepdims=True)
    zn = (z - mu) * lax.rsqrt(var + EPS) * ln_g.astype(jnp.float32) + ln_b.astype(jnp.float32)
    return jax.nn.silu(zn).astype(u.dtype)

def hyena_kernel_fft(L, fw1, fb1, fr1, fw2, fb2, fr2, fw3, fb3):
    f = lambda a: a.astype(jnp.float32)
    t = jnp.linspace(0.0, 1.0, L, dtype=jnp.float32)[:, None]
    n_bands = (HYENA_EMB - 1) // 2
    w = 2.0 * math.pi * jnp.arange(L, dtype=jnp.float32)[:, None] / L
    fr = jnp.linspace(1e-4, n_bands - 1, n_bands, dtype=jnp.float32)[None, :]
    z = jnp.concatenate([t, jnp.cos(fr * w), -jnp.sin(fr * w)], axis=-1)
    h = jnp.sin(f(fr1) * (z @ f(fw1) + f(fb1)))
    h = jnp.sin(f(fr2) * (h @ f(fw2) + f(fb2)))
    h = (h @ f(fw3) + f(fb3)).reshape(L, 2, HYENA_ORDER, HYENA_CH)
    max_decay = math.log(HYENA_DECAY_TARGET) / HYENA_FAST_PCT
    min_decay = math.log(HYENA_DECAY_TARGET) / HYENA_SLOW_PCT
    deltas = jnp.linspace(min_decay, max_decay, HYENA_CH, dtype=jnp.float32)
    window = jnp.exp(-t * jnp.abs(deltas)[None, :]) + HYENA_SHIFT
    h = h * window[:, None, None, :]
    hf, hb = h[:, 0], h[:, 1]
    k = jnp.concatenate([hf[:1] + hb[:1], hf[1:], jnp.zeros_like(hf[:1]), hb[:0:-1]], axis=0)
    k = k / (jnp.sum(jnp.abs(k), axis=0, keepdims=True) + EPS)
    return jnp.fft.rfft(k, axis=0)

def hyena(u, short_w, short_b, kf, hy_d):
    L = u.shape[1]
    u = depthwise_conv(u, short_w, short_b)
    v, x1, x2 = jnp.split(u, 3, axis=-1)
    z = v.astype(jnp.float32)
    for o, gate in enumerate((x1, x2)):
        zf = jnp.fft.rfft(z, n=2 * L, axis=1)
        y = jnp.fft.irfft(zf * kf[None, :, o, :], n=2 * L, axis=1)[:, :L]
        z = gate.astype(jnp.float32) * (y + hy_d[o].astype(jnp.float32) * z)
    return z.astype(u.dtype)

def fourier_mix(u):
    return jnp.fft.fft2(u.astype(jnp.float32), axes=(1, 2), norm='ortho').real.astype(u.dtype)

def context_attention(q, k, v, sink):
    B, S = q.shape[:2]
    scale = HEAD_DIM ** -0.5
    sink_b = jnp.broadcast_to(sink.astype(jnp.float32).reshape(1, N_KV_HEADS, Q_PER_KV, 1, 1),
                              (B, N_KV_HEADS, Q_PER_KV, ATT_BLOCK, 1))

    def block(i):
        qb = lax.dynamic_slice_in_dim(q, i * ATT_BLOCK, ATT_BLOCK, 1).reshape(
            B, ATT_BLOCK, N_KV_HEADS, Q_PER_KV, HEAD_DIM)
        s = jnp.einsum('bqgrd,bkgd->bgrqk', qb, k).astype(jnp.float32) * scale
        p = jax.nn.softmax(jnp.concatenate([s, sink_b], axis=-1), axis=-1)[..., :S]
        o = jnp.einsum('bgrqk,bkgd->bqgrd', p.astype(v.dtype), v)
        return o.reshape(B, ATT_BLOCK, ATT_CH)

    out = lax.map(block, jnp.arange(S // ATT_BLOCK))
    return out.transpose(1, 0, 2, 3).reshape(B, S, ATT_CH)

def latent_attention(q, k, v, ck, cv, sink, cos, sin):
    B, L = q.shape[:2]
    P = ck.shape[1]
    span = ATT_BLOCK + 2 * WINDOW
    scale = HEAD_DIM ** -0.5
    qr = apply_rope(q, cos, sin)
    kr = apply_rope(k, cos, sin)
    pad = ((0, 0), (WINDOW, WINDOW), (0, 0), (0, 0))
    kp = jnp.pad(kr, pad)
    vp = jnp.pad(v, pad)
    sink_b = jnp.broadcast_to(sink.astype(jnp.float32).reshape(1, N_KV_HEADS, Q_PER_KV, 1, 1),
                              (B, N_KV_HEADS, Q_PER_KV, ATT_BLOCK, 1))

    def block(i):
        q0 = i * ATT_BLOCK
        qb = lax.dynamic_slice_in_dim(qr, q0, ATT_BLOCK, 1).reshape(B, ATT_BLOCK, N_KV_HEADS, Q_PER_KV, HEAD_DIM)
        qc = lax.dynamic_slice_in_dim(q, q0, ATT_BLOCK, 1).reshape(B, ATT_BLOCK, N_KV_HEADS, Q_PER_KV, HEAD_DIM)
        kb = lax.dynamic_slice_in_dim(kp, q0, span, 1)
        vb = lax.dynamic_slice_in_dim(vp, q0, span, 1)
        s_loc = jnp.einsum('bqgrd,bkgd->bgrqk', qb, kb).astype(jnp.float32) * scale
        qpos = q0 + jnp.arange(ATT_BLOCK)
        kpos = q0 - WINDOW + jnp.arange(span)
        ok = (jnp.abs(qpos[:, None] - kpos[None, :]) <= WINDOW) & (kpos >= 0)[None, :] & (kpos < L)[None, :]
        s_loc = jnp.where(ok, s_loc, NEG_INF)
        s_ctx = jnp.einsum('bqgrd,bkgd->bgrqk', qc, ck).astype(jnp.float32) * scale
        p = jax.nn.softmax(jnp.concatenate([s_loc, s_ctx, sink_b], axis=-1), axis=-1)
        o = (jnp.einsum('bgrqk,bkgd->bqgrd', p[..., :span].astype(v.dtype), vb)
             + jnp.einsum('bgrqk,bkgd->bqgrd', p[..., span:span + P].astype(cv.dtype), cv))
        return o.reshape(B, ATT_BLOCK, ATT_CH)

    out = lax.map(block, jnp.arange(L // ATT_BLOCK))
    return out.transpose(1, 0, 2, 3).reshape(B, L, ATT_CH)

def token_mixers(h, w_in, dw_w, dw_b, ln_g, ln_b, short_w, short_b, hy_d, w_out, kf, attend):
    B, L, _ = h.shape
    sizes = [2 * CONV_CH, 3 * HYENA_CH, FOURIER_CH, ATT_CH, N_KV_HEADS * HEAD_DIM, N_KV_HEADS * HEAD_DIM]
    u = h @ w_in
    ua, ub, uc, uq, uk, uv = jnp.split(u, np.cumsum(sizes)[:-1].tolist(), axis=-1)
    ya = conformer_conv(ua, dw_w, dw_b, ln_g, ln_b)
    yb = hyena(ub, short_w, short_b, kf, hy_d)
    yc = fourier_mix(uc)
    q = uq.reshape(B, L, N_Q_HEADS, HEAD_DIM)
    k = uk.reshape(B, L, N_KV_HEADS, HEAD_DIM)
    v = uv.reshape(B, L, N_KV_HEADS, HEAD_DIM)
    yd = attend(q, k, v)
    y = jnp.concatenate([ya, yb, yc, yd], axis=-1) @ w_out
    return y, k, v

def hier_moe(h, rc_w, rc_b, rf_w, rf_b, e_gate, e_up, e_down):
    B, L, D = h.shape
    t = h.reshape(-1, D)
    N = t.shape[0]
    rows = jnp.arange(N)
    lc = (t @ rc_w + rc_b).astype(jnp.float32)
    pc = jax.nn.softmax(lc, axis=-1)
    grp = lax.top_k(lc, 1)[1][:, 0]
    pg = pc[rows, grp]
    lf = (t @ rf_w + rf_b).astype(jnp.float32).reshape(N, N_GROUPS, EXPERTS_PER_GROUP)
    top_l, top_i = lax.top_k(lf[rows, grp], TOP_K)
    gw = jax.nn.softmax(top_l, axis=-1) * pg[:, None]
    eid = grp[:, None] * EXPERTS_PER_GROUP + top_i
    A = N * TOP_K
    flat_e = eid.reshape(-1)
    flat_t = jnp.repeat(jnp.arange(N, dtype=jnp.int32), TOP_K)
    flat_w = gw.reshape(-1)
    order = jnp.argsort(flat_e)
    se = flat_e[order]
    counts = jnp.bincount(flat_e, length=N_EXPERTS)
    padded = (counts + MOE_BLOCK - 1) // MOE_BLOCK * MOE_BLOCK
    pend = jnp.cumsum(padded)
    pstart = pend - padded
    start = jnp.cumsum(counts) - counts
    dest = pstart[se] + jnp.arange(A) - start[se]
    nb = -(-A // MOE_BLOCK) + N_EXPERTS
    slot_tok = jnp.zeros((nb * MOE_BLOCK,), jnp.int32).at[dest].set(flat_t[order])
    slot_w = jnp.zeros((nb * MOE_BLOCK,), jnp.float32).at[dest].set(flat_w[order])
    blk_e = jnp.minimum(jnp.searchsorted(pend, jnp.arange(nb) * MOE_BLOCK, side='right'), N_EXPERTS - 1)

    def run(args):
        tok, e = args
        xb = t[tok]
        return (jax.nn.silu(xb @ e_gate[e]) * (xb @ e_up[e])) @ e_down[e]

    yb = lax.map(run, (slot_tok.reshape(nb, MOE_BLOCK), blk_e))
    y = yb.reshape(-1, D) * slot_w[:, None].astype(yb.dtype)
    out = jnp.zeros_like(t).at[slot_tok].add(y)
    return out.reshape(B, L, D)

def trunk_layer(x, mods, n1, n2, mix_p, kf, attend, moe_p):
    sh1, sc1, g1, sh2, sc2, g2 = mods
    h = rmsnorm(x, n1) * (1 + sc1) + sh1
    y, k, v = token_mixers(h, *mix_p, kf, attend)
    x = x + g1 * y
    h = rmsnorm(x, n2) * (1 + sc2) + sh2
    x = x + g2 * hier_moe(h, *moe_p)
    return x, k, v

def setup_inputs(seed: int = 0) -> dict:
    key = jax.random.key(seed)
    ks = iter(jax.random.split(key, 48))
    nrm = lambda shape, scale: jax.random.normal(next(ks), shape, jnp.float32) * scale
    D = D_MODEL
    return {
        "x_prompt": nrm((BATCH, SEQ, D), 1.0),
        "x_sample": nrm((DEC_BATCH, DEC_SEQ, D), 1.0),
        "cache_k": nrm((DEC_BATCH, DEPTH, PAST_LEN, N_KV_HEADS, HEAD_DIM), 1.0),
        "cache_v": nrm((DEC_BATCH, DEPTH, PAST_LEN, N_KV_HEADS, HEAD_DIM), 1.0),
        "c": nrm((DEC_BATCH, D), 1.0),
        "c_ctx": nrm((D,), 1.0),
        "ada_w": nrm((DEPTH, D, N_MOD * D), 0.5 * D ** -0.5),
        "ada_b": nrm((DEPTH, N_MOD * D), 0.02),
        "norm1_g": 1.0 + nrm((DEPTH, D), 0.1),
        "norm2_g": 1.0 + nrm((DEPTH, D), 0.1),
        "w_in": nrm((DEPTH, D, IN_COLS), D ** -0.5),
        "conv_dw_w": nrm((DEPTH, CONV_WIDTH, CONV_CH), CONV_WIDTH ** -0.5),
        "conv_dw_b": nrm((DEPTH, CONV_CH), 0.02),
        "conv_ln_g": 1.0 + nrm((DEPTH, CONV_CH), 0.1),
        "conv_ln_b": nrm((DEPTH, CONV_CH), 0.02),
        "hy_short_w": nrm((DEPTH, SHORT_WIDTH, 3 * HYENA_CH), SHORT_WIDTH ** -0.5),
        "hy_short_b": nrm((DEPTH, 3 * HYENA_CH), 0.02),
        "hy_fw1": nrm((DEPTH, HYENA_EMB, HYENA_FFN), HYENA_EMB ** -0.5),
        "hy_fb1": nrm((DEPTH, HYENA_FFN), 0.02),
        "hy_freq1": 1.0 + nrm((DEPTH, HYENA_FFN), 0.1),
        "hy_fw2": nrm((DEPTH, HYENA_FFN, HYENA_FFN), HYENA_FFN ** -0.5),
        "hy_fb2": nrm((DEPTH, HYENA_FFN), 0.02),
        "hy_freq2": 1.0 + nrm((DEPTH, HYENA_FFN), 0.1),
        "hy_fw3": nrm((DEPTH, HYENA_FFN, 2 * HYENA_ORDER * HYENA_CH), HYENA_FFN ** -0.5),
        "hy_fb3": nrm((DEPTH, 2 * HYENA_ORDER * HYENA_CH), 0.02),
        "hy_d": nrm((DEPTH, HYENA_ORDER, HYENA_CH), 1.0),
        "attn_sink": nrm((DEPTH, N_Q_HEADS), 0.5),
        "w_out": nrm((DEPTH, MIX_WIDTH, D), MIX_WIDTH ** -0.5),
        "router_coarse_w": nrm((DEPTH, D, N_GROUPS), D ** -0.5),
        "router_coarse_b": nrm((DEPTH, N_GROUPS), 0.01),
        "router_fine_w": nrm((DEPTH, D, N_EXPERTS), D ** -0.5),
        "router_fine_b": nrm((DEPTH, N_EXPERTS), 0.01),
        "exp_gate": nrm((DEPTH, N_EXPERTS, D, D_EXPERT), D ** -0.5),
        "exp_up": nrm((DEPTH, N_EXPERTS, D, D_EXPERT), D ** -0.5),
        "exp_down": nrm((DEPTH, N_EXPERTS, D_EXPERT, D), D_EXPERT ** -0.5),
        "norm_f_g": 1.0 + nrm((D,), 0.1),
    }

def reference(x_prompt, x_sample, cache_k, cache_v, c, c_ctx, ada_w, ada_b, norm1_g, norm2_g, w_in,
              conv_dw_w, conv_dw_b, conv_ln_g, conv_ln_b, hy_short_w, hy_short_b, hy_fw1, hy_fb1, hy_freq1,
              hy_fw2, hy_fb2, hy_freq2, hy_fw3, hy_fb3, hy_d, attn_sink, w_out, router_coarse_w,
              router_coarse_b, router_fine_w, router_fine_b, exp_gate, exp_up, exp_down, norm_f_g):
    L_ctx = x_prompt.shape[1]
    L_lat = x_sample.shape[1]
    cos, sin = axial_rope_tables(L_lat)
    xp, xs = x_prompt, x_sample
    ks_out, vs_out = [], []
    for l in range(DEPTH):
        mods_p = adaln(c_ctx[None, :], ada_w[l], ada_b[l])
        mods_s = adaln(c, ada_w[l], ada_b[l])
        filt = (hy_fw1[l], hy_fb1[l], hy_freq1[l], hy_fw2[l], hy_fb2[l], hy_freq2[l], hy_fw3[l], hy_fb3[l])
        kf_p = hyena_kernel_fft(L_ctx, *filt)
        kf_s = hyena_kernel_fft(L_lat, *filt)
        mix_p = (w_in[l], conv_dw_w[l], conv_dw_b[l], conv_ln_g[l], conv_ln_b[l],
                 hy_short_w[l], hy_short_b[l], hy_d[l], w_out[l])
        moe_p = (router_coarse_w[l], router_coarse_b[l], router_fine_w[l], router_fine_b[l],
                 exp_gate[l], exp_up[l], exp_down[l])
        attend_p = functools.partial(context_attention, sink=attn_sink[l])
        attend_s = functools.partial(latent_attention, ck=cache_k[:, l], cv=cache_v[:, l],
                                     sink=attn_sink[l], cos=cos, sin=sin)
        xp, k_ctx, v_ctx = trunk_layer(xp, mods_p, norm1_g[l], norm2_g[l], mix_p, kf_p, attend_p, moe_p)
        ks_out.append(k_ctx)
        vs_out.append(v_ctx)
        xs, _, _ = trunk_layer(xs, mods_s, norm1_g[l], norm2_g[l], mix_p, kf_s, attend_s, moe_p)
    y_prompt = rmsnorm(xp, norm_f_g)
    y_sample = rmsnorm(xs, norm_f_g)
    state_k = jnp.stack(ks_out, axis=1)
    state_v = jnp.stack(vs_out, axis=1)
    return (y_prompt, y_sample, state_k, state_v)


_drawn_inputs = setup_inputs


def setup_inputs(seed=0):
    import zlib

    import numpy as np

    out = dict(_drawn_inputs(seed))
    spreads = {}
    factors = {'cache_k': 4.271,
     'cache_v': 3.865,
     'conv_dw_b': 5.377,
     'conv_ln_g': 2.844,
     'conv_ln_b': 8.0,
     'hy_short_b': 4.044,
     'hy_fb1': 8.0,
     'hy_freq1': 5.461,
     'hy_fb2': 5.546,
     'hy_freq2': 8.0,
     'hy_fb3': 7.811,
     'attn_sink': 36.373,
     'router_coarse_b': 7.316,
     'router_fine_b': 21.522}
    for name, (base, spread) in spreads.items():
        noise = np.random.default_rng([zlib.crc32(name.encode()), seed]).standard_normal(out[name].shape)
        drawn = base * np.exp(spread * noise) if base else spread * noise
        out[name] = __import__('jax').numpy.asarray(drawn.astype(out[name].dtype))
    for name, factor in factors.items():
        out[name] = (out[name] * factor).astype(out[name].dtype)
    return out
```

```python
import numpy as np
import concourse.bass as bass
from concourse import mybir
from contextlib import ExitStack

F32 = mybir.dt.float32
I32 = mybir.dt.int32
U32 = mybir.dt.uint32
ALU = mybir.AluOpType
ACT = mybir.ActivationFunctionType
AX = mybir.AxisListType

P = 128
D = 1024
KC = D // P
LS, LP = 512, 128
T = LS + LP
NT = T // P
DEPTH = 2
CH = 256
TAPS = 31
PAD = TAPS // 2
CONV = LS + PAD + LP
FFN = 64
EMB = 33
HD = 64
NG, EPG, NE, FE = 4, 8, 32, 256
TOPK = 2
GRID_W = 64
EPS = 1e-6
NEG = -1e30
SLOTS = 2
NBLK = 42
WSLOT = 6 * D
TWO_PI_HI = 6.28125
TWO_PI_LO = 2.0 * np.pi - TWO_PI_HI
MAGIC = 12582912.0
ROWS = TAPS + 3 + 9 + 3 + 2
R_DWB, R_LNG, R_LNB, R_SW, R_SB, R_HD = TAPS, TAPS + 1, TAPS + 2, TAPS + 3, TAPS + 12, TAPS + 15


def constants():
    c = {}
    f = lambda a: np.ascontiguousarray(a, dtype=np.float32)

    def tile_rows(a):
        return a.reshape(-1, P, a.shape[-1]).transpose(1, 0, 2)

    for n, L in (("s", LS), ("p", LP)):
        t = np.arange(L, dtype=np.float64)
        w = 2 * np.pi * np.outer(t, np.arange(L) + 0.5) / (2 * L)
        c["fwd_" + n] = f(tile_rows(np.concatenate([np.cos(w), -np.sin(w)], axis=1)))
        c["inv_" + n] = f(tile_rows(np.concatenate([np.cos(w.T), -np.sin(w.T)], axis=0) / L))
        g = 2 * np.pi * (np.outer(t, t) % L) / L
        c["mix_" + n] = f(tile_rows(np.concatenate([np.cos(g), np.sin(g)], axis=1) / np.sqrt(L * CH)))
    t = np.arange(CH, dtype=np.float64)
    g = 2 * np.pi * (np.outer(t, t) % CH) / CH
    c["mix_c"] = f(tile_rows(np.concatenate([np.cos(g), -np.sin(g)], axis=1)))
    feat, win = [], []
    nb = (EMB - 1) // 2
    fr = np.linspace(1e-4, nb - 1, nb)
    lo, hi = np.log(1e-2) / 1.5, np.log(1e-2) / 0.3
    for L in (LS, LP):
        t = np.linspace(0.0, 1.0, L)[:, None]
        w = 2 * np.pi * np.arange(L)[:, None] / L
        feat.append(np.concatenate([t, np.cos(fr * w), -np.sin(fr * w)], axis=1))
        win.append(np.exp(-t * np.abs(np.linspace(lo, hi, CH))[None]) + 0.05)
    c["feat"] = f(np.concatenate(feat).T)
    c["win"] = f(tile_rows(np.concatenate(win)))
    tok = np.arange(LS)
    inv = 10000.0 ** (-np.arange(16) / 16)
    ang = np.concatenate([(tok // GRID_W)[:, None] * inv, (tok % GRID_W)[:, None] * inv], axis=1)
    c["rope"] = f(np.stack([np.tile(np.cos(ang).T, (4, 1)), np.tile(np.sin(ang).T, (4, 1))], axis=1))
    rot = np.zeros((P, P))
    for h in range(2):
        for d in range(32):
            rot[h * 64 + 32 + d, h * 64 + d] = -1
            rot[h * 64 + d, h * 64 + 32 + d] = 1
    i = np.arange(P)
    left = np.where(i[None] < i[:, None], NEG, 0)
    right = np.where(i[None] > i[:, None], NEG, 0)
    c["sq"] = f(np.stack([np.eye(P), np.ones((P, P)), np.full((P, P), 1 / D), np.full((P, P), 1 / CH),
                          rot, i[:, None] < i[None], left, right], axis=1))
    val = (np.arange(NT)[None, :, None] * P + i[:, None, None]) * TOPK + np.arange(TOPK)[None, None] + 1
    row = lambda n: np.tile(np.arange(n)[None], (P, 1))
    c["iota"] = f(np.concatenate([row(P), val.reshape(P, NT * TOPK)], axis=1))
    return c


def trunk(nc, io, out):
    ctx = ExitStack()
    with ctx:
        def sem(name):
            return ctx.enter_context(nc.semaphore(name))

        words = [0]

        def sb(name, shape, dt=F32):
            return ctx.enter_context(nc.sbuf_tensor(name, shape, dt))

        xT = sb("xT", [P, KC, T])
        hT = sb("hT", [P, KC, T])
        yT = sb("yT", [P, KC, T])
        ring = sb("ring", [P, SLOTS, WSLOT])
        dft = sb("dft", [P, 4, 2 * LS])
        inv_s = sb("inv_s", [P, 8, LS])
        fwd_p = sb("fwd_p", [P, 1, 2 * LP])
        inv_p = sb("inv_p", [P, 2, LP])
        mix_p = sb("mix_p", [P, 1, 2 * LP])
        mix_c = sb("mix_c", [P, 2, 2 * CH])
        feat = sb("feat", [EMB, T])
        win = sb("win", [P, NT, CH])
        rope = sb("rope", [P, 2, LS])
        sq = sb("sq", [P, 8, P])
        ident, ones, mean_d, mean_c, rot, tri, mask_l, mask_r = [sq[:, i, :] for i in range(8)]
        iota = sb("iota", [P, P + NT * TOPK])
        epsc = sb("epsc", [P, 1])
        c_raw = sb("c_raw", [P, 2, KC])
        c_act = sb("c_act", [P, KC, 2])
        nf = sb("nf", [P, KC])
        ada_b = sb("ada_bs", [P, 6, KC])
        norms = sb("norms", [P, 2, KC])
        prm = sb("prm", [ROWS, CH])
        prmT = sb("prmT", [P, 2, ROWS])
        frow = sb("frow", [4, FFN])
        frowT = sb("frowT", [FFN, 4])
        fw1 = sb("fw1", [EMB, FFN])
        fw2 = sb("fw2", [FFN, FFN])
        fw3 = sb("fw3", [FFN + 1, 2, 2, CH])
        brow = sb("brow", [1, 40])
        bcast = sb("bcast", [P, 40])
        wr = sb("wr", [P, KC, 36])
        ckv = sb("ckv", [P, 2, P])
        ckT = sb("ckT", [P, P])
        mods = sb("mods", [P, 6, KC, 2])
        gain = sb("gain", [P, 2, KC, 2])
        WORK = 8192
        work = sb("work", [P, WORK])

        def at(base, off, *dims):
            n = int(np.prod(dims))
            v = base[:, off:off + n]
            if len(dims) == 1:
                return v
            names = "abcd"[:len(dims)]
            return v.rearrange("p (" + " ".join(names) + ") -> p " + " ".join(names),
                               **{x: d for x, d in zip(names[1:], dims[1:])})

        hflat = hT[:, :, :].rearrange("p k t -> p (k t)")
        yflat = yT[:, :, :].rearrange("p k t -> p (k t)")
        rms = at(work, 0, T)
        rinv = at(work, T, T)
        GW = PAD + CONV + PAD
        glu = at(work, 0, 2, GW)
        acc = at(work, 2 * GW, 2, CONV)
        sig = at(work, 2 * GW + 2 * CONV, 2, T)
        crs = at(work, 2 * GW + 2 * CONV, CONV)
        crn = at(work, 2 * GW + 2 * CONV + CONV, CONV)
        csq = at(work, 0, 2, CONV)
        fX = at(work, WORK - 3840, NT, CH)
        fA = at(work, WORK - 2560, 2, 2, T)
        qraw = at(work, WORK - 2560, 2, T)
        kraw = at(work, WORK - 1280, T)
        vtok = at(work, WORK - 640, NT, P)
        qrope = at(work, 0, 2, LS)
        krope = at(work, 1024, LS)
        prob = at(work, 1536, 4, 512)
        probT = at(work, 3584, 4, 512)
        rtmp = at(work, 1536, 3, LS)
        ast = sb("ast", [P, 8, 4])
        kvo = sb("kvo", [P, 2, P])
        u = at(work, 0, 6, T)
        zs = at(work, 3840, NT, CH)
        ctmp = at(work, 5120, NT * CH)
        h2 = at(work, 6400, T)
        fa_ = at(work, 3840, T)
        fk_ = at(work, 4480, T)
        h1 = at(work, 5120, T)
        ftime = at(work, 3840, 2, 2, CH)
        fabs = at(work, 5120, 2, 2, CH)
        kspec = at(hflat, 0, 2, NT, CH)
        yspec = at(hflat, 2560, 2, NT, CH)
        evod = at(hflat, 2560, NT, 2, CH)
        rnorm = sb("rnorm", [P, 4])
        xg = at(work, 0, SLOTS, D)
        xe = at(work, 2048, SLOTS, KC, P)
        ye = at(work, 4096, SLOTS, D)
        sg = at(work, 6144, SLOTS, FE)
        hh = at(work, 6656, SLOTS, FE)
        he = at(work, 7168, SLOTS, 2, P)
        htok = ye
        ycomb = at(work, 0, 2, TOPK, D)
        ysum = at(work, 4096, 2, D)
        R = [0]

        def rt(*dims):
            o = R[0]
            R[0] += int(np.prod(dims))
            return at(yflat, o, *dims)

        lg = rt(NT, 36)
        gmax = rt(NT)
        gidx = rt(NT)
        goh = rt(NT, NG)
        gexp = rt(NT, NG)
        gt = rt(NT, NG)
        gsum = rt(NT)
        lfm = rt(NT, NE)
        lt = rt(NT, NE)
        oh = [rt(NT, NE) for _ in range(2)]
        top = [rt(NT) for _ in range(2)]
        tidx = rt(NT)
        both = rt(NT, NE)
        ediff = rt(NT)
        emx = rt(NT)
        eden = rt(NT)
        wgt = [rt(NT) for _ in range(2)]
        rank = rt(NT, NE)
        cnt = rt(NE)
        nbl = rt(NE)
        cum = rt(NE)
        exc = rt(NE)
        thr = rt(NE, NT)
        selr = rt(2, NT)
        sele = rt(2, NT)
        flo = rt(2, NT)
        flt = rt(2, NT, NT)
        ohb = rt(NT, 2, NBLK)
        ohs = rt(NT, 2, P)
        ebt = rt(NBLK, NE)
        ebf = rt(NBLK)
        tabf = rt(NBLK)
        tabz = rt(NBLK)
        assert R[0] <= KC * T, R
        ebi = sb("ebi", [P, NBLK], I32)
        nturn = sb("nturn", [P, 2], I32)
        tabs = sb("tabs", [P, 2, NBLK], I32)
        icol = sb("icol", [P, SLOTS, 2], I32)

        ps = ctx.enter_context(nc.psum_tensor("ps", [P, 8, 512], F32))

        H_dram = nc.dram_tensor("h_scratch", (T, D), F32, kind="Internal").ap()
        Y_dram = nc.dram_tensor("y_scratch", (T * TOPK, D), F32, kind="Internal").ap()

        const_in = sem("const_in")
        cond_in = sem("cond_in")
        x_in = sem("x_in")
        set_up = sem("set_up")
        c_ready = sem("c_ready")
        xT_mm = sem("xT_mm")
        xT_in = sem("xT_in")
        arrived = sem("layer_arrived")
        go = {e: sem("layer_go_" + e) for e in ("pe", "act", "dve", "pool")}
        out_sq = sem("out_sq")
        out_ms = sem("out_ms")
        out_rt = sem("out_rt")
        out_rc = sem("out_rc")
        out_xn = sem("out_xn")
        out_h = sem("out_h")
        out_mm = sem("out_mm")
        out_ev = sem("out_ev")
        out_st = sem("out_st")

        w_full0 = sem("w_full0")
        w_full1 = sem("w_full1")
        w_used = sem("w_used")
        cs_in = sem("cs_in")
        f_in = sem("f_in")
        par_in = sem("par_in")
        par_mm = sem("par_mm")
        par_ev = sem("par_ev")
        mods_ok = sem("mods_ok")
        dchain = sem("dchain")
        sq0 = sem("sq0")
        ms0 = sem("ms0")
        rt0 = sem("rt0")
        rc0 = sem("rc0")
        xn0 = sem("xn0")
        h0 = sem("h0")
        sq1 = sem("sq1")
        ms1 = sem("ms1")
        rt1 = sem("rt1")
        rc1 = sem("rc1")
        xn1 = sem("xn1")
        h1s = sem("h1s")
        cv_mm = sem("cv_mm")
        cv_sig = sem("cv_sig")
        cv_glu = sem("cv_glu")
        cv_tap = sem("cv_tap")
        ln_mm = sem("ln_mm")
        ln_ctr = sem("ln_ctr")
        ln_sq = sem("ln_sq")
        ln_var = sem("ln_var")
        ln_rt = sem("ln_rt")
        ln_rn = sem("ln_rn")
        ln_out = sem("ln_out")
        ya_ok = sem("ya_ok")
        fo_x = sem("fo_x")
        fo_xe = sem("fo_xe")
        fo_a = sem("fo_a")
        fo_ae = sem("fo_ae")
        fo_b = sem("fo_b")
        yc_ok = sem("yc_ok")
        at_mm = sem("at_mm")
        at_ev = sem("at_ev")
        at_rot = sem("at_rot")
        at_rope = sem("at_rope")
        kv_out = sem("kv_out")
        at_s = sem("at_s")
        at_max = sem("at_max")
        at_exp = sem("at_exp")
        at_prob = sem("at_prob")
        at_t = sem("at_t")
        at_te = sem("at_te")
        at_pv = sem("at_pv")
        yd_ok = sem("yd_ok")
        hy_m1 = sem("hy_m1")
        hy_a1 = sem("hy_a1")
        hy_s1 = sem("hy_s1")
        hy_m2 = sem("hy_m2")
        hy_a2 = sem("hy_a2")
        hy_s2 = sem("hy_s2")
        hy_u = sem("hy_u")
        hy_u1 = sem("hy_u1")
        hy_uc = sem("hy_uc")
        hy_f = sem("hy_f")
        hy_raw = sem("hy_raw")
        hy_abs = sem("hy_abs")
        hy_eo = sem("hy_eo")
        hy_norm = sem("hy_norm")
        hy_rn = sem("hy_rn")
        hy_k = sem("hy_k")
        hy_ke = sem("hy_ke")
        hy_zt = sem("hy_zt")
        hy_z = sem("hy_z")
        hy_dz = sem("hy_dz")
        hy_fz = sem("hy_fz")
        hy_y = sem("hy_y")
        hy_inv = sem("hy_inv")
        hy_zn = sem("hy_zn")
        wo_mm = sem("wo_mm")
        x_mid = sem("x_mid")
        hs_mm = sem("hs_mm")
        hs_ev = sem("hs_ev")
        hs_st0 = sem("hs_st0")
        hs_st1 = sem("hs_st1")
        ro_mm = sem("ro_mm")
        ro_sub = sem("ro_sub")
        ro_exp = sem("ro_exp")
        ro_oh = sem("ro_oh")
        ro_rank = sem("ro_rank")
        ro_sub2 = sem("ro_sub2")
        ro_exp2 = sem("ro_exp2")
        ro_tab = sem("ro_tab")
        ro_1h = sem("ro_1h")
        ro_tm = sem("ro_tm")
        ro_tok = sem("ro_tok")
        wg_full0 = sem("wg_full0")
        wg_full1 = sem("wg_full1")
        wd_full0 = sem("wd_full0")
        wd_full1 = sem("wd_full1")
        ic0 = sem("ic0")
        ic1 = sem("ic1")
        xg_in0 = sem("xg_in0")
        xg_in1 = sem("xg_in1")
        xt_mm0 = sem("xt_mm0")
        xt_mm1 = sem("xt_mm1")
        xe_ok0 = sem("xe_ok0")
        xe_ok1 = sem("xe_ok1")
        g_mm0 = sem("g_mm0")
        g_mm1 = sem("g_mm1")
        u_mm0 = sem("u_mm0")
        u_mm1 = sem("u_mm1")
        sg_ok0 = sem("sg_ok0")
        sg_ok1 = sem("sg_ok1")
        hh_ok0 = sem("hh_ok0")
        hh_ok1 = sem("hh_ok1")
        ht_mm0 = sem("ht_mm0")
        ht_mm1 = sem("ht_mm1")
        he_ok0 = sem("he_ok0")
        he_ok1 = sem("he_ok1")
        y_mm0 = sem("y_mm0")
        y_mm1 = sem("y_mm1")
        ye_a0 = sem("ye_a0")
        ye_a1 = sem("ye_a1")
        ye_d0 = sem("ye_d0")
        ye_d1 = sem("ye_d1")
        y_out0 = sem("y_out0")
        y_out1 = sem("y_out1")
        pool_nop = sem("pool_nop")
        yc_in0 = sem("yc_in0")
        yc_in1 = sem("yc_in1")
        yc_sum = sem("yc_sum")
        yc_mm = sem("yc_mm")
        x_new = sem("x_new")
        layer_range = range(w_full0.num, x_new.num + 1)
        assert len(layer_range) == 132, "the layer's semaphores lie in one range"
        w_full = [w_full0, w_full1]
        wg_full = [wg_full0, wg_full1]
        wd_full = [wd_full0, wd_full1]
        hs_st = [hs_st0, hs_st1]
        ic = [ic0, ic1]
        xg_in = [xg_in0, xg_in1]
        xt_mm = [xt_mm0, xt_mm1]
        xe_ok = [xe_ok0, xe_ok1]
        g_mm = [g_mm0, g_mm1]
        u_mm = [u_mm0, u_mm1]
        sg_ok = [sg_ok0, sg_ok1]
        hh_ok = [hh_ok0, hh_ok1]
        ht_mm = [ht_mm0, ht_mm1]
        he_ok = [he_ok0, he_ok1]
        y_mm = [y_mm0, y_mm1]
        ye_a = [ye_a0, ye_a1]
        ye_d = [ye_d0, ye_d1]
        y_out = [y_out0, y_out1]
        yc_in = [yc_in0, yc_in1]
        sq_s, ms_s, rt_s, rc_s, xn_s, h_s = (sq0, sq1), (ms0, ms1), (rt0, rt1), (rc0, rc1), (xn0, xn1), (h0, h1s)

        I_CONV, I_FOUR, I_ATT, I_HY, I_OUT = 8, 9, 10, 11, 12
        ITEMS = 14

        def wait_item(eng, i):
            eng.wait_ge(w_full[i % SLOTS], 16 * (i // SLOTS + 1))

        def slot(i, *dims):
            return at(ring[:, i % SLOTS, :], 0, *dims)

        GRP = ((0, LS), (LS, T))

        def last_of_layer(eng, name):
            eng.drain().then_inc(arrived, 1)
            eng.wait_ge(go[name], 1)
            eng.sem_clear(go[name])

        block = ctx.enter_context(nc.Block())

        @block.sync
        def _(sp):
            sp.dma_start(work[:, 0:NT * D].rearrange("p (t d) -> p t d", t=NT)[:, 0:4, :],
                         io["x_sample"][0].rearrange("(t p) d -> p t d", p=P)).then_inc(x_in, 16)
            sp.dma_start(work[:, 4 * D:NT * D], io["x_prompt"][0]).then_inc(x_in, 16)
            for dst, name in ((sq, "sq"), (iota, "iota"), (mix_c, "mix_c"), (mix_p, "mix_p"), (fwd_p, "fwd_p"),
                              (inv_p, "inv_p"), (feat, "feat"), (win, "win"), (rope, "rope"), (inv_s, "inv_s")):
                full = dst[:, :] if len(dst.shape) == 2 else dst[:, :, :]
                sp.dma_start(full, io["c_" + name]).then_inc(const_in, 16)
            sp.wait_ge(const_in, 16 * 10)
            with sp.Fori(0, DEPTH) as l:
                ada = io["ada_w"][l].rearrange("(p k) n -> p k n", k=KC)
                win_l = io["w_in"][l].rearrange("(p k) n -> p k n", k=KC)
                wout_l = io["w_out"][l].rearrange("(i p) n -> p i n", p=P)
                for i in range(KC):
                    if i >= SLOTS:
                        sp.wait_ge(w_used, i - SLOTS + 1)
                    sp.dma_start(slot(i, WSLOT), ada[:, i, :]).then_inc(w_full[i % SLOTS], 16)
                sp.dma_start(dft[:, :, :], io["c_mix_s"]).then_inc(cs_in, 16)
                for i, lo, n, used, count in ((I_CONV, 0, 512, w_used, KC - 1), (I_FOUR, 1280, 256, w_used, KC),
                                              (I_ATT, 1536, 512, cv_mm, 4), (I_HY, 512, 768, fo_x, NT)):
                    sp.wait_ge(used, count)
                    sp.dma_start(slot(i, KC, n), win_l[:, :, lo:lo + n]).then_inc(w_full[i % SLOTS], 16)
                sp.wait_ge(fo_a, 6)
                sp.dma_start(dft[:, :, :], io["c_fwd_s"]).then_inc(f_in, 16)
                for i, used, count in ((I_OUT, at_mm, 5), (I_OUT + 1, hy_u, 6)):
                    sp.wait_ge(used, count)
                    h = i - I_OUT
                    sp.dma_start(slot(i, 4, D), wout_l[:, 4 * h:4 * h + 4, :]).then_inc(w_full[i % SLOTS], 16)
                for t in range(NT):
                    sp.wait_ge(hs_ev, 2 * t + 2)
                    sp.dma_start(H_dram[t * P:(t + 1) * P, :], htok[:, t % 2, :]).then_inc(hs_st[t % 2], 16)
                sp.wait_ge(wo_mm, KC)
                sp.wait_ge(ro_tab, 1)
                turns = sp.value_load(nturn[0:1, 0:1], min_val=1, max_val=NBLK // 2)
                with sp.Fori(0, turns) as j:
                    for s in range(SLOTS):
                        e = sp.value_load(ebi[0:1, bass.ds(j * SLOTS + s, 1)], min_val=0, max_val=NE - 1)
                        sp.wait_ge(y_mm[s], j * 2 + 1)
                        gw = slot(s, 3, KC * FE)
                        for q, name in ((0, "exp_gate"), (1, "exp_up")):
                            src = io[name].rearrange("l e (p k) f -> (l e) p (k f)", k=KC)
                            sp.dma_start(gw[:, q, :], src[l * NE + e]).then_inc(wg_full[s], 16)
                        src = io["exp_down"].rearrange("l e (p k) f -> (l e) p (k f)", k=2)
                        sp.dma_start(gw[:, 2, :], src[l * NE + e]).then_inc(wd_full[s], 16)
                for s in range(SLOTS):
                    sp.wait_ge(y_out[s], turns * 16 + 16)
                yrow = Y_dram.rearrange("(t p k) d -> t p (k d)", p=P, k=TOPK)
                for t in range(NT):
                    if t >= 2:
                        sp.wait_ge(yc_sum, t - 1)
                    sp.dma_start(ycomb[:, t % 2, :, :].rearrange("p k d -> p (k d)"), yrow[t]) \
                        .then_inc(yc_in[t % 2], 16)
                sp.wait_ge(kv_out, 32)
                sp.wait_ge(arrived, 4)
                sp.sem_clear(layer_range)
                sp.sem_clear(arrived)
                for e in ("pe", "act", "dve", "pool"):
                    sp.sem_inc(go[e])
            for t in range(NT):
                sp.wait_ge(out_ev, 2 * t + 2)
                dst = out["y_sample"][0, t * P:(t + 1) * P, :] if t < 4 else out["y_prompt"][0]
                sp.dma_start(dst, work[:, t * D:(t + 1) * D]).then_inc(out_st, 16)
            sp.wait_ge(out_st, 16 * NT)

        @block.gpsimd
        def _(pool):
            pool.dma_start(c_raw[:, 0, :], io["c"][0].rearrange("(p k) -> p k", k=KC)).then_inc(cond_in, 16)
            pool.dma_start(c_raw[:, 1, :], io["c_ctx"].rearrange("(p k) -> p k", k=KC)).then_inc(cond_in, 16)
            pool.dma_start(nf[:, :], io["norm_f_g"].rearrange("(p k) -> p k", k=KC)).then_inc(cond_in, 16)
            pool.memset(epsc[:, :], EPS).then_inc(set_up, 1)
            with pool.Fori(0, DEPTH) as l:
                for dst, src in (
                        (ada_b[:, :, :], io["ada_b"][l].rearrange("(a p k) -> p a k", a=6, k=KC)),
                        (norms[:, 0, :], io["norm1_g"][l].rearrange("(p k) -> p k", k=KC)),
                        (norms[:, 1, :], io["norm2_g"][l].rearrange("(p k) -> p k", k=KC)),
                        (prm[0:TAPS, :], io["conv_dw_w"][l]),
                        (prm[R_DWB:R_DWB + 1, :], io["conv_dw_b"][l].rearrange("(a c) -> a c", a=1)),
                        (prm[R_LNG:R_LNG + 1, :], io["conv_ln_g"][l].rearrange("(a c) -> a c", a=1)),
                        (prm[R_LNB:R_LNB + 1, :], io["conv_ln_b"][l].rearrange("(a c) -> a c", a=1)),
                        (prm[R_SW:R_SW + 9, :], io["hy_short_w"][l].rearrange("j (g c) -> (j g) c", c=CH)),
                        (prm[R_SB:R_SB + 3, :], io["hy_short_b"][l].rearrange("(g c) -> g c", c=CH)),
                        (prm[R_HD:R_HD + 2, :], io["hy_d"][l]),
                        (frow[0:1, :], io["hy_fb1"][l].rearrange("(a c) -> a c", a=1)),
                        (frow[1:2, :], io["hy_freq1"][l].rearrange("(a c) -> a c", a=1)),
                        (frow[2:3, :], io["hy_fb2"][l].rearrange("(a c) -> a c", a=1)),
                        (frow[3:4, :], io["hy_freq2"][l].rearrange("(a c) -> a c", a=1)),
                        (fw1[:, :], io["hy_fw1"][l]),
                        (fw2[:, :], io["hy_fw2"][l]),
                        (fw3[0:FFN, :, :, :].rearrange("p a b c -> p (a b c)"), io["hy_fw3"][l]),
                        (fw3[FFN:FFN + 1, :, :, :].rearrange("p a b c -> p (a b c)"),
                         io["hy_fb3"][l].rearrange("(a c) -> a c", a=1)),
                        (brow[:, 0:4], io["attn_sink"][l].rearrange("(a c) -> a c", a=1)),
                        (brow[:, 4:8], io["router_coarse_b"][l].rearrange("(a c) -> a c", a=1)),
                        (brow[:, 8:40], io["router_fine_b"][l].rearrange("(a c) -> a c", a=1)),
                        (wr[:, :, 0:4], io["router_coarse_w"][l].rearrange("(p k) n -> p k n", k=KC)),
                        (wr[:, :, 4:36], io["router_fine_w"][l].rearrange("(p k) n -> p k n", k=KC)),
                        (ckv[:, 0, :], io["cache_k"][0, l].rearrange("t h d -> t (h d)")),
                        (ckv[:, 1, :], io["cache_v"][0, l].rearrange("t h d -> t (h d)"))):
                    pool.dma_start(dst, src).then_inc(par_in, 16)
                pool.wait_ge(at_ev, 8)
                for q, name in ((0, "state_k"), (1, "state_v")):
                    pool.dma_start(out[name][0, l].rearrange("t h d -> t (h d)"), kvo[:, q, :]).then_inc(kv_out, 16)
                pool.wait_ge(xn1, KC)
                for s in range(SLOTS):
                    pool.dma_start(xg[:, s, :], io["x_prompt"][0]).then_inc(y_out[s], 16)
                for s in range(SLOTS):
                    pool.wait_ge(y_out[s], 16)
                for q in range(2):
                    pool.wait_ge(hs_st[q], 16 * ((NT + 1 - q) // 2))
                pool.wait_ge(ro_tok, 1)
                turns = pool.value_load(nturn[0:1, 0:1], min_val=1, max_val=NBLK // 2)
                with pool.Fori(0, turns) as j:
                    for s in range(SLOTS):
                        pool.wait_ge(y_out[s], j * 16 + 16)
                        pool.sem_inc(pool_nop)
                        pool.tensor_copy(icol[:, s, :], tabs[:, :, bass.ds(j * SLOTS + s, 1)]
                                         .rearrange("p a b -> p (a b)")).then_inc(ic[s], 1)
                        pool.wait_ge(ic[s], j + 1)
                        pool.sem_inc(pool_nop)
                        pool.wait_ge(xt_mm[s], j + 1)
                        pool.sem_inc(pool_nop)
                        pool.indirect_dma_start(
                            xg[:, s, :], None, H_dram[:, :],
                            bass.IndirectOffsetOnAxis(ap=icol[:, s, 0:1].bitcast(U32), axis=0),
                            bounds_check=T - 1, oob_is_err=False).then_inc(xg_in[s], 16)
                    for s in range(SLOTS):
                        pool.wait_ge(ye_a[s], j + 2)
                        pool.sem_inc(pool_nop)
                        pool.wait_ge(ye_d[s], j + 2)
                        pool.sem_inc(pool_nop)
                        pool.indirect_dma_start(
                            Y_dram[:, :], bass.IndirectOffsetOnAxis(ap=icol[:, s, 1:2].bitcast(U32), axis=0),
                            ye[:, s, :], None,
                            bounds_check=T * TOPK - 1, oob_is_err=False).then_inc(y_out[s], 16)
                pool.wait_ge(par_in, 16 * 25)
                pool.wait_ge(kv_out, 32)
                for s in range(SLOTS):
                    pool.wait_ge(xg_in[s], turns * 16)
                    pool.sem_inc(pool_nop)
                    pool.wait_ge(y_out[s], turns * 16 + 16)
                    pool.sem_inc(pool_nop)
                pool.dma_reset(layer_range)
                last_of_layer(pool, "pool")

        @block.tensor
        def _(pe):
            mm = nc.tensor.matmul

            def group(k, n, lhsT_of, tile_s, tile_p, rhs=hT):
                mm(tile_s, lhsT_of(k), rhs[:, k, 0:LS], start=(k == 0), stop=(k == n - 1))
                return mm(tile_p, lhsT_of(k), rhs[:, k, LS:T], start=(k == 0), stop=(k == n - 1))

            def abs_sum(o, t):
                pe.wait_ge(hy_abs, NT * o + t + 1)
                for q in range(2):
                    for c in range(2):
                        col = c if t < 4 else 2 + c
                        last = mm(ps[:, 5, col:col + 1], fabs[:, t % 2, q, c * P:(c + 1) * P], ones[:, 0:1],
                                  start=(t == 0 and q == 0 and c == 0), stop=(q == 1 and t >= 3), skip_group_check=True)
                last.then_inc(hy_norm, 1)

            def mean_square(sq_sem, ms_sem):
                for k in range(KC):
                    pe.wait_ge(sq_sem, k + 1)
                    last = group(k, KC, lambda _: mean_d, ps[:, 0, :], ps[:, 1, 0:LP])
                last.then_inc(ms_sem, 1)

            pe.wait_ge(const_in, 16 * 10)
            pe.wait_ge(x_in, 32)
            for t in range(NT):
                if t >= 2:
                    pe.wait_ge(xT_in, 2 * (t - 1))
                for k in range(KC):
                    last = nc.tensor.transpose(ps[:, 4 * (t % 2) + k // 4, (k % 4) * P:(k % 4 + 1) * P],
                                               work[:, t * D + k:(t + 1) * D:KC], ident)
                last.then_inc(xT_mm, 1)
            pe.wait_ge(xT_in, 2 * NT)
            pe.wait_ge(c_ready, 1)
            with pe.Fori(0, DEPTH):
                pe.wait_ge(par_in, 16 * 25)
                for c in range(2):
                    nc.tensor.transpose(ps[:, 7, c * ROWS:(c + 1) * ROWS], prm[:, c * P:(c + 1) * P], ident[0:ROWS, 0:ROWS])
                nc.tensor.transpose(ps[0:FFN, 7, 100:104], frow[:, :], ident[0:4, 0:4])
                mm(ps[:, 7, 104:144], ones[0:1, :], brow[:, :], start=True, stop=True)
                nc.tensor.transpose(ps[:, 7, 144:272], ckv[:, 0, :], ident).then_inc(par_mm, 1)
                for k in range(KC):
                    wait_item(pe, k)
                    w = slot(k, 6, D)
                    for a in range(6):
                        for q in range(KC):
                            o = (a * KC + q) * 2
                            last = mm(ps[:, 6, o:o + 2], w[:, a, q:D:KC], c_act[:, k, :],
                                      start=(k == 0 and a == 0 and q == 0), stop=(k == KC - 1),
                                      skip_group_check=True)
                    last.then_inc(w_used, 1)
                mean_square(sq_s[0], ms_s[0])
                wait_item(pe, I_CONV)
                pe.wait_ge(par_ev, 4)
                w = slot(I_CONV, KC, 512)
                for c in range(2):
                    for m in (2 + c, c):
                        for k in range(KC):
                            if c == 0 and m == 2:
                                pe.wait_ge(h_s[0], k + 1)
                            last = group(k, KC, lambda k: w[:, k, m * P:(m + 1) * P], ps[:, m, :], ps[:, 4 + m, 0:LP])
                        last.then_inc(cv_mm, 1)
                wait_item(pe, I_FOUR)
                w = slot(I_FOUR, KC, CH)
                pe.wait_ge(cv_glu, 2)
                for t in range(NT):
                    for k in range(KC):
                        last = mm(ps[:, t, 0:CH], hT[:, k, t * P:(t + 1) * P], w[:, k, :], start=(k == 0), stop=(k == KC - 1))
                    last.then_inc(fo_x, 1)
                pe.wait_ge(cs_in, 16)
                pe.wait_ge(fo_xe, 5)
                for c in range(2):
                    for q in range(2):
                        for t in range(4):
                            last = mm(ps[:, (5 + 2 * c + q) % 8, :], fX[:, t, c * P:(c + 1) * P],
                                      dft[:, t, q * LS:(q + 1) * LS], start=(t == 0), stop=(t == 3))
                        last.then_inc(fo_a, 1)
                for c in range(2):
                    mm(ps[:, 1 + c, 0:CH], fX[:, 4, c * P:(c + 1) * P], mix_p[:, 0, :], start=True, stop=True) \
                        .then_inc(fo_a, 1)
                pe.wait_ge(fo_ae, 6)
                for m in range(2):
                    n = 0
                    for c in range(2):
                        for q in range(2):
                            lhs = mix_c[:, c, q * CH + m * P:q * CH + (m + 1) * P]
                            mm(ps[:, 3 + m, :], lhs, fA[:, c, q, 0:LS], start=(n == 0), stop=(n == 3))
                            last = mm(ps[:, 5 + m, 0:LP], lhs, fA[:, c, q, LS:T], start=(n == 0), stop=(n == 3))
                            n += 1
                    last.then_inc(fo_b, 1)
                wait_item(pe, I_ATT)
                w = slot(I_ATT, KC, 512)
                pe.wait_ge(yc_ok, 4)
                for m in range(2):
                    for k in range(KC):
                        last = group(k, KC, lambda k: w[:, k, m * P:(m + 1) * P],
                                     ps[:, m, :], ps[:, 2 + m, 0:LP])
                    last.then_inc(at_mm, 1)
                for k in range(KC):
                    last = group(k, KC, lambda k: w[:, k, 256:384], ps[:, 4, :], ps[:, 5, 0:LP])
                last.then_inc(at_mm, 1)
                for t in range(4):
                    for k in range(KC):
                        last = mm(ps[:, 6, t * P:(t + 1) * P], hT[:, k, t * P:(t + 1) * P], w[:, k, 384:512],
                                  start=(k == 0), stop=(k == KC - 1))
                last.then_inc(at_mm, 1)
                for k in range(KC):
                    last = mm(ps[:, 7, 0:256], hT[:, k, LS:T], w[:, k, 256:512], start=(k == 0), stop=(k == KC - 1))
                last.then_inc(at_mm, 1)
                pe.wait_ge(at_ev, 8)
                pe.wait_ge(cv_tap, 2 * TAPS)
                for c in range(2):
                    mm(ps[:, 0, :], mean_c, acc[:, c, 0:LS], start=(c == 0), stop=(c == 1))
                    last = mm(ps[:, 4, 0:CONV - LS], mean_c, acc[:, c, LS:CONV], start=(c == 0), stop=(c == 1))
                last.then_inc(ln_mm, 1)
                pe.wait_ge(ln_sq, 2)
                for c in range(2):
                    mm(ps[:, 1, :], mean_c, csq[:, c, 0:LS], start=(c == 0), stop=(c == 1))
                    last = mm(ps[:, 5, 0:CONV - LS], mean_c, csq[:, c, LS:CONV], start=(c == 0), stop=(c == 1))
                last.then_inc(ln_var, 1)
                pe.wait_ge(ln_rt, 2)
                for m in range(3):
                    src = qraw[:, m, 0:LS] if m < 2 else kraw[:, 0:LS]
                    mm(ps[:, m, :], rot, src, start=True, stop=True).then_inc(at_rot, 1)
                pe.wait_ge(at_rope, 3)

                def scores(i):
                    if i > 0:
                        pe.wait_ge(at_exp, 4 * i)
                    for h in range(4):
                        p0, m = HD * (h // 2), h % 2
                        if i < 4:
                            lo, hi = max(i - 1, 0), min(i + 2, 4)
                            mm(ps[:, h, 0:P], qraw[p0:p0 + HD, m, i * P:(i + 1) * P], ckT[p0:p0 + HD, :], start=True, stop=True)
                            last = mm(ps[:, h, P:P + (hi - lo) * P], qrope[p0:p0 + HD, m, i * P:(i + 1) * P],
                                      krope[p0:p0 + HD, lo * P:hi * P], start=True, stop=True)
                        else:
                            last = mm(ps[:, h, 0:P], qraw[p0:p0 + HD, m, LS:T], kraw[p0:p0 + HD, LS:T], start=True, stop=True)
                    last.then_inc(at_s, 1)

                scores(0)
                for i in range(NT):
                    lo, hi = max(i - 1, 0), min(i + 2, 4)
                    nk = 1 + hi - lo if i < 4 else 1
                    pe.wait_ge(at_prob, i + 1)
                    if i > 0:
                        pe.wait_ge(yd_ok, 2 * i)
                    for h in range(4):
                        for t in range(nk):
                            last = nc.tensor.transpose(ps[:, 4 + h, t * P:(t + 1) * P], prob[:, h, t * P:(t + 1) * P], ident)
                        last.then_inc(at_t, 1)
                    if i + 1 < NT:
                        scores(i + 1)
                    pe.wait_ge(at_te, 4 * (i + 1))
                    for h in range(4):
                        kv = h // 2
                        o = ps[HD * (h % 2):HD * (h % 2) + HD, 4 + h // 2, 0:P]
                        for t in range(nk):
                            if i == 4:
                                v = vtok[:, 4, kv * HD:(kv + 1) * HD]
                            elif t == 0:
                                v = ckv[:, 1, kv * HD:(kv + 1) * HD]
                            else:
                                v = vtok[:, lo + t - 1, kv * HD:(kv + 1) * HD]
                            last = mm(o, v, probT[:, h, t * P:(t + 1) * P], start=(t == 0), stop=(t == nk - 1))
                    last.then_inc(at_pv, 1)
                pe.wait_ge(yd_ok, 2 * NT)
                mm(ps[0:FFN, 6, :], fw1[:, :], feat[:, 0:LS], start=True, stop=True)
                mm(ps[0:FFN, 7, 0:LP], fw1[:, :], feat[:, LS:T], start=True, stop=True).then_inc(hy_m1, 1)
                wait_item(pe, I_HY)
                w = slot(I_HY, KC, 768)
                for m in range(6):
                    if m >= 3:
                        pe.wait_ge(hy_uc, m - 2)
                    for k in range(KC):
                        last = group(k, KC, lambda k: w[:, k, m * P:(m + 1) * P], ps[:, m % 3, :], ps[:, 3 + m % 3, 0:LP])
                    last.then_inc(hy_u, 1)
                    if m == 1:
                        pe.wait_ge(hy_s1, 1)
                        mm(ps[0:FFN, 6, :], fw2[:, :], h1[0:FFN, 0:LS], start=True, stop=True)
                        mm(ps[0:FFN, 7, 0:LP], fw2[:, :], h1[0:FFN, LS:T], start=True, stop=True).then_inc(hy_m2, 1)
                pe.wait_ge(hy_s2, 1)
                pe.wait_ge(hy_uc, 6)
                pe.wait_ge(f_in, 16)
                for o in range(2):
                    if o:
                        pe.wait_ge(hy_zn, 2)
                    for t in range(NT):
                        n = NT * o + t
                        if t >= 2:
                            pe.wait_ge(hy_raw, n - 1)
                        mm(ps[:, 6 + t % 2, :], h2[0:FFN + 1, t * P:(t + 1) * P], fw3[:, :, o, :],
                           start=True, stop=True).then_inc(hy_f, 1)
                        if t >= 1:
                            abs_sum(o, t - 1)
                    abs_sum(o, NT - 1)
                    pe.wait_ge(hy_eo, NT * (o + 1))
                    for q in range(2):
                        for f in range(4):
                            for t in range(4):
                                last = mm(ps[:, 2 * q + f // 2, (f % 2) * CH:(f % 2 + 1) * CH],
                                          dft[:, t, q * LS + f * P:q * LS + (f + 1) * P], evod[:, t, q, :],
                                          start=(t == 0), stop=(t == 3))
                    for q in range(2):
                        last = mm(ps[:, 4, q * CH:(q + 1) * CH], fwd_p[:, 0, q * LP:(q + 1) * LP], evod[:, 4, q, :],
                                  start=True, stop=True)
                    last.then_inc(hy_k, 1)
                    pe.wait_ge(hy_ke, o + 1)
                    for t in range(NT):
                        for c in range(2):
                            last = nc.tensor.transpose(ps[:, t // 2, (t % 2) * CH + c * P:(t % 2) * CH + (c + 1) * P],
                                                       u[:, c, t * P:(t + 1) * P], ident)
                    last.then_inc(hy_zt, 1)
                    pe.wait_ge(hy_z, o + 1)
                    for q in range(2):
                        for f in range(4):
                            for t in range(4):
                                last = mm(ps[:, 2 * q + f // 2, (f % 2) * CH:(f % 2 + 1) * CH],
                                          dft[:, t, q * LS + f * P:q * LS + (f + 1) * P], zs[:, t, :],
                                          start=(t == 0), stop=(t == 3))
                    for q in range(2):
                        last = mm(ps[:, 4, q * CH:(q + 1) * CH], fwd_p[:, 0, q * LP:(q + 1) * LP], zs[:, 4, :],
                                  start=True, stop=True)
                    last.then_inc(hy_fz, 1)
                    pe.wait_ge(hy_y, o + 1)
                    pe.wait_ge(hy_rn, o + 1)
                    for c in range(2):
                        for q in range(2):
                            for f in range(4):
                                mm(ps[:, 6 + c, :], yspec[:, q, f, c * P:(c + 1) * P], inv_s[:, 4 * q + f, :],
                                   start=(q + f == 0), stop=(q * 4 + f == 7))
                        for q in range(2):
                            last = mm(ps[:, 4 + c, 0:P], yspec[:, q, 4, c * P:(c + 1) * P], inv_p[:, q, :],
                                      start=(q == 0), stop=(q == 1))
                    last.then_inc(hy_inv, 1)
                wait_item(pe, I_OUT)
                wait_item(pe, I_OUT + 1)
                pe.wait_ge(hy_zn, 4)
                pe.wait_ge(ya_ok, 4)
                w2 = [slot(I_OUT + i, 4, D) for i in range(2)]
                for m in range(KC):
                    if m >= 4:
                        pe.wait_ge(x_mid, 2 * (m - 3))
                    for k in range(KC):
                        last = group(k, KC, lambda k: w2[k // 4][:, k % 4, m:D:KC], ps[:, m % 4, :], ps[:, 4 + m % 4, 0:LP], yT)
                    last.then_inc(wo_mm, 1)
                pe.wait_ge(x_mid, 16)
                mean_square(sq_s[1], ms_s[1])
                for t in range(NT):
                    for k in range(KC):
                        if t == 0:
                            pe.wait_ge(h_s[1], k + 1)
                        last = mm(ps[:, 2, t * 36:(t + 1) * 36], hT[:, k, t * P:(t + 1) * P], wr[:, k, :],
                                  start=(k == 0), stop=(k == KC - 1))
                last.then_inc(ro_mm, 1)
                for t in range(NT):
                    if t >= 2:
                        pe.wait_ge(hs_ev, 2 * (t - 1))
                    for k in range(KC):
                        last = nc.tensor.transpose(ps[:, 4 + 2 * (t % 2) + k // 4, (k % 4) * P:(k % 4 + 1) * P],
                                                   hT[:, k, t * P:(t + 1) * P], ident)
                    last.then_inc(hs_mm, 1)
                pe.wait_ge(ro_oh, 1)
                for t in range(NT):
                    for q in range(t):
                        mm(ps[:, 3, t * NE:(t + 1) * NE], ones, both[:, q, :], start=(q == 0), stop=False)
                    mm(ps[:, 3, t * NE:(t + 1) * NE], tri, both[:, t, :], start=(t == 0), stop=True)
                for t in range(NT):
                    last = mm(ps[:, 3, NT * NE:(NT + 1) * NE], ones, both[:, t, :], start=(t == 0), stop=(t == NT - 1))
                last.then_inc(ro_rank, 1)
                pe.wait_ge(ro_1h, 1)
                n = 0
                for t in range(NT):
                    for q in range(2):
                        last = mm(ps[:, 2, 256:256 + NBLK], ohs[:, t, q, :], ohb[:, t, q, :], start=(n == 0), stop=(n == 9))
                        n += 1
                last.then_inc(ro_tm, 1)
                for s in range(SLOTS):
                    pe.sem_inc(xt_mm[s])
                    pe.sem_inc(y_mm[s])
                pe.wait_ge(ro_tab, 1)
                turns = pe.value_load(nturn[0:1, 0:1], min_val=1, max_val=NBLK // 2)
                with pe.Fori(0, turns) as j:
                    for s in range(SLOTS):
                        w = slot(s, 3, KC, FE)
                        wd = slot(s, 3, 2, D)
                        pe.wait_ge(xg_in[s], j * 16 + 16)
                        if s == 0:
                            pe.wait_ge(xe_ok[1], j * 2 + 1)
                        else:
                            pe.wait_ge(xe_ok[0], j * 2 + 3)
                        for k in range(KC):
                            last = nc.tensor.transpose(ps[:, k // 4, (k % 4) * P:(k % 4 + 1) * P],
                                                       xg[:, s, k * P:(k + 1) * P], ident)
                        last.then_inc(xt_mm[s], 1)
                        pe.wait_ge(xe_ok[s], j * 2 + 3)
                        pe.wait_ge(wg_full[s], j * 32 + 32)
                        if s == 0:
                            pe.wait_ge(hh_ok[1], j + 1)
                        else:
                            pe.wait_ge(hh_ok[0], j + 2)
                        for k in range(KC):
                            last = mm(ps[:, 2, 0:FE], xe[:, s, k, :], w[:, 0, k, :], start=(k == 0), stop=(k == KC - 1))
                        last.then_inc(g_mm[s], 1)
                        for k in range(KC):
                            last = mm(ps[:, 3, 0:FE], xe[:, s, k, :], w[:, 1, k, :], start=(k == 0), stop=(k == KC - 1))
                        last.then_inc(u_mm[s], 1)
                        pe.wait_ge(hh_ok[s], j + 2)
                        if s == 0:
                            pe.wait_ge(he_ok[1], j + 1)
                        else:
                            pe.wait_ge(he_ok[0], j + 2)
                        for k in range(2):
                            last = nc.tensor.transpose(ps[:, 4, k * P:(k + 1) * P], hh[:, s, k:FE:2], ident)
                        last.then_inc(ht_mm[s], 1)
                        pe.wait_ge(he_ok[s], j + 2)
                        pe.wait_ge(wd_full[s], j * 16 + 16)
                        if s == 0:
                            pe.wait_ge(ye_a[1], j + 1)
                            pe.wait_ge(ye_d[1], j + 1)
                        else:
                            pe.wait_ge(ye_a[0], j + 2)
                            pe.wait_ge(ye_d[0], j + 2)
                        for n in range(2):
                            for k in range(2):
                                last = mm(ps[:, 6 + n, :], he[:, s, k, :], wd[:, 2, k, n * 512:(n + 1) * 512],
                                          start=(k == 0), stop=(k == 1))
                            last.then_inc(y_mm[s], 1)
                pe.wait_ge(ye_a[1], turns + 1)
                pe.wait_ge(ye_d[1], turns + 1)
                for t in range(NT):
                    pe.wait_ge(yc_sum, t + 1)
                    if t >= 2:
                        pe.wait_ge(x_new, KC * (t - 1))
                    for k in range(KC):
                        last = nc.tensor.transpose(ps[:, 2 * (t % 2) + k // 4, (k % 4) * P:(k % 4 + 1) * P],
                                                   ysum[:, t % 2, k:D:KC], ident)
                    last.then_inc(yc_mm, 1)
                last_of_layer(pe, "pe")
            mean_square(out_sq, out_ms)
            for t in range(NT):
                if t >= 2:
                    pe.wait_ge(out_ev, 2 * (t - 1))
                for k in range(KC):
                    if t == 0:
                        pe.wait_ge(out_h, k + 1)
                    last = nc.tensor.transpose(ps[:, 2 + 2 * (t % 2) + k // 4, (k % 4) * P:(k % 4 + 1) * P],
                                               hT[:, k, t * P:(t + 1) * P], ident)
                last.then_inc(out_mm, 1)

        @block.scalar
        def _(act):
            A = nc.scalar.activation

            def squares(ready, count, sq_sem):
                act.wait_ge(ready, count)
                for k in range(KC):
                    A(hT[:, k, :], xT[:, k, :], ACT.Square).then_inc(sq_sem, 1)

            def root(ms_sem, rt_sem):
                act.wait_ge(ms_sem, 1)
                A(rms[:, 0:LS], ps[:, 0, :], ACT.Sqrt, bias=epsc[:, :]).then_inc(rt_sem, 1)
                A(rms[:, LS:T], ps[:, 1, 0:LP], ACT.Sqrt, bias=epsc[:, :]).then_inc(rt_sem, 1)

            def modulate(n, xn_sem, h_sem):
                for k in range(KC):
                    act.wait_ge(xn_sem, k + 1)
                    for g, (a, b) in enumerate(GRP):
                        last = A(hT[:, k, a:b], hT[:, k, a:b], ACT.Identity, scale=gain[:, n, k, g:g + 1],
                                 bias=mods[:, 3 * n, k, g:g + 1])
                    last.then_inc(h_sem, 1)

            act.wait_ge(cond_in, 16 * 3)
            for g in range(2):
                last = A(c_act[:, :, g], c_raw[:, g, :], ACT.Silu)
            last.then_inc(c_ready, 1)
            for t in range(NT):
                act.wait_ge(xT_mm, t + 1)
                for q in range(2):
                    A(xT[:, 4 * q:4 * q + 4, t * P:(t + 1) * P],
                      ps[:, 4 * (t % 2) + q, :].rearrange("p (k t) -> p k t", k=4), ACT.Copy).then_inc(xT_in, 1)
            act.wait_ge(set_up, 1)
            act.wait_ge(xT_in, 2 * NT)
            with act.Fori(0, DEPTH):
                squares(xT_in, 2 * NT, sq_s[0])
                root(ms_s[0], rt_s[0])
                act.wait_ge(mods_ok, 3)
                modulate(0, xn_s[0], h_s[0])
                for c in range(2):
                    act.wait_ge(cv_mm, 2 * c + 1)
                    for (a, b), bank in ((GRP[0], 2 + c), (GRP[1], 6 + c)):
                        last = A(sig[:, c, a:b], ps[:, bank, 0:b - a], ACT.Sigmoid)
                    last.then_inc(cv_sig, 1)
                for t in range(NT):
                    act.wait_ge(fo_x, t + 1)
                    A(fX[:, t, :], ps[:, t, 0:CH], ACT.Copy).then_inc(fo_xe, 1)
                for c in range(2):
                    for q in range(2):
                        act.wait_ge(fo_a, 2 * c + q + 1)
                        A(fA[:, c, q, 0:LS], ps[:, (5 + 2 * c + q) % 8, :], ACT.Copy).then_inc(fo_ae, 1)
                for c in range(2):
                    act.wait_ge(fo_a, 5 + c)
                    A(fA[:, c, :, LS:T], ps[:, 1 + c, 0:CH].rearrange("p (q t) -> p q t", q=2), ACT.Copy) \
                        .then_inc(fo_ae, 1)
                for m in range(2):
                    act.wait_ge(fo_b, m + 1)
                    A(yT[:, 4 + m, 0:LS], ps[:, 3 + m, :], ACT.Copy).then_inc(yc_ok, 1)
                    A(yT[:, 4 + m, LS:T], ps[:, 5 + m, 0:LP], ACT.Copy).then_inc(yc_ok, 1)
                for m in range(2):
                    act.wait_ge(at_mm, m + 1)
                    for (a, b), bank in ((GRP[0], m), (GRP[1], 2 + m)):
                        for h in range(2):
                            last = A(qraw[m * HD:(m + 1) * HD, h, a:b], ps[h * HD:(h + 1) * HD, bank, 0:b - a], ACT.Copy)
                        last.then_inc(at_ev, 1)
                act.wait_ge(at_mm, 3)
                A(kraw[:, 0:LS], ps[:, 4, :], ACT.Copy).then_inc(at_ev, 1)
                A(kraw[:, LS:T], ps[:, 5, 0:LP], ACT.Copy).then_inc(at_ev, 1)
                act.wait_ge(at_mm, 4)
                A(vtok[:, 0:4, :], ps[:, 6, :].rearrange("p (t c) -> p t c", t=4), ACT.Copy).then_inc(at_ev, 1)
                act.wait_ge(at_mm, 5)
                A(vtok[:, 4, :], ps[:, 7, P:2 * P], ACT.Copy)
                A(kvo[:, :, :], ps[:, 7, 0:256].rearrange("p (q c) -> p q c", q=2), ACT.Copy).then_inc(at_ev, 1)
                act.wait_ge(ln_ctr, 2)
                for c in range(2):
                    A(csq[:, c, :], acc[:, c, :], ACT.Square).then_inc(ln_sq, 1)
                act.wait_ge(ln_var, 1)
                A(crs[:, 0:LS], ps[:, 1, :], ACT.Sqrt, bias=epsc[:, :]).then_inc(ln_rt, 1)
                A(crs[:, LS:CONV], ps[:, 5, 0:CONV - LS], ACT.Sqrt, bias=epsc[:, :]).then_inc(ln_rt, 1)
                for c in range(2):
                    act.wait_ge(ln_out, c + 1)
                    for (a, b), o in ((GRP[0], 0), (GRP[1], PAD)):
                        A(yT[:, c, a:b], acc[:, c, a + o:b + o], ACT.Silu, scale=prmT[:, c, R_LNG:R_LNG + 1],
                          bias=prmT[:, c, R_LNB:R_LNB + 1]).then_inc(ya_ok, 1)
                for i in range(NT):
                    nk = (3, 4, 4, 3, 1)[i]
                    act.wait_ge(at_max, i + 1)
                    if i > 0:
                        act.wait_ge(at_t, 4 * i)
                    A(ast[:, 3, :], ast[:, 2, :], ACT.Exp)
                    for h in range(4):
                        A(prob[:, h, 0:nk * P], ps[:, h, 0:nk * P], ACT.Exp, bias=ast[:, 1, h:h + 1], scale=HD ** -0.5,
                          accum_out=ast[:, 4, h:h + 1]).then_inc(at_exp, 1)
                    for h in range(4):
                        act.wait_ge(at_t, 4 * i + h + 1)
                        if i > 0 and h == 0:
                            act.wait_ge(at_pv, i)
                        A(probT[:, h, 0:nk * P], ps[:, 4 + h, 0:nk * P], ACT.Copy).then_inc(at_te, 1)
                    act.wait_ge(at_pv, i + 1)
                    for q in range(2):
                        A(yT[:, 6 + q, i * P:(i + 1) * P], ps[:, 4 + q, 0:P], ACT.Copy).then_inc(yd_ok, 1)
                act.wait_ge(hy_a1, 1)
                A(h1[0:FFN, :], fa_[0:FFN, :], ACT.Sin).then_inc(hy_s1, 1)
                for m in range(6):
                    if m == 3:
                        act.wait_ge(hy_a2, 1)
                        A(h2[0:FFN, :], fa_[0:FFN, :], ACT.Sin).then_inc(hy_s2, 1)
                    act.wait_ge(hy_u, m + 1)
                    r = R_SW + 3 + m // 2
                    for (a, b), bank in ((GRP[0], m % 3), (GRP[1], 3 + m % 3)):
                        last = A(u[:, m, a:b], ps[:, bank, 0:b - a], ACT.Identity, scale=prmT[:, m % 2, r:r + 1],
                                 bias=prmT[:, m % 2, R_SB + m // 2:R_SB + m // 2 + 1])
                    last.then_inc(hy_u1, 1)
                for o in range(2):
                    for t in range(NT):
                        n = NT * o + t
                        act.wait_ge(hy_eo, n + 1)
                        if t >= 2:
                            act.wait_ge(hy_norm, n - 1)
                        A(fabs[:, t % 2, :, :], ftime[:, t % 2, :, :], ACT.Abs).then_inc(hy_abs, 1)
                    act.wait_ge(hy_k, o + 1)
                    for q in range(2):
                        A(kspec[:, q, 0:4, :], ps[:, 2 * q:2 * q + 2, :].rearrange("p b (f c) -> p (b f) c", f=2), ACT.Copy)
                        last = A(kspec[:, q, 4, :], ps[:, 4, q * CH:(q + 1) * CH], ACT.Copy)
                    last.then_inc(hy_ke, 1)
                    act.wait_ge(hy_zt, o + 1)
                    A(zs[:, 0:4, :], ps[:, 0:2, :].rearrange("p b (f c) -> p (b f) c", f=2), ACT.Copy)
                    A(zs[:, 4, :], ps[:, 2, 0:CH], ACT.Copy).then_inc(hy_z, 1)
                squares(x_mid, 16, sq_s[1])
                root(ms_s[1], rt_s[1])
                modulate(1, xn_s[1], h_s[1])
                act.wait_ge(ro_sub, 1)
                A(gexp[:, :, :], gt[:, :, :], ACT.Exp).then_inc(ro_exp, 1)
                for t in range(NT):
                    act.wait_ge(hs_mm, t + 1)
                    if t >= 2:
                        act.wait_ge(hs_st[t % 2], 16 * (t // 2))
                    for q in range(2):
                        A(htok[:, t % 2, 512 * q:512 * q + 512], ps[:, 4 + 2 * (t % 2) + q, :], ACT.Copy).then_inc(hs_ev, 1)
                act.wait_ge(ro_sub2, 1)
                A(emx[:, :], ediff[:, :], ACT.Exp).then_inc(ro_exp2, 1)
                for s in range(SLOTS):
                    act.sem_inc(xe_ok[s])
                    act.sem_inc(ye_a[s])
                act.wait_ge(ro_tab, 1)
                turns = act.value_load(nturn[0:1, 0:1], min_val=1, max_val=NBLK // 2)
                for q in range(2):
                    act.wait_ge(hs_st[q], 16 * ((NT + 1 - q) // 2))
                with act.Fori(0, turns) as j:
                    for s in range(SLOTS):
                        act.wait_ge(xt_mm[s], j + 2)
                        for q in range(2):
                            A(xe[:, s, 4 * q:4 * q + 4, :].rearrange("p k t -> p (k t)"), ps[:, q, :], ACT.Copy) \
                                .then_inc(xe_ok[s], 1)
                        act.wait_ge(g_mm[s], j + 1)
                        A(sg[:, s, :], ps[:, 2, 0:FE], ACT.Silu).then_inc(sg_ok[s], 1)
                        act.wait_ge(y_mm[s], j * 2 + 2)
                        act.wait_ge(y_out[s], j * 16 + 16)
                        A(ye[:, s, 0:512], ps[:, 6, :], ACT.Copy).then_inc(ye_a[s], 1)
                last_of_layer(act, "act")
            squares(xT_in, 2 * NT, out_sq)
            root(out_ms, out_rt)
            for k in range(KC):
                act.wait_ge(out_xn, k + 1)
                A(hT[:, k, :], hT[:, k, :], ACT.Copy, scale=nf[:, k:k + 1]).then_inc(out_h, 1)
            for t in range(NT):
                act.wait_ge(out_mm, t + 1)
                for q in range(2):
                    A(work[:, t * D:(t + 1) * D].rearrange("p (c k) -> p k c", k=KC)[:, 4 * q:4 * q + 4, :],
                      ps[:, 2 + 2 * (t % 2) + q, :].rearrange("p (k c) -> p k c", k=4), ACT.Copy).then_inc(out_ev, 1)

        @block.vector
        def _(dve):
            V = nc.vector
            chain = [0]

            def step(ins):
                chain[0] += 1
                ins.then_inc(dchain, 1)
                dve.wait_ge(dchain, chain[0])

            def bc(ap, n):
                return ap.rearrange("p (a b) -> p a b", b=1).to_broadcast([P, ap.shape[1], n])

            def row(ap, n):
                return ap.rearrange("p (b a) -> p b a", b=1).to_broadcast([P, n, ap.shape[1]])

            def normalise(rt_sem, rc_sem, xn_sem):
                dve.wait_ge(rt_sem, 2)
                V.reciprocal(rinv[:, :], rms[:, :]).then_inc(rc_sem, 1)
                dve.wait_ge(rc_sem, 1)
                for k in range(KC):
                    V.tensor_tensor(hT[:, k, :], xT[:, k, :], rinv[:, :], ALU.mult).then_inc(xn_sem, 1)

            def residual(t):
                dve.wait_ge(yc_mm, t + 1)
                for k in range(KC):
                    x = xT[:, k, t * P:(t + 1) * P]
                    g = 0 if t < 4 else 1
                    V.scalar_tensor_tensor(out=x, in0=ps[:, 2 * (t % 2) + k // 4, (k % 4) * P:(k % 4 + 1) * P],
                                           scalar=mods[:, 5, k, g:g + 1], in1=x, op0=ALU.mult, op1=ALU.add) \
                        .then_inc(x_new, 1)

            with dve.Fori(0, DEPTH):
                chain[0] = 0
                dve.wait_ge(par_mm, 1)
                V.tensor_copy(prmT[:, :, :], ps[:, 7, 0:2 * ROWS].rearrange("p (c r) -> p c r", c=2)).then_inc(par_ev, 1)
                V.tensor_copy(frowT[:, :], ps[0:FFN, 7, 100:104]).then_inc(par_ev, 1)
                V.tensor_copy(bcast[:, :], ps[:, 7, 104:144]).then_inc(par_ev, 1)
                V.tensor_copy(ckT[:, :], ps[:, 7, 144:272]).then_inc(par_ev, 1)
                dve.wait_ge(w_used, KC)
                V.tensor_tensor(mods[:, :, :, :].rearrange("p a k g -> p (a k) g"),
                                ps[:, 6, 0:96].rearrange("p (a g) -> p a g", g=2),
                                bc(ada_b[:, :, :].rearrange("p a k -> p (a k)"), 2), ALU.add).then_inc(mods_ok, 1)
                dve.wait_ge(mods_ok, 1)
                for n in range(2):
                    V.scalar_tensor_tensor(out=gain[:, n, :, :], in0=mods[:, 3 * n + 1, :, :], scalar=1.0,
                                           in1=bc(norms[:, n, :], 2), op0=ALU.add, op1=ALU.mult).then_inc(mods_ok, 1)
                normalise(rt_s[0], rc_s[0], xn_s[0])
                dve.wait_ge(xn0, KC)
                for c in range(2):
                    V.memset(glu[:, c, 0:PAD], 0.0)
                    V.memset(glu[:, c, PAD + LS:2 * PAD + LS], 0.0)
                    last = V.memset(glu[:, c, GW - PAD:GW], 0.0)
                step(last)
                for c in range(2):
                    dve.wait_ge(cv_sig, c + 1)
                    dve.wait_ge(cv_mm, 2 * c + 2)
                    V.tensor_tensor(glu[:, c, PAD:PAD + LS], ps[:, c, :], sig[:, c, 0:LS], ALU.mult)
                    V.tensor_tensor(glu[:, c, 2 * PAD + LS:2 * PAD + T], ps[:, 4 + c, 0:LP], sig[:, c, LS:T],
                                    ALU.mult).then_inc(cv_glu, 1)
                dve.wait_ge(cv_glu, 2)
                for j in range(TAPS):
                    for c in range(2):
                        if j == 0:
                            V.tensor_scalar(acc[:, c, :], glu[:, c, j:j + CONV], prmT[:, c, j:j + 1],
                                            prmT[:, c, R_DWB:R_DWB + 1], ALU.mult, ALU.add).then_inc(cv_tap, 1)
                        else:
                            dve.wait_ge(cv_tap, 2 * j + c - 1)
                            V.scalar_tensor_tensor(out=acc[:, c, :], in0=glu[:, c, j:j + CONV], scalar=prmT[:, c, j:j + 1],
                                                   in1=acc[:, c, :], op0=ALU.mult, op1=ALU.add).then_inc(cv_tap, 1)
                dve.wait_ge(ln_mm, 1)
                for c in range(2):
                    V.tensor_tensor(acc[:, c, 0:LS], acc[:, c, 0:LS], ps[:, 0, :], ALU.subtract)
                    V.tensor_tensor(acc[:, c, LS:CONV], acc[:, c, LS:CONV], ps[:, 4, 0:CONV - LS],
                                    ALU.subtract).then_inc(ln_ctr, 1)
                dve.wait_ge(ln_rt, 2)
                V.reciprocal(crn[:, :], crs[:, :]).then_inc(ln_rn, 1)
                dve.wait_ge(ln_rn, 1)
                for c in range(2):
                    V.tensor_tensor(acc[:, c, :], acc[:, c, :], crn[:, :], ALU.mult).then_inc(ln_out, 1)
                dve.wait_ge(ya_ok, 4)
                for m in range(3):
                    src, dst = (qraw[:, m, 0:LS], qrope[:, m, :]) if m < 2 else (kraw[:, 0:LS], krope[:, :])
                    dve.wait_ge(at_rot, m + 1)
                    V.tensor_tensor(rtmp[:, m, :], ps[:, m, :], rope[:, 1, :], ALU.mult)
                    step(V.tensor_tensor(dst, src, rope[:, 0, :], ALU.mult))
                    V.tensor_tensor(dst, dst, rtmp[:, m, :], ALU.add).then_inc(at_rope, 1)
                sink = bcast[:, 0:4]
                for i in range(NT):
                    nk = (3, 4, 4, 3, 1)[i]
                    dve.wait_ge(at_s, i + 1)
                    if 1 <= i < 4:
                        step(V.tensor_tensor(ps[:, 0:4, P:2 * P], ps[:, 0:4, P:2 * P], row(mask_l, 4), ALU.add))
                    if i < 3:
                        step(V.tensor_tensor(ps[:, 0:4, (nk - 1) * P:nk * P], ps[:, 0:4, (nk - 1) * P:nk * P],
                                             row(mask_r, 4), ALU.add))
                    step(V.tensor_reduce(ast[:, 0, :], ps[:, 0:4, 0:nk * P], AX.X, ALU.max))
                    step(V.scalar_tensor_tensor(out=ast[:, 5, :], in0=ast[:, 0, :], scalar=HD ** -0.5, in1=sink,
                                                op0=ALU.mult, op1=ALU.max))
                    V.tensor_scalar(ast[:, 1, :], ast[:, 5, :], -1.0, None, ALU.mult)
                    V.tensor_tensor(ast[:, 2, :], sink, ast[:, 5, :], ALU.subtract).then_inc(at_max, 1)
                    dve.wait_ge(at_exp, 4 * i + 4)
                    step(V.tensor_tensor(ast[:, 6, :], ast[:, 3, :], ast[:, 4, :], ALU.add))
                    step(V.reciprocal(ast[:, 7, :], ast[:, 6, :]))
                    V.tensor_tensor(prob[:, :, 0:nk * P], prob[:, :, 0:nk * P], bc(ast[:, 7, :], nk * P),
                                    ALU.mult).then_inc(at_prob, 1)
                dve.wait_ge(yd_ok, 2 * NT)

                def sine_argument(done):
                    a, k = fa_[0:FFN, :], fk_[0:FFN, :]
                    step(V.tensor_scalar(k, a, 1 / (2 * np.pi), MAGIC, ALU.mult, ALU.add))
                    step(V.tensor_scalar(k, k, -MAGIC, None, ALU.add))
                    step(V.scalar_tensor_tensor(out=a, in0=k, scalar=-TWO_PI_HI, in1=a, op0=ALU.mult, op1=ALU.add))
                    step(V.scalar_tensor_tensor(out=a, in0=k, scalar=-float(TWO_PI_LO), in1=a, op0=ALU.mult, op1=ALU.add))
                    V.tensor_scalar(a, a, 3.1415925, -3.1415925, ALU.min, ALU.max).then_inc(done, 1)

                def short(m):
                    dve.wait_ge(hy_u1, m + 1)
                    for tap, (oa, ob, ia, ib) in ((R_SW, (1, 0, 0, -1)), (R_SW + 6, (0, -1, 1, 0))):
                        w_ = prmT[:, m % 2, tap + m // 2:tap + m // 2 + 1]
                        for (a, b), bank in ((GRP[0], m % 3), (GRP[1], 3 + m % 3)):
                            last = V.scalar_tensor_tensor(out=u[:, m, a + oa:b + ob], in0=ps[:, bank, ia:b - a + ib], scalar=w_,
                                                          in1=u[:, m, a + oa:b + ob], op0=ALU.mult, op1=ALU.add)
                        if tap == R_SW:
                            step(last)
                    last.then_inc(hy_uc, 1)

                for n, (mm_sem, done, fb) in enumerate(((hy_m1, hy_a1, 0), (hy_m2, hy_a2, 2))):
                    dve.wait_ge(mm_sem, 1)
                    for (a, b), bank in ((GRP[0], 6), (GRP[1], 7)):
                        last = V.tensor_scalar(fa_[0:FFN, a:b], ps[0:FFN, bank, 0:b - a], frowT[:, fb:fb + 1],
                                               frowT[:, fb + 1:fb + 2], ALU.add, ALU.mult)
                    step(last)
                    sine_argument(done)
                    if n == 0:
                        V.memset(h2[FFN:FFN + 1, :], 1.0)
                        for m in range(2):
                            short(m)
                for m in range(2, 6):
                    short(m)
                for o in range(2):
                    for t in range(NT):
                        n = NT * o + t
                        dve.wait_ge(hy_f, n + 1)
                        if n == 0:
                            dve.wait_ge(hy_s2, 1)
                        if n >= 2:
                            dve.wait_ge(hy_abs, n - 1)
                        f = ftime[:, t % 2, :, :]
                        V.tensor_tensor(f, ps[:, 6 + t % 2, :].rearrange("p (q c) -> p q c", q=2), row(win[:, t, :], 2),
                                        ALU.mult).then_inc(hy_raw, 1)
                        dve.wait_ge(hy_raw, n + 1)
                        V.tensor_tensor(evod[:, t, 1, :], f[:, 0, :], f[:, 1, :], ALU.subtract)
                        if t in (0, 4):
                            step(V.tensor_tensor(evod[:, t, 0, :], f[:, 0, :], f[:, 1, :], ALU.add))
                            step(V.tensor_copy(f[0:1, 0, :], evod[0:1, t, 0, :]))
                            V.memset(f[0:1, 1, :], 0.0).then_inc(hy_eo, 1)
                        else:
                            V.tensor_tensor(evod[:, t, 0, :], f[:, 0, :], f[:, 1, :], ALU.add).then_inc(hy_eo, 1)
                    dve.wait_ge(hy_norm, NT * (o + 1))
                    step(V.tensor_scalar(rnorm[:, :], ps[:, 5, 0:4], EPS, None, ALU.add))
                    V.reciprocal(rnorm[:, :], rnorm[:, :]).then_inc(hy_rn, 1)
                    dve.wait_ge(hy_zt, o + 1)
                    for c in range(2):
                        V.tensor_scalar(u[:, c, :], u[:, c, :], prmT[:, c, R_HD + o:R_HD + o + 1], None, ALU.mult) \
                            .then_inc(hy_dz, 1)
                    dve.wait_ge(hy_fz, o + 1)
                    for (a, b), zr, zi in (((0, 4), ps[:, 0:2, :], ps[:, 2:4, :]),
                                           ((4, 5), ps[:, 4:5, 0:CH], ps[:, 4:5, CH:2 * CH])):
                        nn = (b - a) * CH
                        if a == 0:
                            flat = lambda v: v.rearrange("p (b f) c -> p b (f c)", f=2)
                            tm = ctmp[:, 0:nn].rearrange("p (b c) -> p b c", b=2)
                        else:
                            flat = lambda v: v
                            tm = ctmp[:, 4 * CH:5 * CH].rearrange("p (b c) -> p b c", b=1)
                        kr, ki = flat(kspec[:, 0, a:b, :]), flat(kspec[:, 1, a:b, :])
                        yr, yi = flat(yspec[:, 0, a:b, :]), flat(yspec[:, 1, a:b, :])
                        V.tensor_tensor(yr, zr, kr, ALU.mult)
                        step(V.tensor_tensor(tm, zi, ki, ALU.mult))
                        step(V.tensor_tensor(yr, yr, tm, ALU.subtract))
                        V.tensor_tensor(yi, zr, ki, ALU.mult)
                        step(V.tensor_tensor(tm, zi, kr, ALU.mult))
                        last = V.tensor_tensor(yi, yi, tm, ALU.add)
                        if a == 0:
                            step(last)
                    last.then_inc(hy_y, 1)
                    dve.wait_ge(hy_inv, o + 1)
                    dve.wait_ge(hy_dz, 2 * (o + 1))
                    dve.wait_ge(hy_rn, o + 1)
                    for c in range(2):
                        for g, (a, b) in enumerate(GRP):
                            src = ps[:, 6 + c, :] if g == 0 else ps[:, 4 + c, 0:P]
                            last = V.scalar_tensor_tensor(out=u[:, c, a:b], in0=src, scalar=rnorm[:, 2 * g + c:2 * g + c + 1],
                                                          in1=u[:, c, a:b], op0=ALU.mult, op1=ALU.add)
                        step(last)
                        dst = u[:, c, :] if o == 0 else yT[:, 2 + c, :]
                        V.tensor_tensor(dst, u[:, c, :], u[:, 2 + 2 * o + c, :], ALU.mult).then_inc(hy_zn, 1)
                for m in range(KC):
                    dve.wait_ge(wo_mm, m + 1)
                    for g, (a, b) in enumerate(GRP):
                        bank = m % 4 + 4 * g
                        V.scalar_tensor_tensor(out=xT[:, m, a:b], in0=ps[:, bank, 0:b - a], scalar=mods[:, 2, m, g:g + 1],
                                               in1=xT[:, m, a:b], op0=ALU.mult, op1=ALU.add).then_inc(x_mid, 1)
                normalise(rt_s[1], rc_s[1], xn_s[1])
                dve.wait_ge(ro_mm, 1)
                step(V.tensor_tensor(lg[:, :, :], ps[:, 2, 0:NT * 36].rearrange("p (t n) -> p t n", t=NT),
                                     row(bcast[:, 4:40], NT), ALU.add))
                lc, lf = lg[:, :, 0:NG], lg[:, :, NG:36]
                step(V.tensor_reduce(gmax[:, :], lc, AX.X, ALU.max))
                V.tensor_tensor(gt[:, :, :], lc, bc(gmax[:, :], NG), ALU.subtract).then_inc(ro_sub, 1)
                step(V.tensor_tensor(goh[:, :, :], lc, bc(gmax[:, :], NG), ALU.is_lt))
                step(V.scalar_tensor_tensor(out=goh[:, :, :], in0=goh[:, :, :], scalar=1000.0, in1=row(iota[:, 0:NG], NT),
                                            op0=ALU.mult, op1=ALU.add))
                step(V.tensor_reduce(gidx[:, :], goh[:, :, :], AX.X, ALU.min))
                step(V.tensor_tensor(goh[:, :, :], row(iota[:, 0:NG], NT), bc(gidx[:, :], NG), ALU.is_equal))
                step(V.tensor_scalar(goh[:, :, :], goh[:, :, :], -1.0, 1e30, ALU.add, ALU.mult))
                for g in range(NG):
                    last = V.tensor_tensor(lfm[:, :, g * EPG:(g + 1) * EPG], lf[:, :, g * EPG:(g + 1) * EPG],
                                           goh[:, :, g:g + 1].to_broadcast([P, NT, EPG]), ALU.add)
                step(last)
                for q in range(2):
                    step(V.tensor_reduce(top[q][:, :], lfm[:, :, :], AX.X, ALU.max))
                    step(V.tensor_tensor(lt[:, :, :], lfm[:, :, :], bc(top[q][:, :], NE), ALU.is_lt))
                    step(V.scalar_tensor_tensor(out=lt[:, :, :], in0=lt[:, :, :], scalar=1000.0, in1=row(iota[:, 0:NE], NT),
                                                op0=ALU.mult, op1=ALU.add))
                    step(V.tensor_reduce(tidx[:, :], lt[:, :, :], AX.X, ALU.min))
                    step(V.tensor_tensor(oh[q][:, :, :], row(iota[:, 0:NE], NT), bc(tidx[:, :], NE), ALU.is_equal))
                    if q == 0:
                        step(V.scalar_tensor_tensor(out=lfm[:, :, :], in0=oh[0][:, :, :], scalar=-3e30, in1=lfm[:, :, :],
                                                    op0=ALU.mult, op1=ALU.add))
                V.tensor_tensor(both[:, :, :], oh[0][:, :, :], oh[1][:, :, :], ALU.add).then_inc(ro_oh, 1)
                V.tensor_tensor(ediff[:, :], top[1][:, :], top[0][:, :], ALU.subtract).then_inc(ro_sub2, 1)
                dve.wait_ge(ro_exp, 1)
                step(V.tensor_reduce(gsum[:, :], gexp[:, :, :], AX.X, ALU.add))
                dve.wait_ge(ro_exp2, 1)
                step(V.scalar_tensor_tensor(out=eden[:, :], in0=emx[:, :], scalar=1.0, in1=gsum[:, :], op0=ALU.add, op1=ALU.mult))
                step(V.reciprocal(wgt[0][:, :], eden[:, :]))
                step(V.tensor_tensor(wgt[1][:, :], wgt[0][:, :], emx[:, :], ALU.mult))
                dve.wait_ge(ro_rank, 1)
                V.tensor_copy(rank[:, :, :], ps[:, 3, 0:NT * NE].rearrange("p (t n) -> p t n", t=NT))
                step(V.tensor_copy(cnt[:, :], ps[:, 3, NT * NE:(NT + 1) * NE]))
                step(V.tensor_scalar(thr[:, 0, :], iota[:, 0:NT], float(P), None, ALU.mult))
                thr0 = thr[:, 0, :]
                step(V.tensor_tensor(ebt[:, 0:NE, 0:NT], bc(cnt[:, :], NT), row(thr0, NE), ALU.is_gt))
                step(V.tensor_reduce(nbl[:, :], ebt[:, 0:NE, 0:NT], AX.X, ALU.add))
                step(V.tensor_tensor_scan(out=cum[:, :], data0=ones[:, 0:NE], data1=nbl[:, :], initial=0.0,
                                          op0=ALU.mult, op1=ALU.add))
                step(V.tensor_tensor(exc[:, :], cum[:, :], nbl[:, :], ALU.subtract))
                step(V.tensor_tensor(ebt[:, :, :], row(cum[:, :], NBLK), bc(iota[:, 0:NBLK], NE), ALU.is_le))
                step(V.tensor_reduce(ebf[:, :], ebt[:, :, :], AX.X, ALU.add))
                V.tensor_scalar(ebi[:, :], ebf[:, :], float(NE - 1), None, ALU.min)
                step(V.tensor_scalar(nturn[:, 1:2], cum[:, NE - 1:NE], 1.0, None, ALU.add))
                V.tensor_scalar(nturn[:, 0:1], nturn[:, 1:2], 1, None, ALU.arith_shift_right).then_inc(ro_tab, 1)
                for q in range(2):
                    step(V.tensor_tensor(lt[:, :, :], oh[q][:, :, :], rank[:, :, :], ALU.mult))
                    step(V.tensor_reduce(selr[:, q, :], lt[:, :, :], AX.X, ALU.add))
                    step(V.tensor_tensor(lt[:, :, :], oh[q][:, :, :], row(exc[:, :], NT), ALU.mult))
                    step(V.tensor_reduce(sele[:, q, :], lt[:, :, :], AX.X, ALU.add))
                sr = selr[:, :, :].rearrange("p a b -> p (a b)")
                se = sele[:, :, :].rearrange("p a b -> p (a b)")
                fl = flo[:, :, :].rearrange("p a b -> p (a b)")
                ft = flt[:, :, :, :].rearrange("p a b c -> p (a b) c")
                step(V.tensor_tensor(ft[:, :, 0:4], bc(sr, 4), row(thr[:, 0, 1:5], 2 * NT), ALU.is_ge))
                step(V.tensor_reduce(fl, ft[:, :, 0:4], AX.X, ALU.add))
                V.scalar_tensor_tensor(out=sr, in0=fl, scalar=-float(P), in1=sr, op0=ALU.mult, op1=ALU.add)
                step(V.tensor_tensor(se, se, fl, ALU.add))
                for t in range(NT):
                    for q in range(2):
                        V.tensor_scalar(ohs[:, t, q, :], iota[:, 0:P], selr[:, q, t:t + 1], None, ALU.is_equal)
                        last = V.tensor_scalar(ohb[:, t, q, :], iota[:, 0:NBLK], sele[:, q, t:t + 1],
                                               iota[:, P + t * TOPK + q:P + t * TOPK + q + 1], ALU.is_equal, ALU.mult)
                last.then_inc(ro_1h, 1)
                dve.wait_ge(ro_tm, 1)
                step(V.tensor_scalar(tabz[:, :], ps[:, 2, 256:256 + NBLK], 0.0, 8192.0, ALU.is_equal, ALU.mult))
                step(V.scalar_tensor_tensor(out=tabf[:, :], in0=ps[:, 2, 256:256 + NBLK], scalar=-1.0, in1=tabz[:, :],
                                            op0=ALU.add, op1=ALU.add))
                step(V.tensor_copy(tabs[:, 1, :], tabf[:, :]))
                V.tensor_scalar(tabs[:, 0, :], tabs[:, 1, :], 1, None, ALU.arith_shift_right).then_inc(ro_tok, 1)
                for s in range(SLOTS):
                    dve.sem_inc(hh_ok[s])
                    dve.sem_inc(he_ok[s])
                    dve.sem_inc(ye_d[s])
                turns = dve.value_load(nturn[0:1, 0:1], min_val=1, max_val=NBLK // 2)
                with dve.Fori(0, turns) as j:
                    for s in range(SLOTS):
                        dve.wait_ge(sg_ok[s], j + 1)
                        dve.wait_ge(u_mm[s], j + 1)
                        V.tensor_tensor(hh[:, s, :], sg[:, s, :], ps[:, 3, 0:FE], ALU.mult).then_inc(hh_ok[s], 1)
                        dve.wait_ge(ht_mm[s], j + 1)
                        V.tensor_copy(he[:, s, :, :].rearrange("p k t -> p (k t)"), ps[:, 4, 0:2 * P]).then_inc(he_ok[s], 1)
                        dve.wait_ge(y_mm[s], j * 2 + 3)
                        dve.wait_ge(y_out[s], j * 16 + 16)
                        V.tensor_copy(ye[:, s, 512:1024], ps[:, 7, :]).then_inc(ye_d[s], 1)
                for s in range(SLOTS):
                    dve.wait_ge(y_out[s], turns * 16 + 16)
                for t in range(NT):
                    dve.wait_ge(yc_in[t % 2], 16 * (t // 2 + 1))
                    if t >= 2:
                        dve.wait_ge(yc_mm, t - 1)
                    step(V.tensor_scalar(ysum[:, t % 2, :], ycomb[:, t % 2, 0, :], wgt[0][:, t:t + 1], None, ALU.mult))
                    V.scalar_tensor_tensor(out=ysum[:, t % 2, :], in0=ycomb[:, t % 2, 1, :], scalar=wgt[1][:, t:t + 1],
                                           in1=ysum[:, t % 2, :], op0=ALU.mult, op1=ALU.add).then_inc(yc_sum, 1)
                    if t >= 1:
                        residual(t - 1)
                residual(NT - 1)
                last_of_layer(dve, "dve")
            normalise(out_rt, out_rc, out_xn)


INPUTS = ("x_prompt x_sample cache_k cache_v c c_ctx ada_w ada_b norm1_g norm2_g w_in conv_dw_w conv_dw_b "
          "conv_ln_g conv_ln_b hy_short_w hy_short_b hy_fw1 hy_fb1 hy_freq1 hy_fw2 hy_fb2 hy_freq2 hy_fw3 hy_fb3 "
          "hy_d attn_sink w_out router_coarse_w router_coarse_b router_fine_w router_fine_b exp_gate exp_up "
          "exp_down norm_f_g").split()
OUTPUTS = {"y_prompt": (1, LP, D), "y_sample": (1, LS, D), "state_k": (1, DEPTH, LP, 2, HD),
           "state_v": (1, DEPTH, LP, 2, HD)}


def program(nc, arrays):
    io = {}
    for name, a in arrays.items():
        io[name] = nc.dram_tensor("in_" + name, a.shape, mybir.dt.from_np(a.dtype), kind="ExternalInput").ap()
    out = {n: nc.dram_tensor("out_" + n, s, F32, kind="ExternalOutput").ap() for n, s in OUTPUTS.items()}
    trunk(nc, io, out)


def kernel(**inputs):
    import concourse.bacc as bacc
    from concourse.bass_utils import run_bass_kernel_spmd

    arrays = {n: np.ascontiguousarray(inputs[n]) for n in INPUTS}
    arrays.update({"c_" + n: a for n, a in constants().items()})
    nc = bacc.Bacc("TRN2", target_bir_lowering=False, num_devices=1)
    program(nc, arrays)
    r = run_bass_kernel_spmd(nc, [{"in_" + n: a for n, a in arrays.items()}], core_ids=[0])
    return tuple(r.results[0]["out_" + n] for n in OUTPUTS)
```

```python
import numpy as np
import concourse.bass as bass
from concourse import mybir
from contextlib import ExitStack

F32 = mybir.dt.float32
I32 = mybir.dt.int32
U32 = mybir.dt.uint32
ALU = mybir.AluOpType
ACT = mybir.ActivationFunctionType
AX = mybir.AxisListType

P = 128
D = 1024
KC = D // P
LS, LP = 512, 128
T = LS + LP
NT = T // P
DEPTH = 2
CH = 256
TAPS = 31
PAD = TAPS // 2
CONV = LS + PAD + LP
FFN = 64
EMB = 33
HD = 64
NG, EPG, NE, FE = 4, 8, 32, 256
TOPK = 2
GRID_W = 64
EPS = 1e-6
NEG = -1e30
SLOTS = 2
NBLK = 42
WSLOT = 6 * D
TWO_PI_HI = 6.28125
TWO_PI_LO = 2.0 * np.pi - TWO_PI_HI
MAGIC = 12582912.0
ROWS = TAPS + 3 + 9 + 3 + 2
R_DWB, R_LNG, R_LNB, R_SW, R_SB, R_HD = TAPS, TAPS + 1, TAPS + 2, TAPS + 3, TAPS + 12, TAPS + 15


def constants():
    c = {}
    f = lambda a: np.ascontiguousarray(a, dtype=np.float32)

    def tile_rows(a):
        return a.reshape(-1, P, a.shape[-1]).transpose(1, 0, 2)

    for n, L in (("s", LS), ("p", LP)):
        t = np.arange(L, dtype=np.float64)
        w = 2 * np.pi * np.outer(t, np.arange(L) + 0.5) / (2 * L)
        c["fwd_" + n] = f(tile_rows(np.concatenate([np.cos(w), -np.sin(w)], axis=1)))
        c["inv_" + n] = f(tile_rows(np.concatenate([np.cos(w.T), -np.sin(w.T)], axis=0) / L))
        g = 2 * np.pi * (np.outer(t, t) % L) / L
        c["mix_" + n] = f(tile_rows(np.concatenate([np.cos(g), np.sin(g)], axis=1) / np.sqrt(L * CH)))
    t = np.arange(CH, dtype=np.float64)
    g = 2 * np.pi * (np.outer(t, t) % CH) / CH
    c["mix_c"] = f(tile_rows(np.concatenate([np.cos(g), -np.sin(g)], axis=1)))
    feat, win = [], []
    nb = (EMB - 1) // 2
    fr = np.linspace(1e-4, nb - 1, nb)
    lo, hi = np.log(1e-2) / 1.5, np.log(1e-2) / 0.3
    for L in (LS, LP):
        t = np.linspace(0.0, 1.0, L)[:, None]
        w = 2 * np.pi * np.arange(L)[:, None] / L
        feat.append(np.concatenate([t, np.cos(fr * w), -np.sin(fr * w)], axis=1))
        win.append(np.exp(-t * np.abs(np.linspace(lo, hi, CH))[None]) + 0.05)
    c["feat"] = f(np.concatenate(feat).T)
    c["win"] = f(tile_rows(np.concatenate(win)))
    tok = np.arange(LS)
    inv = 10000.0 ** (-np.arange(16) / 16)
    ang = np.concatenate([(tok // GRID_W)[:, None] * inv, (tok % GRID_W)[:, None] * inv], axis=1)
    c["rope"] = f(np.stack([np.tile(np.cos(ang).T, (4, 1)), np.tile(np.sin(ang).T, (4, 1))], axis=1))
    rot = np.zeros((P, P))
    for h in range(2):
        for d in range(32):
            rot[h * 64 + 32 + d, h * 64 + d] = -1
            rot[h * 64 + d, h * 64 + 32 + d] = 1
    i = np.arange(P)
    left = np.where(i[None] < i[:, None], NEG, 0)
    right = np.where(i[None] > i[:, None], NEG, 0)
    c["sq"] = f(np.stack([np.eye(P), np.ones((P, P)), np.full((P, P), 1 / D), np.full((P, P), 1 / CH),
                          rot, i[:, None] < i[None], left, right], axis=1))
    val = (np.arange(NT)[None, :, None] * P + i[:, None, None]) * TOPK + np.arange(TOPK)[None, None] + 1
    row = lambda n: np.tile(np.arange(n)[None], (P, 1))
    c["iota"] = f(np.concatenate([row(P), val.reshape(P, NT * TOPK)], axis=1))
    return c


def trunk(nc, io, out):
    ctx = ExitStack()
    with ctx:
        def sem(name):
            return ctx.enter_context(nc.semaphore(name))

        words = [0]

        def sb(name, shape, dt=F32):
            return ctx.enter_context(nc.sbuf_tensor(name, shape, dt))

        xT = sb("xT", [P, KC, T])
        hT = sb("hT", [P, KC, T])
        yT = sb("yT", [P, KC, T])
        ring = sb("ring", [P, SLOTS, WSLOT])
        dft = sb("dft", [P, 4, 2 * LS])
        inv_s = sb("inv_s", [P, 8, LS])
        fwd_p = sb("fwd_p", [P, 1, 2 * LP])
        inv_p = sb("inv_p", [P, 2, LP])
        mix_p = sb("mix_p", [P, 1, 2 * LP])
        mix_c = sb("mix_c", [P, 2, 2 * CH])
        feat = sb("feat", [EMB, T])
        win = sb("win", [P, NT, CH])
        rope = sb("rope", [P, 2, LS])
        sq = sb("sq", [P, 8, P])
        ident, ones, mean_d, mean_c, rot, tri, mask_l, mask_r = [sq[:, i, :] for i in range(8)]
        iota = sb("iota", [P, P + NT * TOPK])
        epsc = sb("epsc", [P, 1])
        c_raw = sb("c_raw", [P, 2, KC])
        c_act = sb("c_act", [P, KC, 2])
        nf = sb("nf", [P, KC])
        ada_b = sb("ada_bs", [P, 6, KC])
        norms = sb("norms", [P, 2, KC])
        prm = sb("prm", [ROWS, CH])
        prmT = sb("prmT", [P, 2, ROWS])
        frow = sb("frow", [4, FFN])
        frowT = sb("frowT", [FFN, 4])
        fw1 = sb("fw1", [EMB, FFN])
        fw2 = sb("fw2", [FFN, FFN])
        fw3 = sb("fw3", [FFN + 1, 2, 2, CH])
        brow = sb("brow", [1, 40])
        bcast = sb("bcast", [P, 40])
        wr = sb("wr", [P, KC, 36])
        ckv = sb("ckv", [P, 2, P])
        ckT = sb("ckT", [P, P])
        mods = sb("mods", [P, 6, KC, 2])
        gain = sb("gain", [P, 2, KC, 2])
        WORK = 8192
        work = sb("work", [P, WORK])

        def at(base, off, *dims):
            n = int(np.prod(dims))
            v = base[:, off:off + n]
            if len(dims) == 1:
                return v
            names = "abcd"[:len(dims)]
            return v.rearrange("p (" + " ".join(names) + ") -> p " + " ".join(names),
                               **{x: d for x, d in zip(names[1:], dims[1:])})

        hflat = hT[:, :, :].rearrange("p k t -> p (k t)")
        yflat = yT[:, :, :].rearrange("p k t -> p (k t)")
        rms = at(work, 0, T)
        rinv = at(work, T, T)
        GW = PAD + CONV + PAD
        glu = at(work, 0, 2, GW)
        acc = at(work, 2 * GW, 2, CONV)
        sig = at(work, 2 * GW + 2 * CONV, 2, T)
        crs = at(work, 2 * GW + 2 * CONV, CONV)
        crn = at(work, 2 * GW + 2 * CONV + CONV, CONV)
        csq = at(work, 0, 2, CONV)
        fX = at(work, WORK - 3840, NT, CH)
        fA = at(work, WORK - 2560, 2, 2, T)
        qraw = at(work, WORK - 2560, 2, T)
        kraw = at(work, WORK - 1280, T)
        vtok = at(work, WORK - 640, NT, P)
        qrope = at(work, 0, 2, LS)
        krope = at(work, 1024, LS)
        prob = at(work, 1536, 4, 512)
        probT = at(work, 3584, 4, 512)
        rtmp = at(work, 1536, 3, LS)
        otok = at(work, 5632, 256)
        ast = sb("ast", [P, 2, 8, 4])
        kvo = sb("kvo", [P, 2, P])
        u = at(work, 0, 6, T)
        zs = at(work, 3840, NT, CH)
        ctmp = at(work, 5120, NT * CH)
        h1 = at(work, 2 * T, T)
        h2 = at(work, 3 * T, T)
        fa_ = at(work, 4 * T, T)
        fk_ = at(work, 5 * T, T)
        ftime = at(work, 6 * T, 2, 2, CH)
        fabs = at(work, 6 * T + 1024, 2, 2, CH)
        fsum = at(work, 6 * T + 2048, 2, 2, CH)
        adarow = at(work, 2 * T, 2 * D)
        kspec = at(hflat, 0, 2, NT, CH)
        yspec = at(hflat, 2560, 2, NT, CH)
        evod = at(yflat, 0, NT, 2, CH)
        knew = at(yflat, 2560, 2, NT, CH)
        rnorm = sb("rnorm", [P, 2, 4])
        xg = at(work, 0, SLOTS, D)
        xe = at(work, 2048, SLOTS, KC, P)
        ye = at(work, 4096, SLOTS, D)
        sg = at(work, 6144, SLOTS, FE)
        hh = at(work, 6656, SLOTS, FE)
        he = at(work, 7168, SLOTS, 2, P)
        htok = ye
        ycomb = at(work, 0, 2, TOPK, D)
        ysum = at(work, 4096, 2, D)
        R = [0]

        def rt(*dims):
            o = R[0]
            R[0] += int(np.prod(dims))
            return at(yflat, o, *dims)

        lg = rt(NT, 36)
        gmax = rt(NT)
        gidx = rt(NT)
        goh = rt(NT, NG)
        gexp = rt(NT, NG)
        gt = rt(NT, NG)
        gsum = rt(NT)
        lfm = rt(NT, NE)
        lt = rt(NT, NE)
        oh = [rt(NT, NE) for _ in range(2)]
        top = [rt(NT) for _ in range(2)]
        tidx = rt(NT)
        both = rt(NT, NE)
        ediff = rt(NT)
        emx = rt(NT)
        eden = rt(NT)
        wgt = [rt(NT) for _ in range(2)]
        rank = rt(NT, NE)
        cnt = rt(NE)
        nbl = rt(NE)
        cum = rt(NE)
        exc = rt(NE)
        thr = rt(NE, NT)
        selr = rt(2, NT)
        sele = rt(2, NT)
        flo = rt(2, NT)
        flt = rt(2, NT, NT)
        ohb = rt(NT, 2, NBLK + SLOTS)
        ohs = rt(NT, 2, P)
        ebt = rt(NBLK, NE)
        ebf = rt(NBLK)
        tabf = rt(NBLK + SLOTS)
        tabz = rt(NBLK + SLOTS)
        assert R[0] <= KC * T, R
        ebi = sb("ebi", [P, NBLK], I32)
        nturn = sb("nturn", [P, 2], I32)
        tabs = sb("tabs", [P, 2, NBLK + SLOTS], I32)
        icol = sb("icol", [P, SLOTS, 2], I32)

        ps = ctx.enter_context(nc.psum_tensor("ps", [P, 8, 512], F32))

        H_dram = nc.dram_tensor("h_scratch", (T, D), F32, kind="Internal").ap()
        K_dram = nc.dram_tensor("k_scratch", (2, P, 2 * NT * CH), F32, kind="Internal").ap()
        Y_dram = nc.dram_tensor("y_scratch", (T * TOPK, D), F32, kind="Internal").ap()

        const_in = sem("const_in")
        cond_in = sem("cond_in")
        x_in = sem("x_in")
        set_up = sem("set_up")
        c_ready = sem("c_ready")
        xT_mm = sem("xT_mm")
        xT_in = sem("xT_in")
        arrived = sem("layer_arrived")
        go = {e: sem("layer_go_" + e) for e in ("pe", "act", "dve", "pool")}
        out_st = sem("out_st")

        w_full0 = sem("w_full0")
        w_full1 = sem("w_full1")
        w_used = sem("w_used")
        cs_in = sem("cs_in")
        f_in = sem("f_in")
        par_in = sem("par_in")
        fpar_in = sem("fpar_in")
        row_mm = sem("row_mm")
        row_ev = sem("row_ev")
        ada_t = sem("ada_t")
        par_mm = sem("par_mm")
        par_ev = sem("par_ev")
        mods_ok = sem("mods_ok")
        dchain = sem("dchain")
        sq0 = sem("sq0")
        ss0 = sem("ss0")
        ms0 = sem("ms0")
        rt0 = sem("rt0")
        rc0 = sem("rc0")
        xn0 = sem("xn0")
        h0 = sem("h0")
        sq1 = sem("sq1")
        ss1 = sem("ss1")
        ms1 = sem("ms1")
        rt1 = sem("rt1")
        rc1 = sem("rc1")
        xn1 = sem("xn1")
        h1s = sem("h1s")
        cv_mm = sem("cv_mm")
        cv_sig = sem("cv_sig")
        cv_glu = sem("cv_glu")
        cv_tap = sem("cv_tap")
        ln_mm = sem("ln_mm")
        ln_ctr = sem("ln_ctr")
        ln_sq = sem("ln_sq")
        ln_var = sem("ln_var")
        ln_rt = sem("ln_rt")
        ln_rn = sem("ln_rn")
        ln_out = sem("ln_out")
        ya_ok = sem("ya_ok")
        fo_x = sem("fo_x")
        fo_xe = sem("fo_xe")
        fo_a = sem("fo_a")
        fo_ae = sem("fo_ae")
        fo_b = sem("fo_b")
        yc_ok = sem("yc_ok")
        at_mm = sem("at_mm")
        at_ev = sem("at_ev")
        at_rot = sem("at_rot")
        at_rope = sem("at_rope")
        kv_out = sem("kv_out")
        at_s = sem("at_s")
        at_max = sem("at_max")
        at_exp = sem("at_exp")
        at_prob = sem("at_prob")
        at_t = sem("at_t")
        at_te = sem("at_te")
        at_pv = sem("at_pv")
        at_o = sem("at_o")
        at_ot = sem("at_ot")
        yd_ok = sem("yd_ok")
        hy_m1 = sem("hy_m1")
        hy_a1 = sem("hy_a1")
        hy_s1 = sem("hy_s1")
        hy_m2 = sem("hy_m2")
        hy_a2 = sem("hy_a2")
        hy_s2 = sem("hy_s2")
        hy_u = sem("hy_u")
        hy_u1 = sem("hy_u1")
        hy_uc = sem("hy_uc")
        hy_f = sem("hy_f")
        hy_raw = sem("hy_raw")
        hy_abs = sem("hy_abs")
        hy_eo = sem("hy_eo")
        hy_norm = sem("hy_norm")
        hy_rn = sem("hy_rn")
        hy_k = sem("hy_k")
        hy_ke = sem("hy_ke")
        hy_sum = sem("hy_sum")
        k_out = sem("k_out")
        k_in = sem("k_in")
        hy_zt = sem("hy_zt")
        hy_z = sem("hy_z")
        hy_dz = sem("hy_dz")
        hy_fz = sem("hy_fz")
        hy_y = sem("hy_y")
        hy_inv = sem("hy_inv")
        hy_zn = sem("hy_zn")
        wo_mm = sem("wo_mm")
        x_mid = sem("x_mid")
        hs_mm = sem("hs_mm")
        hs_ev = sem("hs_ev")
        hs_st0 = sem("hs_st0")
        hs_st1 = sem("hs_st1")
        ro_mm = sem("ro_mm")
        ro_sub = sem("ro_sub")
        ro_exp = sem("ro_exp")
        ro_oh = sem("ro_oh")
        ro_rank = sem("ro_rank")
        ro_sub2 = sem("ro_sub2")
        ro_exp2 = sem("ro_exp2")
        ro_tab = sem("ro_tab")
        ro_1h = sem("ro_1h")
        ro_tm = sem("ro_tm")
        ro_tok = sem("ro_tok")
        wg_full0 = sem("wg_full0")
        wg_full1 = sem("wg_full1")
        wd_full0 = sem("wd_full0")
        wd_full1 = sem("wd_full1")
        ic0 = sem("ic0")
        ic1 = sem("ic1")
        xg_in0 = sem("xg_in0")
        xg_in1 = sem("xg_in1")
        xt_mm0 = sem("xt_mm0")
        xt_mm1 = sem("xt_mm1")
        xe_ok0 = sem("xe_ok0")
        xe_ok1 = sem("xe_ok1")
        g_mm0 = sem("g_mm0")
        g_mm1 = sem("g_mm1")
        u_mm0 = sem("u_mm0")
        u_mm1 = sem("u_mm1")
        sg_ok0 = sem("sg_ok0")
        sg_ok1 = sem("sg_ok1")
        hh_ok0 = sem("hh_ok0")
        hh_ok1 = sem("hh_ok1")
        ht_mm0 = sem("ht_mm0")
        ht_mm1 = sem("ht_mm1")
        he_ok0 = sem("he_ok0")
        he_ok1 = sem("he_ok1")
        y_mm0 = sem("y_mm0")
        y_mm1 = sem("y_mm1")
        ye_a0 = sem("ye_a0")
        ye_a1 = sem("ye_a1")
        ye_d0 = sem("ye_d0")
        ye_d1 = sem("ye_d1")
        y_out0 = sem("y_out0")
        y_out1 = sem("y_out1")
        pool_nop = sem("pool_nop")
        yc_in0 = sem("yc_in0")
        yc_in1 = sem("yc_in1")
        yc_sum = sem("yc_sum")
        yc_mm = sem("yc_mm")
        x_new = sem("x_new")
        layer_range = range(w_full0.num, x_new.num + 1)
        assert len(layer_range) == 143, "the layer's semaphores lie in one range"
        w_full = [w_full0, w_full1]
        wg_full = [wg_full0, wg_full1]
        wd_full = [wd_full0, wd_full1]
        hs_st = [hs_st0, hs_st1]
        ic = [ic0, ic1]
        xg_in = [xg_in0, xg_in1]
        xt_mm = [xt_mm0, xt_mm1]
        xe_ok = [xe_ok0, xe_ok1]
        g_mm = [g_mm0, g_mm1]
        u_mm = [u_mm0, u_mm1]
        sg_ok = [sg_ok0, sg_ok1]
        hh_ok = [hh_ok0, hh_ok1]
        ht_mm = [ht_mm0, ht_mm1]
        he_ok = [he_ok0, he_ok1]
        y_mm = [y_mm0, y_mm1]
        ye_a = [ye_a0, ye_a1]
        ye_d = [ye_d0, ye_d1]
        y_out = [y_out0, y_out1]
        yc_in = [yc_in0, yc_in1]
        sq_s, ss_s, ms_s, rt_s, rc_s, xn_s, h_s = (sq0, sq1), (ss0, ss1), (ms0, ms1), (rt0, rt1), (rc0, rc1), (xn0, xn1), (h0, h1s)

        I_CONV, I_FOUR, I_ATT, I_HY, I_OUT = 8, 9, 10, 11, 12
        ITEMS = 14

        def wait_item(eng, i):
            eng.wait_ge(w_full[i % SLOTS], 16 * (i // SLOTS + 1))

        def slot(i, *dims):
            return at(ring[:, i % SLOTS, :], 0, *dims)

        GRP = ((0, LS), (LS, T))

        def last_of_layer(eng, name):
            eng.drain().then_inc(arrived, 1)
            eng.wait_ge(go[name], 1)
            eng.sem_clear(go[name])

        block = ctx.enter_context(nc.Block())

        @block.sync
        def _(sp):
            sp.dma_start(work[:, 0:NT * D].rearrange("p (t d) -> p t d", t=NT)[:, 0:4, :],
                         io["x_sample"][0].rearrange("(t p) d -> p t d", p=P)).then_inc(x_in, 16)
            sp.dma_start(work[:, 4 * D:NT * D], io["x_prompt"][0]).then_inc(x_in, 16)
            for dst, name in ((sq, "sq"), (iota, "iota"), (mix_c, "mix_c"), (mix_p, "mix_p"), (fwd_p, "fwd_p"),
                              (inv_p, "inv_p"), (feat, "feat"), (win, "win"), (rope, "rope"), (inv_s, "inv_s")):
                full = dst[:, :] if len(dst.shape) == 2 else dst[:, :, :]
                sp.dma_start(full, io["c_" + name]).then_inc(const_in, 16)
            with sp.Fori(0, DEPTH) as l:
                ada = io["ada_w"][l].rearrange("(p k) n -> p k n", k=KC)
                win_l = io["w_in"][l].rearrange("(p k) n -> p k n", k=KC)
                wout_l = io["w_out"][l].rearrange("(i p) n -> p i n", p=P)
                for i in range(KC):
                    if i >= SLOTS:
                        sp.wait_ge(w_used, i - SLOTS + 1)
                    sp.dma_start(slot(i, WSLOT), ada[:, i, :]).then_inc(w_full[i % SLOTS], 16)
                    if i == 1:
                        sp.dma_start(dft[:, :, :], io["c_fwd_s"]).then_inc(f_in, 16)
                for i, lo, n, used, count in ((I_CONV, 0, 512, w_used, KC - 1), (I_FOUR, 1280, 256, w_used, KC),
                                              (I_ATT, 1536, 512, cv_mm, 4), (I_HY, 512, 768, fo_x, NT)):
                    sp.wait_ge(used, count)
                    if i == I_FOUR:
                        sp.wait_ge(hy_k, 6)
                        sp.dma_start(dft[:, :, :], io["c_mix_s"]).then_inc(cs_in, 16)
                    sp.dma_start(slot(i, KC, n), win_l[:, :, lo:lo + n]).then_inc(w_full[i % SLOTS], 16)
                sp.wait_ge(fo_a, 6)
                sp.dma_start(dft[:, :, :], io["c_fwd_s"]).then_inc(f_in, 16)
                for i, used, count in ((I_OUT, at_mm, 5), (I_OUT + 1, hy_u, 6)):
                    sp.wait_ge(used, count)
                    if used is hy_u:
                        sp.wait_ge(k_out, 32)
                        sp.dma_start(kspec.rearrange("p q t c -> p (q t c)"), K_dram[0]).then_inc(k_in, 16)
                    h = i - I_OUT
                    sp.dma_start(slot(i, 4, D), wout_l[:, 4 * h:4 * h + 4, :]).then_inc(w_full[i % SLOTS], 16)
                sp.wait_ge(hy_y, 1)
                sp.dma_start(kspec.rearrange("p q t c -> p (q t c)"), K_dram[1]).then_inc(k_in, 16)
                for t in range(NT):
                    sp.wait_ge(hs_ev, 2 * t + 2)
                    sp.dma_start(H_dram[t * P:(t + 1) * P, :], htok[:, t % 2, :]).then_inc(hs_st[t % 2], 16)
                sp.wait_ge(wo_mm, KC)
                sp.wait_ge(ro_tab, 1)
                turns = sp.value_load(nturn[0:1, 0:1], min_val=1, max_val=NBLK // 2)
                with sp.Fori(0, turns) as j:
                    for s in range(SLOTS):
                        e = sp.value_load(ebi[0:1, bass.ds(j * SLOTS + s, 1)], min_val=0, max_val=NE - 1)
                        sp.wait_ge(y_mm[s], j * 2 + 1)
                        gw = slot(s, 3, KC * FE)
                        for q, name in ((0, "exp_gate"), (1, "exp_up")):
                            src = io[name].rearrange("l e (p k) f -> (l e) p (k f)", k=KC)
                            sp.dma_start(gw[:, q, :], src[l * NE + e]).then_inc(wg_full[s], 16)
                        src = io["exp_down"].rearrange("l e (p k) f -> (l e) p (k f)", k=2)
                        sp.dma_start(gw[:, 2, :], src[l * NE + e]).then_inc(wd_full[s], 16)
                for s in range(SLOTS):
                    sp.wait_ge(y_out[s], turns * 16 + 16)
                yrow = Y_dram.rearrange("(t p k) d -> t p (k d)", p=P, k=TOPK)
                for t in range(NT):
                    if t >= 2:
                        sp.wait_ge(yc_sum, t - 1)
                    sp.dma_start(ycomb[:, t % 2, :, :].rearrange("p k d -> p (k d)"), yrow[t]) \
                        .then_inc(yc_in[t % 2], 16)
                sp.wait_ge(kv_out, 32)
                sp.wait_ge(arrived, 4)
                sp.sem_clear(layer_range)
                sp.sem_clear(arrived)
                for e in ("pe", "act", "dve", "pool"):
                    sp.sem_inc(go[e])
            for t in range(NT):
                sp.wait_ge(hs_ev, 2 * t + 2)
                dst = out["y_sample"][0, t * P:(t + 1) * P, :] if t < 4 else out["y_prompt"][0]
                sp.dma_start(dst, work[:, t * D:(t + 1) * D]).then_inc(out_st, 16)
            sp.wait_ge(out_st, 16 * NT)

        @block.gpsimd
        def _(pool):
            pool.dma_start(c_raw[:, 0, :], io["c"][0].rearrange("(p k) -> p k", k=KC)).then_inc(cond_in, 16)
            pool.dma_start(c_raw[:, 1, :], io["c_ctx"].rearrange("(p k) -> p k", k=KC)).then_inc(cond_in, 16)
            pool.dma_start(nf[:, :], io["norm_f_g"].rearrange("(p k) -> p k", k=KC)).then_inc(cond_in, 16)
            pool.memset(epsc[:, :], EPS).then_inc(set_up, 1)
            with pool.Fori(0, DEPTH) as l:
                for dst, src in (
                        (frow[0:1, :], io["hy_fb1"][l].rearrange("(a c) -> a c", a=1)),
                        (frow[1:2, :], io["hy_freq1"][l].rearrange("(a c) -> a c", a=1)),
                        (frow[2:3, :], io["hy_fb2"][l].rearrange("(a c) -> a c", a=1)),
                        (frow[3:4, :], io["hy_freq2"][l].rearrange("(a c) -> a c", a=1)),
                        (fw1[:, :], io["hy_fw1"][l]),
                        (fw2[:, :], io["hy_fw2"][l]),
                        (fw3[0:FFN, :, :, :].rearrange("p a b c -> p (a b c)"), io["hy_fw3"][l]),
                        (fw3[FFN:FFN + 1, :, :, :].rearrange("p a b c -> p (a b c)"),
                         io["hy_fb3"][l].rearrange("(a c) -> a c", a=1))):
                    pool.dma_start(dst, src).then_inc(fpar_in, 16)
                for dst, src in (
                        (ada_b[:, :, :], io["ada_b"][l].rearrange("(a p k) -> p a k", a=6, k=KC)),
                        (norms[:, 0, :], io["norm1_g"][l].rearrange("(p k) -> p k", k=KC)),
                        (norms[:, 1, :], io["norm2_g"][l].rearrange("(p k) -> p k", k=KC)),
                        (prm[0:TAPS, :], io["conv_dw_w"][l]),
                        (prm[R_DWB:R_DWB + 1, :], io["conv_dw_b"][l].rearrange("(a c) -> a c", a=1)),
                        (prm[R_LNG:R_LNG + 1, :], io["conv_ln_g"][l].rearrange("(a c) -> a c", a=1)),
                        (prm[R_LNB:R_LNB + 1, :], io["conv_ln_b"][l].rearrange("(a c) -> a c", a=1)),
                        (prm[R_SW:R_SW + 9, :], io["hy_short_w"][l].rearrange("j (g c) -> (j g) c", c=CH)),
                        (prm[R_SB:R_SB + 3, :], io["hy_short_b"][l].rearrange("(g c) -> g c", c=CH)),
                        (prm[R_HD:R_HD + 2, :], io["hy_d"][l]),
                        (brow[:, 0:4], io["attn_sink"][l].rearrange("(a c) -> a c", a=1)),
                        (brow[:, 4:8], io["router_coarse_b"][l].rearrange("(a c) -> a c", a=1)),
                        (brow[:, 8:40], io["router_fine_b"][l].rearrange("(a c) -> a c", a=1)),
                        (wr[:, :, 0:4], io["router_coarse_w"][l].rearrange("(p k) n -> p k n", k=KC)),
                        (wr[:, :, 4:36], io["router_fine_w"][l].rearrange("(p k) n -> p k n", k=KC)),
                        (ckv[:, 0, :], io["cache_k"][0, l].rearrange("t h d -> t (h d)")),
                        (ckv[:, 1, :], io["cache_v"][0, l].rearrange("t h d -> t (h d)"))):
                    pool.dma_start(dst, src).then_inc(par_in, 16)
                for o in range(2):
                    for t in range(NT):
                        pool.wait_ge(hy_abs, NT * o + t + 1)
                        g = 0 if t < 4 else 1
                        if t == 0 and o:
                            pool.wait_ge(hy_norm, 1)
                        if t in (0, 4):
                            last = pool.tensor_copy(fsum[:, g, :, :], fabs[:, t % 2, :, :])
                        else:
                            last = pool.tensor_tensor(fsum[:, g, :, :], fsum[:, g, :, :], fabs[:, t % 2, :, :], ALU.add)
                        last.then_inc(hy_sum, 1)
                        pool.wait_ge(hy_sum, 7 * o + t + 1)
                    for g in range(2):
                        pool.tensor_tensor(fsum[:, g, 0, :], fsum[:, g, 0, :], fsum[:, g, 1, :], ALU.add).then_inc(hy_sum, 1)
                pool.wait_ge(at_ev, 8)
                for q, name in ((0, "state_k"), (1, "state_v")):
                    pool.dma_start(out[name][0, l].rearrange("t h d -> t (h d)"), kvo[:, q, :]).then_inc(kv_out, 16)
                pool.wait_ge(xn1, KC)
                for s in range(SLOTS):
                    pool.dma_start(xg[:, s, :], io["x_prompt"][0]).then_inc(y_out[s], 16)
                for s in range(SLOTS):
                    pool.wait_ge(y_out[s], 16)
                for q in range(2):
                    pool.wait_ge(hs_st[q], 16 * ((NT + 1 - q) // 2))
                pool.wait_ge(ro_tok, 1)
                turns = pool.value_load(nturn[0:1, 0:1], min_val=1, max_val=NBLK // 2)

                def gather_rows(s):
                    pool.indirect_dma_start(
                        xg[:, s, :], None, H_dram[:, :],
                        bass.IndirectOffsetOnAxis(ap=icol[:, s, 0:1].bitcast(U32), axis=0),
                        bounds_check=T - 1, oob_is_err=False).then_inc(xg_in[s], 16)

                for s in range(SLOTS):
                    pool.tensor_copy(icol[:, s, 0:1], tabs[:, 0, s:s + 1]).then_inc(ic[s], 1)
                for s in range(SLOTS):
                    pool.wait_ge(ic[s], 1)
                    gather_rows(s)
                with pool.Fori(0, turns) as j:
                    for s in range(SLOTS):
                        pool.wait_ge(xg_in[s], j * 16 + 16)
                        pool.sem_inc(pool_nop)
                        pool.wait_ge(y_out[s], j * 16 + 16)
                        pool.sem_inc(pool_nop)
                        pool.tensor_copy(icol[:, s, 0:1], tabs[:, 0, bass.ds(j * SLOTS + SLOTS + s, 1)])
                        pool.tensor_copy(icol[:, s, 1:2], tabs[:, 1, bass.ds(j * SLOTS + s, 1)]).then_inc(ic[s], 1)
                        pool.wait_ge(ic[s], j + 2)
                        pool.sem_inc(pool_nop)
                        pool.wait_ge(xt_mm[s], j + 1)
                        pool.sem_inc(pool_nop)
                        gather_rows(s)
                        pool.wait_ge(ye_a[s], j + 2)
                        pool.sem_inc(pool_nop)
                        pool.wait_ge(ye_d[s], j + 2)
                        pool.sem_inc(pool_nop)
                        pool.indirect_dma_start(
                            Y_dram[:, :], bass.IndirectOffsetOnAxis(ap=icol[:, s, 1:2].bitcast(U32), axis=0),
                            ye[:, s, :], None,
                            bounds_check=T * TOPK - 1, oob_is_err=False).then_inc(y_out[s], 16)
                pool.wait_ge(par_in, 16 * 17)
                pool.wait_ge(fpar_in, 16 * 8)
                pool.wait_ge(kv_out, 32)
                for s in range(SLOTS):
                    pool.wait_ge(xg_in[s], turns * 16 + 16)
                    pool.sem_inc(pool_nop)
                    pool.wait_ge(y_out[s], turns * 16 + 16)
                    pool.sem_inc(pool_nop)
                pool.dma_reset(layer_range)
                last_of_layer(pool, "pool")

        @block.tensor
        def _(pe):
            mm = nc.tensor.matmul

            def group(k, n, lhsT_of, tile_s, tile_p, rhs=hT):
                mm(tile_s, lhsT_of(k), rhs[:, k, 0:LS], start=(k == 0), stop=(k == n - 1))
                return mm(tile_p, lhsT_of(k), rhs[:, k, LS:T], start=(k == 0), stop=(k == n - 1))

            def mean_square(ss_sem, ms_sem):
                pe.wait_ge(ss_sem, KC - 1)
                mm(ps[:, 0, :], mean_d, hT[:, 0, 0:LS], start=True, stop=True)
                mm(ps[:, 1, 0:LP], mean_d, hT[:, 0, LS:T], start=True, stop=True).then_inc(ms_sem, 1)

            pe.wait_ge(const_in, 16 * 10)
            pe.wait_ge(x_in, 32)
            for t in range(NT):
                if t >= 2:
                    pe.wait_ge(xT_in, 2 * (t - 1))
                for k in range(KC):
                    last = nc.tensor.transpose(ps[:, 4 * (t % 2) + k // 4, (k % 4) * P:(k % 4 + 1) * P],
                                               work[:, t * D + k:(t + 1) * D:KC], ident)
                last.then_inc(xT_mm, 1)
            pe.wait_ge(xT_in, 2 * NT)
            pe.wait_ge(c_ready, 1)
            with pe.Fori(0, DEPTH):
                mean_square(ss0, ms0)

                def ada(k):
                    wait_item(pe, k)
                    w = slot(k, 6 * D)
                    for b in range(4):
                        for g in range(3):
                            col = 2 * D * g + 512 * b
                            last = mm(ps[32 * g:32 * g + 2, 4 + b, :], c_act[:, k, :], w[:, col:col + 512],
                                      start=(k == 0), stop=(k == KC - 1))
                    last.then_inc(w_used, 1)

                def filter_rows(o):
                    for t in range(NT):
                        n = NT * o + t
                        if t >= 2:
                            pe.wait_ge(hy_raw, n - 1)
                        mm(ps[:, t % 2, :], h2[0:FFN + 1, t * P:(t + 1) * P], fw3[:, :, o, :],
                           start=True, stop=True).then_inc(hy_f, 1)

                def filter_spectrum(o):
                    pe.wait_ge(hy_eo, NT * (o + 1))
                    for q in range(2):
                        for f in range(4):
                            for t in range(4):
                                last = mm(ps[:, 2 * q + f // 2, (f % 2) * CH:(f % 2 + 1) * CH],
                                          dft[:, t, q * LS + f * P:q * LS + (f + 1) * P], evod[:, t, q, :],
                                          start=(t == 0), stop=(t == 3))
                        last.then_inc(hy_k, 1)
                    pe.wait_ge(hy_ke, 4 * o + 1)
                    for q in range(2):
                        last = mm(ps[:, 0, q * CH:(q + 1) * CH], fwd_p[:, 0, q * LP:(q + 1) * LP], evod[:, 4, q, :],
                                  start=True, stop=True)
                    last.then_inc(hy_k, 1)
                    pe.wait_ge(hy_sum, 7 * (o + 1))
                    for g in range(2):
                        for c in range(2):
                            last = mm(ps[:, 1, 2 * g + c:2 * g + c + 1], fsum[:, g, 0, c * P:(c + 1) * P], ones[:, 0:1],
                                      start=True, stop=True)
                    last.then_inc(hy_norm, 1)

                ada(0)
                ada(1)
                pe.wait_ge(rt0, 2)
                pe.wait_ge(fpar_in, 16 * 8)
                pe.wait_ge(const_in, 16 * 10)
                nc.tensor.transpose(ps[0:FFN, 2, 0:4], frow[:, :], ident[0:4, 0:4]).then_inc(row_mm, 1)
                mm(ps[0:FFN, 0, :], fw1[:, :], feat[:, 0:LS], start=True, stop=True)
                mm(ps[0:FFN, 1, 0:LP], fw1[:, :], feat[:, LS:T], start=True, stop=True).then_inc(hy_m1, 1)
                ada(2)
                pe.wait_ge(hy_s1, 1)
                mm(ps[0:FFN, 0, :], fw2[:, :], h1[0:FFN, 0:LS], start=True, stop=True)
                mm(ps[0:FFN, 1, 0:LP], fw2[:, :], h1[0:FFN, LS:T], start=True, stop=True).then_inc(hy_m2, 1)
                ada(3)
                pe.wait_ge(hy_s2, 1)
                filter_rows(0)
                ada(4)
                pe.wait_ge(f_in, 16)
                filter_spectrum(0)
                ada(5)
                pe.wait_ge(hy_ke, 4)
                pe.wait_ge(hy_rn, 1)
                filter_rows(1)
                ada(6)
                filter_spectrum(1)
                ada(7)
                pe.wait_ge(par_in, 16 * 17)
                pe.wait_ge(hy_ke, 8)
                pe.wait_ge(hy_rn, 2)
                for c in range(2):
                    nc.tensor.transpose(ps[:, 3, c * ROWS:(c + 1) * ROWS], prm[:, c * P:(c + 1) * P], ident[0:ROWS, 0:ROWS])
                mm(ps[:, 3, 104:144], ones[0:1, :], brow[:, :], start=True, stop=True)
                nc.tensor.transpose(ps[:, 3, 144:272], ckv[:, 0, :], ident).then_inc(par_mm, 1)
                pe.wait_ge(row_ev, 3)
                for g in range(3):
                    for a in range(2):
                        for q in range(KC):
                            o = (a * KC + q) * 2
                            last = nc.tensor.transpose(ps[:, g, o:o + 2],
                                                       adarow[32 * g:32 * g + 2, a * D + q:(a + 1) * D:KC],
                                                       ident[32 * g:32 * g + 2, 32 * g:32 * g + 2])
                last.then_inc(ada_t, 1)
                wait_item(pe, I_CONV)
                pe.wait_ge(par_ev, 3)
                w = slot(I_CONV, KC, 512)
                for c in range(2):
                    for m in (2 + c, c):
                        for k in range(KC):
                            if c == 0 and m == 2:
                                pe.wait_ge(h_s[0], k + 1)
                            last = group(k, KC, lambda k: w[:, k, m * P:(m + 1) * P], ps[:, m, :], ps[:, 4 + m, 0:LP])
                        last.then_inc(cv_mm, 1)
                wait_item(pe, I_FOUR)
                w = slot(I_FOUR, KC, CH)
                pe.wait_ge(cv_glu, 2)
                for t in range(NT):
                    for k in range(KC):
                        last = mm(ps[:, t, 0:CH], hT[:, k, t * P:(t + 1) * P], w[:, k, :], start=(k == 0), stop=(k == KC - 1))
                    last.then_inc(fo_x, 1)
                pe.wait_ge(cs_in, 16)
                pe.wait_ge(fo_xe, 5)
                for c in range(2):
                    for q in range(2):
                        for t in range(4):
                            last = mm(ps[:, (5 + 2 * c + q) % 8, :], fX[:, t, c * P:(c + 1) * P],
                                      dft[:, t, q * LS:(q + 1) * LS], start=(t == 0), stop=(t == 3))
                        last.then_inc(fo_a, 1)
                for c in range(2):
                    mm(ps[:, 1 + c, 0:CH], fX[:, 4, c * P:(c + 1) * P], mix_p[:, 0, :], start=True, stop=True) \
                        .then_inc(fo_a, 1)
                pe.wait_ge(fo_ae, 6)
                for m in range(2):
                    n = 0
                    for c in range(2):
                        for q in range(2):
                            lhs = mix_c[:, c, q * CH + m * P:q * CH + (m + 1) * P]
                            mm(ps[:, 3 + m, :], lhs, fA[:, c, q, 0:LS], start=(n == 0), stop=(n == 3))
                            last = mm(ps[:, 5 + m, 0:LP], lhs, fA[:, c, q, LS:T], start=(n == 0), stop=(n == 3))
                            n += 1
                    last.then_inc(fo_b, 1)
                wait_item(pe, I_ATT)
                w = slot(I_ATT, KC, 512)
                pe.wait_ge(yc_ok, 4)
                for m in range(2):
                    for k in range(KC):
                        last = group(k, KC, lambda k: w[:, k, m * P:(m + 1) * P],
                                     ps[:, m, :], ps[:, 2 + m, 0:LP])
                    last.then_inc(at_mm, 1)
                for k in range(KC):
                    last = group(k, KC, lambda k: w[:, k, 256:384], ps[:, 4, :], ps[:, 5, 0:LP])
                last.then_inc(at_mm, 1)
                for t in range(4):
                    for k in range(KC):
                        last = mm(ps[:, 6, t * P:(t + 1) * P], hT[:, k, t * P:(t + 1) * P], w[:, k, 384:512],
                                  start=(k == 0), stop=(k == KC - 1))
                last.then_inc(at_mm, 1)
                for k in range(KC):
                    last = mm(ps[:, 7, 0:256], hT[:, k, LS:T], w[:, k, 256:512], start=(k == 0), stop=(k == KC - 1))
                last.then_inc(at_mm, 1)
                pe.wait_ge(at_ev, 8)
                pe.wait_ge(cv_tap, 2 * TAPS)
                for c in range(2):
                    mm(ps[:, 0, :], mean_c, acc[:, c, 0:LS], start=(c == 0), stop=(c == 1))
                    last = mm(ps[:, 4, 0:CONV - LS], mean_c, acc[:, c, LS:CONV], start=(c == 0), stop=(c == 1))
                last.then_inc(ln_mm, 1)
                pe.wait_ge(ln_sq, 2)
                for c in range(2):
                    mm(ps[:, 1, :], mean_c, csq[:, c, 0:LS], start=(c == 0), stop=(c == 1))
                    last = mm(ps[:, 5, 0:CONV - LS], mean_c, csq[:, c, LS:CONV], start=(c == 0), stop=(c == 1))
                last.then_inc(ln_var, 1)
                pe.wait_ge(ln_rt, 2)
                for m in range(3):
                    src = qraw[:, m, 0:LS] if m < 2 else kraw[:, 0:LS]
                    mm(ps[:, m, :], rot, src, start=True, stop=True).then_inc(at_rot, 1)
                pe.wait_ge(at_rope, 3)

                def score(i, h):
                    if i > 0:
                        pe.wait_ge(at_exp, 4 * (i - 1) + h + 1)
                    p0, m = HD * (h // 2), h % 2
                    if i < 4:
                        lo, hi = max(i - 1, 0), min(i + 2, 4)
                        mm(ps[:, h, 0:P], qraw[p0:p0 + HD, m, i * P:(i + 1) * P], ckT[p0:p0 + HD, :], start=True, stop=True)
                        last = mm(ps[:, h, P:P + (hi - lo) * P], qrope[p0:p0 + HD, m, i * P:(i + 1) * P],
                                  krope[p0:p0 + HD, lo * P:hi * P], start=True, stop=True)
                    else:
                        last = mm(ps[:, h, 0:P], qraw[p0:p0 + HD, m, LS:T], kraw[p0:p0 + HD, LS:T], start=True, stop=True)
                    last.then_inc(at_s, 1)

                for h in range(4):
                    score(0, h)
                for i in range(NT):
                    lo, hi = max(i - 1, 0), min(i + 2, 4)
                    nk = 1 + hi - lo if i < 4 else 1
                    if i > 0:
                        pe.wait_ge(yd_ok, i)
                    for h in range(4):
                        pe.wait_ge(at_exp, 4 * i + h + 1)
                        for t in range(nk):
                            last = nc.tensor.transpose(ps[:, 4 + h, t * P:(t + 1) * P], prob[:, h, t * P:(t + 1) * P], ident)
                        last.then_inc(at_t, 1)
                        if i + 1 < NT:
                            score(i + 1, h)
                    for h in range(4):
                        kv = h // 2
                        pe.wait_ge(at_te, 4 * i + h + 1)
                        for t in range(nk):
                            if i == 4:
                                v = vtok[:, 4, kv * HD:(kv + 1) * HD]
                            elif t == 0:
                                v = ckv[:, 1, kv * HD:(kv + 1) * HD]
                            else:
                                v = vtok[:, lo + t - 1, kv * HD:(kv + 1) * HD]
                            last = mm(ps[:, 4, h * HD:(h + 1) * HD], probT[:, h, t * P:(t + 1) * P], v,
                                      start=(t == 0), stop=(t == nk - 1))
                    last.then_inc(at_pv, 1)
                    pe.wait_ge(at_o, i + 1)
                    for q in range(2):
                        last = nc.tensor.transpose(ps[:, 5, q * P:(q + 1) * P], otok[:, q * P:(q + 1) * P], ident)
                    last.then_inc(at_ot, 1)
                pe.wait_ge(yd_ok, NT)
                wait_item(pe, I_HY)
                w = slot(I_HY, KC, 768)
                for m in range(6):
                    if m >= 4:
                        pe.wait_ge(hy_uc, m - 3)
                    for k in range(KC):
                        last = group(k, KC, lambda k: w[:, k, m * P:(m + 1) * P], ps[:, m % 4, :], ps[:, 4 + m % 4, 0:LP])
                    last.then_inc(hy_u, 1)
                pe.wait_ge(hy_uc, 6)
                pe.wait_ge(f_in, 32)
                for o in range(2):
                    if o:
                        pe.wait_ge(hy_zn, 2)
                    for t in range(NT):
                        for c in range(2):
                            last = nc.tensor.transpose(ps[:, t // 2, (t % 2) * CH + c * P:(t % 2) * CH + (c + 1) * P],
                                                       u[:, c, t * P:(t + 1) * P], ident)
                    last.then_inc(hy_zt, 1)
                    pe.wait_ge(hy_z, o + 1)
                    for q in range(2):
                        for f in range(4):
                            for t in range(4):
                                last = mm(ps[:, 2 * q + f // 2, (f % 2) * CH:(f % 2 + 1) * CH],
                                          dft[:, t, q * LS + f * P:q * LS + (f + 1) * P], zs[:, t, :],
                                          start=(t == 0), stop=(t == 3))
                    for q in range(2):
                        last = mm(ps[:, 4, q * CH:(q + 1) * CH], fwd_p[:, 0, q * LP:(q + 1) * LP], zs[:, 4, :],
                                  start=True, stop=True)
                    last.then_inc(hy_fz, 1)
                    pe.wait_ge(hy_y, o + 1)
                    for c in range(2):
                        for q in range(2):
                            for f in range(4):
                                mm(ps[:, 6 + c, :], yspec[:, q, f, c * P:(c + 1) * P], inv_s[:, 4 * q + f, :],
                                   start=(q + f == 0), stop=(q * 4 + f == 7))
                        for q in range(2):
                            last = mm(ps[:, 4 + c, 0:P], yspec[:, q, 4, c * P:(c + 1) * P], inv_p[:, q, :],
                                      start=(q == 0), stop=(q == 1))
                    last.then_inc(hy_inv, 1)
                wait_item(pe, I_OUT)
                wait_item(pe, I_OUT + 1)
                pe.wait_ge(hy_zn, 4)
                pe.wait_ge(ya_ok, 4)
                w2 = [slot(I_OUT + i, 4, D) for i in range(2)]
                for m in range(KC):
                    if m >= 4:
                        pe.wait_ge(x_mid, 2 * (m - 3))
                    for k in range(KC):
                        last = group(k, KC, lambda k: w2[k // 4][:, k % 4, m:D:KC], ps[:, m % 4, :], ps[:, 4 + m % 4, 0:LP], yT)
                    last.then_inc(wo_mm, 1)
                pe.wait_ge(x_mid, 16)
                mean_square(ss1, ms1)
                for t in range(NT):
                    for k in range(KC):
                        if t == 0:
                            pe.wait_ge(h_s[1], k + 1)
                        last = mm(ps[:, 2, t * 36:(t + 1) * 36], hT[:, k, t * P:(t + 1) * P], wr[:, k, :],
                                  start=(k == 0), stop=(k == KC - 1))
                last.then_inc(ro_mm, 1)
                for t in range(NT):
                    if t >= 2:
                        pe.wait_ge(hs_ev, 2 * (t - 1))
                    for k in range(KC):
                        last = nc.tensor.transpose(ps[:, 4 + 2 * (t % 2) + k // 4, (k % 4) * P:(k % 4 + 1) * P],
                                                   hT[:, k, t * P:(t + 1) * P], ident)
                    last.then_inc(hs_mm, 1)
                pe.wait_ge(ro_oh, 1)
                for t in range(NT):
                    for q in range(t):
                        mm(ps[:, 3, t * NE:(t + 1) * NE], ones, both[:, q, :], start=(q == 0), stop=False)
                    mm(ps[:, 3, t * NE:(t + 1) * NE], tri, both[:, t, :], start=(t == 0), stop=True)
                for t in range(NT):
                    last = mm(ps[:, 3, NT * NE:(NT + 1) * NE], ones, both[:, t, :], start=(t == 0), stop=(t == NT - 1))
                last.then_inc(ro_rank, 1)
                pe.wait_ge(ro_1h, 1)
                n = 0
                for t in range(NT):
                    for q in range(2):
                        last = mm(ps[:, 2, 256:256 + NBLK + SLOTS], ohs[:, t, q, :], ohb[:, t, q, :], start=(n == 0), stop=(n == 9))
                        n += 1
                last.then_inc(ro_tm, 1)
                def rows_in(s, k0, k1):
                    for k in range(k0, k1):
                        last = nc.tensor.transpose(ps[:, k // 4, (k % 4) * P:(k % 4 + 1) * P],
                                                   xg[:, s, k * P:(k + 1) * P], ident)
                    return last

                for s in range(SLOTS):
                    pe.sem_inc(y_mm[s])
                pe.wait_ge(ro_tab, 1)
                turns = pe.value_load(nturn[0:1, 0:1], min_val=1, max_val=NBLK // 2)
                pe.wait_ge(xg_in[0], 16)
                rows_in(0, 0, KC).then_inc(xt_mm[0], 1)
                with pe.Fori(0, turns) as j:
                    for s in range(SLOTS):
                        w = slot(s, 3, KC, FE)
                        wd = slot(s, 3, 2, D)
                        pe.wait_ge(xe_ok[s], j * 2 + 2)
                        pe.wait_ge(wg_full[s], j * 32 + 32)
                        for k in range(KC):
                            last = mm(ps[:, 2, 0:FE], xe[:, s, k, :], w[:, 0, k, :], start=(k == 0), stop=(k == KC - 1))
                        last.then_inc(g_mm[s], 1)
                        for k in range(KC):
                            last = mm(ps[:, 3, 0:FE], xe[:, s, k, :], w[:, 1, k, :], start=(k == 0), stop=(k == KC - 1))
                        last.then_inc(u_mm[s], 1)
                        if s == 0:
                            pe.wait_ge(xg_in[1], j * 16 + 16)
                        else:
                            pe.wait_ge(xg_in[0], j * 16 + 32)
                        rows_in(1 - s, 0, 4)
                        pe.wait_ge(hh_ok[s], j + 1)
                        for k in range(2):
                            last = nc.tensor.transpose(ps[:, 4, k * P:(k + 1) * P], hh[:, s, k:FE:2], ident)
                        last.then_inc(ht_mm[s], 1)
                        rows_in(1 - s, 4, KC).then_inc(xt_mm[1 - s], 1)
                        pe.wait_ge(he_ok[s], j + 1)
                        pe.wait_ge(wd_full[s], j * 16 + 16)
                        other = j + 1 if s == 0 else j + 2
                        pe.wait_ge(ye_a[1 - s], other)
                        pe.wait_ge(ye_d[1 - s], other)
                        for n in range(2):
                            for k in range(2):
                                last = mm(ps[:, 6 + n, :], he[:, s, k, :], wd[:, 2, k, n * 512:(n + 1) * 512],
                                          start=(k == 0), stop=(k == 1))
                            last.then_inc(y_mm[s], 1)
                pe.wait_ge(ye_a[1], turns + 1)
                pe.wait_ge(ye_d[1], turns + 1)
                for t in range(NT):
                    pe.wait_ge(yc_sum, t + 1)
                    if t >= 2:
                        pe.wait_ge(x_new, KC * (t - 1))
                    for k in range(KC):
                        last = nc.tensor.transpose(ps[:, 2 * (t % 2) + k // 4, (k % 4) * P:(k % 4 + 1) * P],
                                                   ysum[:, t % 2, k:D:KC], ident)
                    last.then_inc(yc_mm, 1)
                last_of_layer(pe, "pe")
            mean_square(ss0, ms0)
            for t in range(NT):
                if t >= 2:
                    pe.wait_ge(hs_ev, 2 * (t - 1))
                for k in range(KC):
                    if t == 0:
                        pe.wait_ge(h0, k + 1)
                    last = nc.tensor.transpose(ps[:, 2 + 2 * (t % 2) + k // 4, (k % 4) * P:(k % 4 + 1) * P],
                                               hT[:, k, t * P:(t + 1) * P], ident)
                last.then_inc(hs_mm, 1)

        @block.scalar
        def _(act):
            A = nc.scalar.activation

            def squares(ready, step_, base, sq_sem):
                for k in range(KC):
                    act.wait_ge(ready, base + step_ * k)
                    A(hT[:, k, :], xT[:, k, :], ACT.Square).then_inc(sq_sem, 1)

            def root(ms_sem, rt_sem):
                act.wait_ge(ms_sem, 1)
                A(rms[:, 0:LS], ps[:, 0, :], ACT.Sqrt, bias=epsc[:, :]).then_inc(rt_sem, 1)
                A(rms[:, LS:T], ps[:, 1, 0:LP], ACT.Sqrt, bias=epsc[:, :]).then_inc(rt_sem, 1)

            def modulate(n, xn_sem, h_sem):
                for k in range(KC):
                    act.wait_ge(xn_sem, k + 1)
                    for g, (a, b) in enumerate(GRP):
                        last = A(hT[:, k, a:b], hT[:, k, a:b], ACT.Identity, scale=gain[:, n, k, g:g + 1],
                                 bias=mods[:, 3 * n, k, g:g + 1])
                    last.then_inc(h_sem, 1)

            act.wait_ge(cond_in, 16 * 3)
            for g in range(2):
                last = A(c_act[:, :, g], c_raw[:, g, :], ACT.Silu)
            last.then_inc(c_ready, 1)
            for t in range(NT):
                act.wait_ge(xT_mm, t + 1)
                for q in range(2):
                    A(xT[:, 4 * q:4 * q + 4, t * P:(t + 1) * P],
                      ps[:, 4 * (t % 2) + q, :].rearrange("p (k t) -> p k t", k=4), ACT.Copy).then_inc(xT_in, 1)
            act.wait_ge(set_up, 1)
            act.wait_ge(xT_in, 2 * NT)
            with act.Fori(0, DEPTH):
                squares(xT_in, 0, 2 * NT, sq0)
                root(ms0, rt0)
                act.wait_ge(hy_a1, 1)
                A(h1[0:FFN, :], fa_[0:FFN, :], ACT.Sin).then_inc(hy_s1, 1)
                act.wait_ge(hy_a2, 1)
                A(h2[0:FFN, :], fa_[0:FFN, :], ACT.Sin).then_inc(hy_s2, 1)
                for o in range(2):
                    for t in range(NT):
                        n = NT * o + t
                        act.wait_ge(hy_eo, n + 1)
                        if n >= 2:
                            act.wait_ge(hy_sum, 7 * ((n - 2) // NT) + (n - 2) % NT + 1)
                        A(fabs[:, t % 2, :, :], ftime[:, t % 2, :, :], ACT.Abs).then_inc(hy_abs, 1)
                    if o:
                        act.wait_ge(k_out, 16)
                    for q in range(2):
                        act.wait_ge(hy_k, 3 * o + q + 1)
                        A(knew[:, q, 0:4, :], ps[:, 2 * q:2 * q + 2, :].rearrange("p b (f c) -> p (b f) c", f=2), ACT.Copy) \
                            .then_inc(hy_ke, 1)
                    act.wait_ge(hy_k, 3 * o + 3)
                    for q in range(2):
                        A(knew[:, q, 4, :], ps[:, 0, q * CH:(q + 1) * CH], ACT.Copy).then_inc(hy_ke, 1)
                    act.wait_ge(hy_ke, 4 * (o + 1))
                    act.dma_start(K_dram[o], knew.rearrange("p q t c -> p (q t c)")).then_inc(k_out, 16)
                act.wait_ge(w_used, KC)
                A(adarow[0:2, :], ps[0:2, 4:8, :].rearrange("p b c -> p (b c)"), ACT.Copy).then_inc(row_ev, 1)
                act.wait_ge(mods_ok, 5)
                modulate(0, xn_s[0], h_s[0])
                for c in range(2):
                    act.wait_ge(cv_mm, 2 * c + 1)
                    for (a, b), bank in ((GRP[0], 2 + c), (GRP[1], 6 + c)):
                        last = A(sig[:, c, a:b], ps[:, bank, 0:b - a], ACT.Sigmoid)
                    last.then_inc(cv_sig, 1)
                for t in range(NT):
                    act.wait_ge(fo_x, t + 1)
                    A(fX[:, t, :], ps[:, t, 0:CH], ACT.Copy).then_inc(fo_xe, 1)
                for c in range(2):
                    for q in range(2):
                        act.wait_ge(fo_a, 2 * c + q + 1)
                        A(fA[:, c, q, 0:LS], ps[:, (5 + 2 * c + q) % 8, :], ACT.Copy).then_inc(fo_ae, 1)
                for c in range(2):
                    act.wait_ge(fo_a, 5 + c)
                    A(fA[:, c, :, LS:T], ps[:, 1 + c, 0:CH].rearrange("p (q t) -> p q t", q=2), ACT.Copy) \
                        .then_inc(fo_ae, 1)
                act.wait_ge(k_out, 32)
                for m in range(2):
                    act.wait_ge(fo_b, m + 1)
                    A(yT[:, 4 + m, 0:LS], ps[:, 3 + m, :], ACT.Copy).then_inc(yc_ok, 1)
                    A(yT[:, 4 + m, LS:T], ps[:, 5 + m, 0:LP], ACT.Copy).then_inc(yc_ok, 1)
                for m in range(2):
                    act.wait_ge(at_mm, m + 1)
                    for (a, b), bank in ((GRP[0], m), (GRP[1], 2 + m)):
                        for h in range(2):
                            last = A(qraw[m * HD:(m + 1) * HD, h, a:b], ps[h * HD:(h + 1) * HD, bank, 0:b - a], ACT.Copy)
                        last.then_inc(at_ev, 1)
                act.wait_ge(at_mm, 3)
                A(kraw[:, 0:LS], ps[:, 4, :], ACT.Copy).then_inc(at_ev, 1)
                A(kraw[:, LS:T], ps[:, 5, 0:LP], ACT.Copy).then_inc(at_ev, 1)
                act.wait_ge(at_mm, 4)
                A(vtok[:, 0:4, :], ps[:, 6, :].rearrange("p (t c) -> p t c", t=4), ACT.Copy).then_inc(at_ev, 1)
                act.wait_ge(at_mm, 5)
                A(vtok[:, 4, :], ps[:, 7, P:2 * P], ACT.Copy)
                A(kvo[:, :, :], ps[:, 7, 0:256].rearrange("p (q c) -> p q c", q=2), ACT.Copy).then_inc(at_ev, 1)
                act.wait_ge(ln_ctr, 2)
                for c in range(2):
                    A(csq[:, c, :], acc[:, c, :], ACT.Square).then_inc(ln_sq, 1)
                act.wait_ge(ln_var, 1)
                A(crs[:, 0:LS], ps[:, 1, :], ACT.Sqrt, bias=epsc[:, :]).then_inc(ln_rt, 1)
                A(crs[:, LS:CONV], ps[:, 5, 0:CONV - LS], ACT.Sqrt, bias=epsc[:, :]).then_inc(ln_rt, 1)
                for c in range(2):
                    act.wait_ge(ln_out, c + 1)
                    for (a, b), o in ((GRP[0], 0), (GRP[1], PAD)):
                        A(yT[:, c, a:b], acc[:, c, a + o:b + o], ACT.Silu, scale=prmT[:, c, R_LNG:R_LNG + 1],
                          bias=prmT[:, c, R_LNB:R_LNB + 1]).then_inc(ya_ok, 1)
                for i in range(NT):
                    nk = (3, 4, 4, 3, 1)[i]
                    act.wait_ge(at_max, i + 1)
                    A(ast[:, i % 2, 3, :], ast[:, i % 2, 2, :], ACT.Exp)
                    for h in range(4):
                        if i > 0:
                            act.wait_ge(at_t, 4 * (i - 1) + h + 1)
                        A(prob[:, h, 0:nk * P], ps[:, h, 0:nk * P], ACT.Exp, bias=ast[:, i % 2, 1, h:h + 1], scale=HD ** -0.5,
                          accum_out=ast[:, i % 2, 4, h:h + 1]).then_inc(at_exp, 1)
                    for h in range(4):
                        act.wait_ge(at_t, 4 * i + h + 1)
                        if i > 0 and h == 0:
                            act.wait_ge(at_pv, i)
                        A(probT[:, h, 0:nk * P], ps[:, 4 + h, 0:nk * P], ACT.Copy).then_inc(at_te, 1)
                    act.wait_ge(at_ot, i + 1)
                    A(yT[:, 6:8, i * P:(i + 1) * P], ps[:, 5, 0:2 * P].rearrange("p (q t) -> p q t", q=2), ACT.Copy) \
                        .then_inc(yd_ok, 1)
                for m in range(6):
                    act.wait_ge(hy_u, m + 1)
                    r = R_SW + 3 + m // 2
                    for (a, b), bank in ((GRP[0], m % 4), (GRP[1], 4 + m % 4)):
                        last = A(u[:, m, a:b], ps[:, bank, 0:b - a], ACT.Identity, scale=prmT[:, m % 2, r:r + 1],
                                 bias=prmT[:, m % 2, R_SB + m // 2:R_SB + m // 2 + 1])
                    last.then_inc(hy_u1, 1)
                for o in range(2):
                    act.wait_ge(hy_zt, o + 1)
                    A(zs[:, 0:4, :], ps[:, 0:2, :].rearrange("p b (f c) -> p (b f) c", f=2), ACT.Copy)
                    A(zs[:, 4, :], ps[:, 2, 0:CH], ACT.Copy).then_inc(hy_z, 1)
                squares(x_mid, 2, 2, sq1)
                root(ms1, rt1)
                modulate(1, xn_s[1], h_s[1])
                act.wait_ge(ro_sub, 1)
                A(gexp[:, :, :], gt[:, :, :], ACT.Exp).then_inc(ro_exp, 1)
                for t in range(NT):
                    act.wait_ge(hs_mm, t + 1)
                    if t >= 2:
                        act.wait_ge(hs_st[t % 2], 16 * (t // 2))
                    for q in range(2):
                        A(htok[:, t % 2, 512 * q:512 * q + 512], ps[:, 4 + 2 * (t % 2) + q, :], ACT.Copy).then_inc(hs_ev, 1)
                act.wait_ge(ro_sub2, 1)
                A(emx[:, :], ediff[:, :], ACT.Exp).then_inc(ro_exp2, 1)
                for s in range(SLOTS):
                    act.sem_inc(ye_a[s])
                act.wait_ge(ro_tab, 1)
                turns = act.value_load(nturn[0:1, 0:1], min_val=1, max_val=NBLK // 2)
                for q in range(2):
                    act.wait_ge(hs_st[q], 16 * ((NT + 1 - q) // 2))

                def rows_out(s):
                    for q in range(2):
                        A(xe[:, s, 4 * q:4 * q + 4, :].rearrange("p k t -> p (k t)"), ps[:, q, :], ACT.Copy) \
                            .then_inc(xe_ok[s], 1)

                act.wait_ge(xt_mm[0], 1)
                rows_out(0)
                with act.Fori(0, turns) as j:
                    for s in range(SLOTS):
                        act.wait_ge(g_mm[s], j + 1)
                        A(sg[:, s, :], ps[:, 2, 0:FE], ACT.Silu).then_inc(sg_ok[s], 1)
                        act.wait_ge(xt_mm[1 - s], j + 1 if s == 0 else j + 2)
                        rows_out(1 - s)
                        act.wait_ge(y_mm[s], j * 2 + 2)
                        act.wait_ge(y_out[s], j * 16 + 16)
                        A(ye[:, s, 0:512], ps[:, 6, :], ACT.Copy).then_inc(ye_a[s], 1)
                last_of_layer(act, "act")
            squares(xT_in, 0, 2 * NT, sq0)
            root(ms0, rt0)
            for k in range(KC):
                act.wait_ge(xn0, k + 1)
                A(hT[:, k, :], hT[:, k, :], ACT.Copy, scale=nf[:, k:k + 1]).then_inc(h0, 1)
            for t in range(NT):
                act.wait_ge(hs_mm, t + 1)
                for q in range(2):
                    A(work[:, t * D:(t + 1) * D].rearrange("p (c k) -> p k c", k=KC)[:, 4 * q:4 * q + 4, :],
                      ps[:, 2 + 2 * (t % 2) + q, :].rearrange("p (k c) -> p k c", k=4), ACT.Copy).then_inc(hs_ev, 1)

        @block.vector
        def _(dve):
            V = nc.vector
            chain = [0]

            def step(ins):
                chain[0] += 1
                ins.then_inc(dchain, 1)
                dve.wait_ge(dchain, chain[0])

            def bc(ap, n):
                return ap.rearrange("p (a b) -> p a b", b=1).to_broadcast([P, ap.shape[1], n])

            def row(ap, n):
                return ap.rearrange("p (b a) -> p b a", b=1).to_broadcast([P, n, ap.shape[1]])

            def add_square(k, sq_sem, ss_sem):
                dve.wait_ge(sq_sem, k + 1)
                if k >= 2:
                    dve.wait_ge(ss_sem, k - 1)
                V.tensor_tensor(hT[:, 0, :], hT[:, 0, :], hT[:, k, :], ALU.add).then_inc(ss_sem, 1)

            def normalise(rt_sem, rc_sem, xn_sem):
                dve.wait_ge(rt_sem, 2)
                V.reciprocal(rinv[:, :], rms[:, :]).then_inc(rc_sem, 1)
                dve.wait_ge(rc_sem, 1)
                for k in range(KC):
                    V.tensor_tensor(hT[:, k, :], xT[:, k, :], rinv[:, :], ALU.mult).then_inc(xn_sem, 1)

            def residual(t):
                dve.wait_ge(yc_mm, t + 1)
                for k in range(KC):
                    x = xT[:, k, t * P:(t + 1) * P]
                    g = 0 if t < 4 else 1
                    V.scalar_tensor_tensor(out=x, in0=ps[:, 2 * (t % 2) + k // 4, (k % 4) * P:(k % 4 + 1) * P],
                                           scalar=mods[:, 5, k, g:g + 1], in1=x, op0=ALU.mult, op1=ALU.add) \
                        .then_inc(x_new, 1)

            with dve.Fori(0, DEPTH):
                chain[0] = 0
                for k in range(1, KC):
                    add_square(k, sq0, ss0)
                normalise(rt0, rc0, xn0)

                def sine_argument(done):
                    a, k = fa_[0:FFN, :], fk_[0:FFN, :]
                    step(V.tensor_scalar(k, a, 1 / (2 * np.pi), MAGIC, ALU.mult, ALU.add))
                    step(V.tensor_scalar(k, k, -MAGIC, None, ALU.add))
                    step(V.scalar_tensor_tensor(out=a, in0=k, scalar=-TWO_PI_HI, in1=a, op0=ALU.mult, op1=ALU.add))
                    step(V.scalar_tensor_tensor(out=a, in0=k, scalar=-float(TWO_PI_LO), in1=a, op0=ALU.mult, op1=ALU.add))
                    V.tensor_scalar(a, a, 3.1415925, -3.1415925, ALU.min, ALU.max).then_inc(done, 1)

                dve.wait_ge(row_mm, 1)
                V.memset(h2[FFN:FFN + 1, :], 1.0)
                step(V.tensor_copy(frowT[:, :], ps[0:FFN, 2, 0:4]))
                for n, (mm_sem, done, fb) in enumerate(((hy_m1, hy_a1, 0), (hy_m2, hy_a2, 2))):
                    dve.wait_ge(mm_sem, 1)
                    for (a, b), bank in ((GRP[0], 0), (GRP[1], 1)):
                        last = V.tensor_scalar(fa_[0:FFN, a:b], ps[0:FFN, bank, 0:b - a], frowT[:, fb:fb + 1],
                                               frowT[:, fb + 1:fb + 2], ALU.add, ALU.mult)
                    step(last)
                    sine_argument(done)
                for o in range(2):
                    for t in range(NT):
                        n = NT * o + t
                        dve.wait_ge(hy_f, n + 1)
                        if n == 0:
                            dve.wait_ge(hy_s2, 1)
                        if n >= 2:
                            dve.wait_ge(hy_abs, n - 1)
                        f = ftime[:, t % 2, :, :]
                        V.tensor_tensor(f, ps[:, t % 2, :].rearrange("p (q c) -> p q c", q=2), row(win[:, t, :], 2),
                                        ALU.mult).then_inc(hy_raw, 1)
                        dve.wait_ge(hy_raw, n + 1)
                        V.tensor_tensor(evod[:, t, 1, :], f[:, 0, :], f[:, 1, :], ALU.subtract)
                        if t in (0, 4):
                            step(V.tensor_tensor(evod[:, t, 0, :], f[:, 0, :], f[:, 1, :], ALU.add))
                            step(V.tensor_copy(f[0:1, 0, :], evod[0:1, t, 0, :]))
                            V.memset(f[0:1, 1, :], 0.0).then_inc(hy_eo, 1)
                        else:
                            V.tensor_tensor(evod[:, t, 0, :], f[:, 0, :], f[:, 1, :], ALU.add).then_inc(hy_eo, 1)
                    dve.wait_ge(hy_norm, o + 1)
                    step(V.tensor_scalar(rnorm[:, o, :], ps[:, 1, 0:4], EPS, None, ALU.add))
                    V.reciprocal(rnorm[:, o, :], rnorm[:, o, :]).then_inc(hy_rn, 1)
                dve.wait_ge(w_used, KC)
                for g in range(1, 3):
                    V.tensor_copy(adarow[32 * g:32 * g + 2, :], ps[32 * g:32 * g + 2, 4:8, :].rearrange("p b c -> p (b c)")) \
                        .then_inc(row_ev, 1)
                dve.wait_ge(par_mm, 1)
                V.tensor_copy(prmT[:, :, :], ps[:, 3, 0:2 * ROWS].rearrange("p (c r) -> p c r", c=2)).then_inc(par_ev, 1)
                V.tensor_copy(bcast[:, :], ps[:, 3, 104:144]).then_inc(par_ev, 1)
                V.tensor_copy(ckT[:, :], ps[:, 3, 144:272]).then_inc(par_ev, 1)
                dve.wait_ge(ada_t, 1)
                for g in range(3):
                    V.tensor_tensor(mods[:, 2 * g:2 * g + 2, :, :].rearrange("p a k g -> p (a k) g"),
                                    ps[:, g, 0:32].rearrange("p (a g) -> p a g", g=2),
                                    bc(ada_b[:, 2 * g:2 * g + 2, :].rearrange("p a k -> p (a k)"), 2), ALU.add).then_inc(mods_ok, 1)
                dve.wait_ge(mods_ok, 3)
                for n in range(2):
                    V.scalar_tensor_tensor(out=gain[:, n, :, :], in0=mods[:, 3 * n + 1, :, :], scalar=1.0,
                                           in1=bc(norms[:, n, :], 2), op0=ALU.add, op1=ALU.mult).then_inc(mods_ok, 1)
                dve.wait_ge(xn0, KC)
                for c in range(2):
                    V.memset(glu[:, c, 0:PAD], 0.0)
                    V.memset(glu[:, c, PAD + LS:2 * PAD + LS], 0.0)
                    last = V.memset(glu[:, c, GW - PAD:GW], 0.0)
                step(last)
                for c in range(2):
                    dve.wait_ge(cv_sig, c + 1)
                    dve.wait_ge(cv_mm, 2 * c + 2)
                    V.tensor_tensor(glu[:, c, PAD:PAD + LS], ps[:, c, :], sig[:, c, 0:LS], ALU.mult)
                    V.tensor_tensor(glu[:, c, 2 * PAD + LS:2 * PAD + T], ps[:, 4 + c, 0:LP], sig[:, c, LS:T],
                                    ALU.mult).then_inc(cv_glu, 1)
                dve.wait_ge(cv_glu, 2)
                for j in range(TAPS):
                    for c in range(2):
                        if j == 0:
                            V.tensor_scalar(acc[:, c, :], glu[:, c, j:j + CONV], prmT[:, c, j:j + 1],
                                            prmT[:, c, R_DWB:R_DWB + 1], ALU.mult, ALU.add).then_inc(cv_tap, 1)
                        else:
                            dve.wait_ge(cv_tap, 2 * j + c - 1)
                            V.scalar_tensor_tensor(out=acc[:, c, :], in0=glu[:, c, j:j + CONV], scalar=prmT[:, c, j:j + 1],
                                                   in1=acc[:, c, :], op0=ALU.mult, op1=ALU.add).then_inc(cv_tap, 1)
                dve.wait_ge(ln_mm, 1)
                for c in range(2):
                    V.tensor_tensor(acc[:, c, 0:LS], acc[:, c, 0:LS], ps[:, 0, :], ALU.subtract)
                    V.tensor_tensor(acc[:, c, LS:CONV], acc[:, c, LS:CONV], ps[:, 4, 0:CONV - LS],
                                    ALU.subtract).then_inc(ln_ctr, 1)
                dve.wait_ge(ln_rt, 2)
                V.reciprocal(crn[:, :], crs[:, :]).then_inc(ln_rn, 1)
                dve.wait_ge(ln_rn, 1)
                for c in range(2):
                    V.tensor_tensor(acc[:, c, :], acc[:, c, :], crn[:, :], ALU.mult).then_inc(ln_out, 1)
                dve.wait_ge(ya_ok, 4)
                for m in range(3):
                    src, dst = (qraw[:, m, 0:LS], qrope[:, m, :]) if m < 2 else (kraw[:, 0:LS], krope[:, :])
                    dve.wait_ge(at_rot, m + 1)
                    V.tensor_tensor(rtmp[:, m, :], ps[:, m, :], rope[:, 1, :], ALU.mult)
                    step(V.tensor_tensor(dst, src, rope[:, 0, :], ALU.mult))
                    V.tensor_tensor(dst, dst, rtmp[:, m, :], ALU.add).then_inc(at_rope, 1)
                sink = bcast[:, 0:4]

                def divide(i):
                    dve.wait_ge(at_exp, 4 * i + 4)
                    step(V.tensor_tensor(ast[:, i % 2, 6, :], ast[:, i % 2, 3, :], ast[:, i % 2, 4, :], ALU.add))
                    step(V.reciprocal(ast[:, i % 2, 7, :], ast[:, i % 2, 6, :]))
                    dve.wait_ge(at_pv, i + 1)
                    V.tensor_tensor(otok.rearrange("p (h c) -> p h c", h=4), ps[:, 4, 0:256].rearrange("p (h c) -> p h c", h=4),
                                    bc(ast[:, i % 2, 7, :], HD), ALU.mult).then_inc(at_o, 1)

                for i in range(NT):
                    nk = (3, 4, 4, 3, 1)[i]
                    dve.wait_ge(at_s, 4 * (i + 1))
                    if 1 <= i < 4:
                        step(V.tensor_tensor(ps[:, 0:4, P:2 * P], ps[:, 0:4, P:2 * P], row(mask_l, 4), ALU.add))
                    if i < 3:
                        step(V.tensor_tensor(ps[:, 0:4, (nk - 1) * P:nk * P], ps[:, 0:4, (nk - 1) * P:nk * P],
                                             row(mask_r, 4), ALU.add))
                    step(V.tensor_reduce(ast[:, i % 2, 0, :], ps[:, 0:4, 0:nk * P], AX.X, ALU.max))
                    step(V.scalar_tensor_tensor(out=ast[:, i % 2, 5, :], in0=ast[:, i % 2, 0, :], scalar=HD ** -0.5, in1=sink,
                                                op0=ALU.mult, op1=ALU.max))
                    V.tensor_scalar(ast[:, i % 2, 1, :], ast[:, i % 2, 5, :], -1.0, None, ALU.mult)
                    V.tensor_tensor(ast[:, i % 2, 2, :], sink, ast[:, i % 2, 5, :], ALU.subtract).then_inc(at_max, 1)
                    if i > 0:
                        divide(i - 1)
                divide(NT - 1)
                dve.wait_ge(yd_ok, NT)

                def short(m):
                    dve.wait_ge(hy_u1, m + 1)
                    for tap, (oa, ob, ia, ib) in ((R_SW, (1, 0, 0, -1)), (R_SW + 6, (0, -1, 1, 0))):
                        w_ = prmT[:, m % 2, tap + m // 2:tap + m // 2 + 1]
                        for (a, b), bank in ((GRP[0], m % 4), (GRP[1], 4 + m % 4)):
                            last = V.scalar_tensor_tensor(out=u[:, m, a + oa:b + ob], in0=ps[:, bank, ia:b - a + ib], scalar=w_,
                                                          in1=u[:, m, a + oa:b + ob], op0=ALU.mult, op1=ALU.add)
                        if tap == R_SW:
                            step(last)
                    last.then_inc(hy_uc, 1)

                for m in range(6):
                    short(m)
                for o in range(2):
                    dve.wait_ge(hy_zt, o + 1)
                    for c in range(2):
                        V.tensor_scalar(u[:, c, :], u[:, c, :], prmT[:, c, R_HD + o:R_HD + o + 1], None, ALU.mult) \
                            .then_inc(hy_dz, 1)
                    dve.wait_ge(hy_fz, o + 1)
                    dve.wait_ge(k_in, 16 * (o + 1))
                    for (a, b), zr, zi in (((0, 4), ps[:, 0:2, :], ps[:, 2:4, :]),
                                           ((4, 5), ps[:, 4:5, 0:CH], ps[:, 4:5, CH:2 * CH])):
                        nn = (b - a) * CH
                        if a == 0:
                            flat = lambda v: v.rearrange("p (b f) c -> p b (f c)", f=2)
                            tm = ctmp[:, 0:nn].rearrange("p (b c) -> p b c", b=2)
                        else:
                            flat = lambda v: v
                            tm = ctmp[:, 4 * CH:5 * CH].rearrange("p (b c) -> p b c", b=1)
                        kr, ki = flat(kspec[:, 0, a:b, :]), flat(kspec[:, 1, a:b, :])
                        yr, yi = flat(yspec[:, 0, a:b, :]), flat(yspec[:, 1, a:b, :])
                        V.tensor_tensor(yr, zr, kr, ALU.mult)
                        step(V.tensor_tensor(tm, zi, ki, ALU.mult))
                        step(V.tensor_tensor(yr, yr, tm, ALU.subtract))
                        V.tensor_tensor(yi, zr, ki, ALU.mult)
                        step(V.tensor_tensor(tm, zi, kr, ALU.mult))
                        last = V.tensor_tensor(yi, yi, tm, ALU.add)
                        if a == 0:
                            step(last)
                    last.then_inc(hy_y, 1)
                    dve.wait_ge(hy_inv, o + 1)
                    dve.wait_ge(hy_dz, 2 * (o + 1))
                    dve.wait_ge(hy_rn, o + 1)
                    for c in range(2):
                        for g, (a, b) in enumerate(GRP):
                            src = ps[:, 6 + c, :] if g == 0 else ps[:, 4 + c, 0:P]
                            last = V.scalar_tensor_tensor(out=u[:, c, a:b], in0=src, scalar=rnorm[:, o, 2 * g + c:2 * g + c + 1],
                                                          in1=u[:, c, a:b], op0=ALU.mult, op1=ALU.add)
                        step(last)
                        dst = u[:, c, :] if o == 0 else yT[:, 2 + c, :]
                        V.tensor_tensor(dst, u[:, c, :], u[:, 2 + 2 * o + c, :], ALU.mult).then_inc(hy_zn, 1)
                for m in range(KC):
                    if m >= 2:
                        add_square(m - 1, sq1, ss1)
                    dve.wait_ge(wo_mm, m + 1)
                    for g, (a, b) in enumerate(GRP):
                        bank = m % 4 + 4 * g
                        V.scalar_tensor_tensor(out=xT[:, m, a:b], in0=ps[:, bank, 0:b - a], scalar=mods[:, 2, m, g:g + 1],
                                               in1=xT[:, m, a:b], op0=ALU.mult, op1=ALU.add).then_inc(x_mid, 1)
                add_square(KC - 1, sq1, ss1)
                normalise(rt1, rc1, xn1)
                dve.wait_ge(ro_mm, 1)
                step(V.tensor_tensor(lg[:, :, :], ps[:, 2, 0:NT * 36].rearrange("p (t n) -> p t n", t=NT),
                                     row(bcast[:, 4:40], NT), ALU.add))
                lc, lf = lg[:, :, 0:NG], lg[:, :, NG:36]
                step(V.tensor_reduce(gmax[:, :], lc, AX.X, ALU.max))
                V.tensor_tensor(gt[:, :, :], lc, bc(gmax[:, :], NG), ALU.subtract).then_inc(ro_sub, 1)
                step(V.tensor_tensor(goh[:, :, :], lc, bc(gmax[:, :], NG), ALU.is_lt))
                step(V.scalar_tensor_tensor(out=goh[:, :, :], in0=goh[:, :, :], scalar=1000.0, in1=row(iota[:, 0:NG], NT),
                                            op0=ALU.mult, op1=ALU.add))
                step(V.tensor_reduce(gidx[:, :], goh[:, :, :], AX.X, ALU.min))
                step(V.tensor_tensor(goh[:, :, :], row(iota[:, 0:NG], NT), bc(gidx[:, :], NG), ALU.is_equal))
                step(V.tensor_scalar(goh[:, :, :], goh[:, :, :], -1.0, 1e30, ALU.add, ALU.mult))
                for g in range(NG):
                    last = V.tensor_tensor(lfm[:, :, g * EPG:(g + 1) * EPG], lf[:, :, g * EPG:(g + 1) * EPG],
                                           goh[:, :, g:g + 1].to_broadcast([P, NT, EPG]), ALU.add)
                step(last)
                for q in range(2):
                    step(V.tensor_reduce(top[q][:, :], lfm[:, :, :], AX.X, ALU.max))
                    step(V.tensor_tensor(lt[:, :, :], lfm[:, :, :], bc(top[q][:, :], NE), ALU.is_lt))
                    step(V.scalar_tensor_tensor(out=lt[:, :, :], in0=lt[:, :, :], scalar=1000.0, in1=row(iota[:, 0:NE], NT),
                                                op0=ALU.mult, op1=ALU.add))
                    step(V.tensor_reduce(tidx[:, :], lt[:, :, :], AX.X, ALU.min))
                    step(V.tensor_tensor(oh[q][:, :, :], row(iota[:, 0:NE], NT), bc(tidx[:, :], NE), ALU.is_equal))
                    if q == 0:
                        step(V.scalar_tensor_tensor(out=lfm[:, :, :], in0=oh[0][:, :, :], scalar=-3e30, in1=lfm[:, :, :],
                                                    op0=ALU.mult, op1=ALU.add))
                V.tensor_tensor(both[:, :, :], oh[0][:, :, :], oh[1][:, :, :], ALU.add).then_inc(ro_oh, 1)
                V.tensor_tensor(ediff[:, :], top[1][:, :], top[0][:, :], ALU.subtract).then_inc(ro_sub2, 1)
                dve.wait_ge(ro_exp, 1)
                step(V.tensor_reduce(gsum[:, :], gexp[:, :, :], AX.X, ALU.add))
                dve.wait_ge(ro_exp2, 1)
                step(V.scalar_tensor_tensor(out=eden[:, :], in0=emx[:, :], scalar=1.0, in1=gsum[:, :], op0=ALU.add, op1=ALU.mult))
                step(V.reciprocal(wgt[0][:, :], eden[:, :]))
                step(V.tensor_tensor(wgt[1][:, :], wgt[0][:, :], emx[:, :], ALU.mult))
                dve.wait_ge(ro_rank, 1)
                V.tensor_copy(rank[:, :, :], ps[:, 3, 0:NT * NE].rearrange("p (t n) -> p t n", t=NT))
                step(V.tensor_copy(cnt[:, :], ps[:, 3, NT * NE:(NT + 1) * NE]))
                step(V.tensor_scalar(thr[:, 0, :], iota[:, 0:NT], float(P), None, ALU.mult))
                thr0 = thr[:, 0, :]
                step(V.tensor_tensor(ebt[:, 0:NE, 0:NT], bc(cnt[:, :], NT), row(thr0, NE), ALU.is_gt))
                step(V.tensor_reduce(nbl[:, :], ebt[:, 0:NE, 0:NT], AX.X, ALU.add))
                step(V.tensor_tensor_scan(out=cum[:, :], data0=ones[:, 0:NE], data1=nbl[:, :], initial=0.0,
                                          op0=ALU.mult, op1=ALU.add))
                step(V.tensor_tensor(exc[:, :], cum[:, :], nbl[:, :], ALU.subtract))
                step(V.tensor_tensor(ebt[:, :, :], row(cum[:, :], NBLK), bc(iota[:, 0:NBLK], NE), ALU.is_le))
                step(V.tensor_reduce(ebf[:, :], ebt[:, :, :], AX.X, ALU.add))
                V.tensor_scalar(ebi[:, :], ebf[:, :], float(NE - 1), None, ALU.min)
                step(V.tensor_scalar(nturn[:, 1:2], cum[:, NE - 1:NE], 1.0, None, ALU.add))
                V.tensor_scalar(nturn[:, 0:1], nturn[:, 1:2], 1, None, ALU.arith_shift_right).then_inc(ro_tab, 1)
                for q in range(2):
                    step(V.tensor_tensor(lt[:, :, :], oh[q][:, :, :], rank[:, :, :], ALU.mult))
                    step(V.tensor_reduce(selr[:, q, :], lt[:, :, :], AX.X, ALU.add))
                    step(V.tensor_tensor(lt[:, :, :], oh[q][:, :, :], row(exc[:, :], NT), ALU.mult))
                    step(V.tensor_reduce(sele[:, q, :], lt[:, :, :], AX.X, ALU.add))
                sr = selr[:, :, :].rearrange("p a b -> p (a b)")
                se = sele[:, :, :].rearrange("p a b -> p (a b)")
                fl = flo[:, :, :].rearrange("p a b -> p (a b)")
                ft = flt[:, :, :, :].rearrange("p a b c -> p (a b) c")
                step(V.tensor_tensor(ft[:, :, 0:4], bc(sr, 4), row(thr[:, 0, 1:5], 2 * NT), ALU.is_ge))
                step(V.tensor_reduce(fl, ft[:, :, 0:4], AX.X, ALU.add))
                V.scalar_tensor_tensor(out=sr, in0=fl, scalar=-float(P), in1=sr, op0=ALU.mult, op1=ALU.add)
                step(V.tensor_tensor(se, se, fl, ALU.add))
                for t in range(NT):
                    for q in range(2):
                        V.tensor_scalar(ohs[:, t, q, :], iota[:, 0:P], selr[:, q, t:t + 1], None, ALU.is_equal)
                        last = V.tensor_scalar(ohb[:, t, q, :], iota[:, 0:NBLK + SLOTS], sele[:, q, t:t + 1],
                                               iota[:, P + t * TOPK + q:P + t * TOPK + q + 1], ALU.is_equal, ALU.mult)
                last.then_inc(ro_1h, 1)
                dve.wait_ge(ro_tm, 1)
                step(V.tensor_scalar(tabz[:, :], ps[:, 2, 256:256 + NBLK + SLOTS], 0.0, 8192.0, ALU.is_equal, ALU.mult))
                step(V.scalar_tensor_tensor(out=tabf[:, :], in0=ps[:, 2, 256:256 + NBLK + SLOTS], scalar=-1.0, in1=tabz[:, :],
                                            op0=ALU.add, op1=ALU.add))
                step(V.tensor_copy(tabs[:, 1, :], tabf[:, :]))
                V.tensor_scalar(tabs[:, 0, :], tabs[:, 1, :], 1, None, ALU.arith_shift_right).then_inc(ro_tok, 1)
                for s in range(SLOTS):
                    dve.sem_inc(ye_d[s])
                turns = dve.value_load(nturn[0:1, 0:1], min_val=1, max_val=NBLK // 2)
                with dve.Fori(0, turns) as j:
                    for s in range(SLOTS):
                        dve.wait_ge(sg_ok[s], j + 1)
                        dve.wait_ge(u_mm[s], j + 1)
                        V.tensor_tensor(hh[:, s, :], sg[:, s, :], ps[:, 3, 0:FE], ALU.mult).then_inc(hh_ok[s], 1)
                        dve.wait_ge(ht_mm[s], j + 1)
                        V.tensor_copy(he[:, s, :, :].rearrange("p k t -> p (k t)"), ps[:, 4, 0:2 * P]).then_inc(he_ok[s], 1)
                        dve.wait_ge(y_mm[s], j * 2 + 3)
                        dve.wait_ge(y_out[s], j * 16 + 16)
                        V.tensor_copy(ye[:, s, 512:1024], ps[:, 7, :]).then_inc(ye_d[s], 1)
                for s in range(SLOTS):
                    dve.wait_ge(y_out[s], turns * 16 + 16)
                for t in range(NT):
                    dve.wait_ge(yc_in[t % 2], 16 * (t // 2 + 1))
                    if t >= 2:
                        dve.wait_ge(yc_mm, t - 1)
                    step(V.tensor_scalar(ysum[:, t % 2, :], ycomb[:, t % 2, 0, :], wgt[0][:, t:t + 1], None, ALU.mult))
                    V.scalar_tensor_tensor(out=ysum[:, t % 2, :], in0=ycomb[:, t % 2, 1, :], scalar=wgt[1][:, t:t + 1],
                                           in1=ysum[:, t % 2, :], op0=ALU.mult, op1=ALU.add).then_inc(yc_sum, 1)
                    if t >= 1:
                        residual(t - 1)
                residual(NT - 1)
                last_of_layer(dve, "dve")
            for k in range(1, KC):
                add_square(k, sq0, ss0)
            normalise(rt0, rc0, xn0)


INPUTS = ("x_prompt x_sample cache_k cache_v c c_ctx ada_w ada_b norm1_g norm2_g w_in conv_dw_w conv_dw_b "
          "conv_ln_g conv_ln_b hy_short_w hy_short_b hy_fw1 hy_fb1 hy_freq1 hy_fw2 hy_fb2 hy_freq2 hy_fw3 hy_fb3 "
          "hy_d attn_sink w_out router_coarse_w router_coarse_b router_fine_w router_fine_b exp_gate exp_up "
          "exp_down norm_f_g").split()
OUTPUTS = {"y_prompt": (1, LP, D), "y_sample": (1, LS, D), "state_k": (1, DEPTH, LP, 2, HD),
           "state_v": (1, DEPTH, LP, 2, HD)}


def program(nc, arrays):
    io = {}
    for name, a in arrays.items():
        io[name] = nc.dram_tensor("in_" + name, a.shape, mybir.dt.from_np(a.dtype), kind="ExternalInput").ap()
    out = {n: nc.dram_tensor("out_" + n, s, F32, kind="ExternalOutput").ap() for n, s in OUTPUTS.items()}
    trunk(nc, io, out)


def kernel(**inputs):
    import concourse.bacc as bacc
    from concourse.bass_utils import run_bass_kernel_spmd

    arrays = {n: np.ascontiguousarray(inputs[n]) for n in INPUTS}
    arrays.update({"c_" + n: a for n, a in constants().items()})
    nc = bacc.Bacc("TRN2", target_bir_lowering=False, num_devices=1)
    program(nc, arrays)
    r = run_bass_kernel_spmd(nc, [{"in_" + n: a for n, a in arrays.items()}], core_ids=[0])
    return tuple(r.results[0]["out_" + n] for n in OUTPUTS)
```

```python
import numpy as np
import concourse.bass as bass
from concourse import mybir
from contextlib import ExitStack

F32 = mybir.dt.float32
I32 = mybir.dt.int32
U32 = mybir.dt.uint32
ALU = mybir.AluOpType
ACT = mybir.ActivationFunctionType
AX = mybir.AxisListType

P = 128
D = 1024
KC = D // P
LS, LP = 512, 128
T = LS + LP
NT = T // P
DEPTH = 2
CH = 256
TAPS = 31
PAD = TAPS // 2
CONV = LS + PAD + LP
FFN = 64
EMB = 33
HD = 64
NG, EPG, NE, FE = 4, 8, 32, 256
TOPK = 2
SLOTS = 2
GRID_W = 64
EPS = 1e-6
NEG = -1e30
BR = 96
NTHR = -(-T // BR)
NBLK = -(-(T * TOPK + NE * (BR - 1)) // BR // SLOTS) * SLOTS
WSLOT = 6 * D
TWO_PI_HI = 6.28125
TWO_PI_LO = 2.0 * np.pi - TWO_PI_HI
MAGIC = 12582912.0
ROWS = TAPS + 3 + 9 + 3 + 2
R_DWB, R_LNG, R_LNB, R_SW, R_SB, R_HD = TAPS, TAPS + 1, TAPS + 2, TAPS + 3, TAPS + 12, TAPS + 15


def constants():
    c = {}
    f = lambda a: np.ascontiguousarray(a, dtype=np.float32)

    def tile_rows(a):
        return a.reshape(-1, P, a.shape[-1]).transpose(1, 0, 2)

    for n, L in (("s", LS), ("p", LP)):
        t = np.arange(L, dtype=np.float64)
        w = 2 * np.pi * np.outer(t, np.arange(L) + 0.5) / (2 * L)
        c["fwd_" + n] = f(tile_rows(np.concatenate([np.cos(w), -np.sin(w)], axis=1)))
        c["inv_" + n] = f(tile_rows(np.concatenate([np.cos(w.T), -np.sin(w.T)], axis=0) / L))
        g = 2 * np.pi * (np.outer(t, t) % L) / L
        c["mix_" + n] = f(tile_rows(np.concatenate([np.cos(g), np.sin(g)], axis=1) / np.sqrt(L * CH)))
    t = np.arange(CH, dtype=np.float64)
    g = 2 * np.pi * (np.outer(t, t) % CH) / CH
    c["mix_c"] = f(tile_rows(np.concatenate([np.cos(g), -np.sin(g)], axis=1)))
    feat, win = [], []
    nb = (EMB - 1) // 2
    fr = np.linspace(1e-4, nb - 1, nb)
    lo, hi = np.log(1e-2) / 1.5, np.log(1e-2) / 0.3
    for L in (LS, LP):
        t = np.linspace(0.0, 1.0, L)[:, None]
        w = 2 * np.pi * np.arange(L)[:, None] / L
        feat.append(np.concatenate([t, np.cos(fr * w), -np.sin(fr * w)], axis=1))
        win.append(np.exp(-t * np.abs(np.linspace(lo, hi, CH))[None]) + 0.05)
    c["feat"] = f(np.concatenate(feat).T)
    c["win"] = f(tile_rows(np.concatenate(win)))
    tok = np.arange(LS)
    inv = 10000.0 ** (-np.arange(16) / 16)
    ang = np.concatenate([(tok // GRID_W)[:, None] * inv, (tok % GRID_W)[:, None] * inv], axis=1)
    c["rope"] = f(np.stack([np.tile(np.cos(ang).T, (4, 1)), np.tile(np.sin(ang).T, (4, 1))], axis=1))
    rot = np.zeros((P, P))
    for h in range(2):
        for d in range(32):
            rot[h * 64 + 32 + d, h * 64 + d] = -1
            rot[h * 64 + d, h * 64 + 32 + d] = 1
    i = np.arange(P)
    left = np.where(i[None] < i[:, None], NEG, 0)
    right = np.where(i[None] > i[:, None], NEG, 0)
    c["sq"] = f(np.stack([np.eye(P), np.ones((P, P)), np.full((P, P), 1 / D), np.full((P, P), 1 / CH),
                          rot, i[:, None] < i[None], left, right], axis=1))
    val = (np.arange(NT)[None, :, None] * P + i[:, None, None]) * TOPK + np.arange(TOPK)[None, None] + 1
    row = lambda n: np.tile(np.arange(n)[None], (P, 1))
    c["iota"] = f(np.concatenate([row(P), val.transpose(0, 2, 1).reshape(P, TOPK * NT)], axis=1))
    return c


def trunk(nc, io, out):
    ctx = ExitStack()
    with ctx:
        def sem(name):
            return ctx.enter_context(nc.semaphore(name))

        def sb(name, shape, dt=F32):
            return ctx.enter_context(nc.sbuf_tensor(name, shape, dt))

        xT = sb("xT", [P, KC, T])
        hT = sb("hT", [P, KC, T])
        yT = sb("yT", [P, KC, T])
        ring = sb("ring", [P, SLOTS, WSLOT])
        dft = sb("dft", [P, 4, 2 * LS])
        inv_s = sb("inv_s", [P, 8, LS])
        fwd_p = sb("fwd_p", [P, 1, 2 * LP])
        inv_p = sb("inv_p", [P, 2, LP])
        mix_p = sb("mix_p", [P, 1, 2 * LP])
        mix_c = sb("mix_c", [P, 2, 2 * CH])
        feat = sb("feat", [EMB, T])
        win = sb("win", [P, NT, CH])
        rope = sb("rope", [P, 2, LS])
        sq = sb("sq", [P, 8, P])
        ident, ones, mean_d, mean_c, rot, tri, mask_l, mask_r = [sq[:, i, :] for i in range(8)]
        iota = sb("iota", [P, P + NT * TOPK])
        epsc = sb("epsc", [P, 1])
        c_raw = sb("c_raw", [P, 2, KC])
        c_act = sb("c_act", [P, KC, 32])
        nf = sb("nf", [P, KC])
        ada_b = sb("ada_bs", [P, 6, KC])
        norms = sb("norms", [P, 2, KC])
        prm_ = sb("prm", [P, CH])
        prm = prm_[0:ROWS, :]
        kvo = prm_.rearrange("p (q c) -> p q c", q=2)
        prmT = sb("prmT", [P, 2, ROWS])
        frow = sb("frow", [4, FFN])
        frowT = sb("frowT", [FFN, 4])
        fw1 = sb("fw1", [EMB, FFN])
        fw2 = sb("fw2", [FFN, FFN])
        fw3_ = sb("fw3", [P, 2 * 2 * CH])
        fw3 = fw3_[0:FFN + 1, :].rearrange("p (a b c) -> p a b c", a=2, b=2)
        brow = sb("brow", [1, 40])
        bcast = sb("bcast", [P, 40])
        wr = sb("wr", [P, KC, 36])
        ckv = sb("ckv", [P, 2, P])
        ckT = sb("ckT", [P, P])
        mods = sb("mods", [P, 6, KC, 2])
        gain = sb("gain", [P, 2, KC, 2])
        WORK = 8192
        work = sb("work", [P, WORK])

        def at(base, off, *dims):
            n = int(np.prod(dims))
            v = base[:, off:off + n]
            if len(dims) == 1:
                return v
            names = "abcd"[:len(dims)]
            return v.rearrange("p (" + " ".join(names) + ") -> p " + " ".join(names),
                               **{x: d for x, d in zip(names[1:], dims[1:])})

        hflat = hT[:, :, :].rearrange("p k t -> p (k t)")
        yflat = yT[:, :, :].rearrange("p k t -> p (k t)")
        rms = at(work, 0, T)
        rinv = at(work, T, T)
        GW = PAD + CONV + PAD
        CW = 3 * LS
        sig = at(work, 0, 2, T)
        glu = at(work, CW, 2, GW)
        csq = at(work, CW, 2, CONV)
        acc = at(work, CW + 2 * GW, 2, CONV)
        crs = at(work, CW + 2 * GW + 2 * CONV, CONV)
        crn = at(work, CW + 2 * GW + 3 * CONV, CONV)
        fX = at(work, WORK - 3840, NT, CH)
        fA = at(work, WORK - 2560, 2, 2, T)
        qraw = at(work, WORK - 2560, 2, T)
        kraw = at(work, WORK - 1280, T)
        vtok = at(work, WORK - 640, NT, P)
        qrope = at(work, 0, 2, LS)
        krope = at(work, 1024, LS)
        prob = at(work, 1536, 4, 512)
        probT = at(work, 3584, 4, 512)
        otok = at(work, 5632, 256)
        ast = sb("ast", [P, 2, 8, 4])
        u = ([yT[:, 2 + c, :] for c in range(2)] + [at(ring[:, 0, :], 4 * D + i * T, T) for i in range(3)]
             + [fw3_[:, 0:T]])
        zs = at(work, 3840, NT, CH)
        ctmp = at(work, 5120, 2, 2, 2, CH)
        h1 = at(work, 2 * T, T)
        h2 = at(work, 3 * T, T)
        fa_ = at(work, 4 * T, T)
        fk_ = at(work, 5 * T, T)
        ftime = at(work, 6 * T, 2, 2, CH)
        fabs = at(work, 6 * T + 1024, 2, 2, CH)
        fsum = at(work, 6 * T + 2048, 2, 2, CH)
        adarow = at(work, 2 * T, 2 * D)
        kspec = at(hflat, 0, 2, NT, CH)
        yspec = at(hflat, 2560, 2, NT, CH)
        evod = at(yflat, 0, NT, 2, CH)
        knew = at(yflat, 2560, 2, NT, CH)
        rnorm = sb("rnorm", [P, 2, 4])
        xg = at(work, 0, SLOTS, D)
        xe = at(work, 2048, SLOTS, KC, BR)
        ye = at(work, 4096, SLOTS, D)
        sg = at(work, 6144, SLOTS, 2 * BR)
        he = at(work, 6144 + 4 * BR, SLOTS, 2, BR)
        htok = ye
        ycomb = at(work, 0, 2, TOPK, D)
        ysum = at(work, 4096, 2, D)
        R = [0]

        def rt(*dims):
            o = R[0]
            R[0] += int(np.prod(dims))
            return at(yflat, o, *dims)

        lg = rt(NT, 36)
        gmax = rt(NT)
        gidx = rt(NT)
        goh = rt(NT, NG)
        gt = rt(NT, NG)
        gexp = rt(NT, NG)
        gsum = rt(NT)
        lfm = rt(NT, NE)
        lt = rt(NT, NE)
        top = [rt(NT) for _ in range(2)]
        tidx = rt(NT)
        oh = [rt(NT, NE) for _ in range(2)]
        both = rt(NT + 1, NE)
        before = rt(NT + 1, NE)
        lgT = at(work, 7 * D, T)
        ediff = rt(NT)
        emx = rt(NT)
        eden = rt(NT)
        wgt = [rt(NT) for _ in range(2)]
        rank = rt(NT, NE)
        cnt = rt(NE)
        nbl = rt(NE)
        cum = rt(NE)
        exc = rt(NE)
        thr = rt(NTHR)
        selr = rt(2, NT)
        sele = rt(2, NT)
        flo = rt(2, NT)
        flt = rt(2, NT, NTHR - 1)
        ohb = rt(2 * NT, NBLK + SLOTS)
        ohs = rt(2 * NT, BR)
        ebt = at(work, 2 * D, NBLK, NE)
        ebf = rt(NBLK)
        tabf = rt(NBLK + SLOTS)
        tabz = rt(NBLK + SLOTS)
        assert R[0] <= KC * T, R
        ebi = sb("ebi", [P, NBLK], I32)
        nturn = sb("nturn", [P, 2], I32)
        tabs = sb("tabs", [P, 2, NBLK + SLOTS], I32)
        icol = sb("icol", [P, SLOTS, 2], I32)

        ps = ctx.enter_context(nc.psum_tensor("ps", [P, 8, 512], F32))

        H_dram = nc.dram_tensor("h_scratch", (T, D), F32, kind="Internal").ap()
        K_dram = nc.dram_tensor("k_scratch", (2, P, 2 * NT * CH), F32, kind="Internal").ap()
        Y_dram = nc.dram_tensor("y_scratch", (T * TOPK, D), F32, kind="Internal").ap()

        const_in = sem("const_in")
        cond_in = sem("cond_in")
        x_in = sem("x_in")
        set_up = sem("set_up")
        c_ready = sem("c_ready")
        xT_mm = sem("xT_mm")
        xT_in = sem("xT_in")
        arrived = sem("layer_arrived")
        go = {e: sem("layer_go_" + e) for e in ("pe", "act", "dve", "pool")}
        out_st = sem("out_st")
        ada_in0 = sem("ada_in0")
        ada_in1 = sem("ada_in1")
        par_in = sem("par_in")
        fpar_in = sem("fpar_in")

        w_full0 = sem("w_full0")
        w_full1 = sem("w_full1")
        w_used = sem("w_used")
        cs_in = sem("cs_in")
        f_in = sem("f_in")
        row_mm = sem("row_mm")
        row_ev = sem("row_ev")
        ada_t = sem("ada_t")
        par_mm = sem("par_mm")
        par_ev = sem("par_ev")
        mods_ok = sem("mods_ok")
        dchain = sem("dchain")
        sq0 = sem("sq0")
        ss0 = sem("ss0")
        ms0 = sem("ms0")
        rt0 = sem("rt0")
        xn0 = sem("xn0")
        h0 = sem("h0")
        sq1 = sem("sq1")
        ss1 = sem("ss1")
        ms1 = sem("ms1")
        rt1 = sem("rt1")
        xn1 = sem("xn1")
        h1s = sem("h1s")
        cv_mm = sem("cv_mm")
        cv_sig = sem("cv_sig")
        cv_glu = sem("cv_glu")
        cv_tap = sem("cv_tap")
        ln_mm = sem("ln_mm")
        ln_ctr = sem("ln_ctr")
        ln_sq = sem("ln_sq")
        ln_var = sem("ln_var")
        ln_rt = sem("ln_rt")
        ln_out = sem("ln_out")
        ya_ok = sem("ya_ok")
        fo_x = sem("fo_x")
        fo_xe = sem("fo_xe")
        fo_a = sem("fo_a")
        fo_ae = sem("fo_ae")
        fo_b = sem("fo_b")
        yc_ok = sem("yc_ok")
        at_mm = sem("at_mm")
        at_ev = sem("at_ev")
        at_rot = sem("at_rot")
        at_rope = sem("at_rope")
        kv_out = sem("kv_out")
        at_s = sem("at_s")
        at_max = sem("at_max")
        at_exp = sem("at_exp")
        at_t = sem("at_t")
        at_te = sem("at_te")
        at_pv = sem("at_pv")
        at_o = sem("at_o")
        at_ot = sem("at_ot")
        yd_ok = sem("yd_ok")
        hy_m1 = sem("hy_m1")
        hy_a1 = sem("hy_a1")
        hy_s1 = sem("hy_s1")
        hy_m2 = sem("hy_m2")
        hy_a2 = sem("hy_a2")
        hy_s2 = sem("hy_s2")
        hy_u = sem("hy_u")
        hy_u1 = sem("hy_u1")
        hy_uc = sem("hy_uc")
        hy_f = sem("hy_f")
        hy_raw = sem("hy_raw")
        hy_abs = sem("hy_abs")
        hy_eo = sem("hy_eo")
        hy_norm = sem("hy_norm")
        hy_rn = sem("hy_rn")
        hy_k = sem("hy_k")
        hy_ke = sem("hy_ke")
        hy_sum = sem("hy_sum")
        k_out = sem("k_out")
        k_in = sem("k_in")
        hy_zt = sem("hy_zt")
        hy_z = sem("hy_z")
        hy_dz = sem("hy_dz")
        hy_fz = sem("hy_fz")
        hy_y = sem("hy_y")
        hy_inv = sem("hy_inv")
        hy_zn = sem("hy_zn")
        wo_mm = sem("wo_mm")
        x_mid = sem("x_mid")
        hs_mm = sem("hs_mm")
        hs_ev = sem("hs_ev")
        hs_st0 = sem("hs_st0")
        hs_st1 = sem("hs_st1")
        ro_mm = sem("ro_mm")
        ro_lt = sem("ro_lt")
        ro_lg = sem("ro_lg")
        ro_sub = sem("ro_sub")
        ro_exp = sem("ro_exp")
        ro_oh = sem("ro_oh")
        ro_rank = sem("ro_rank")
        ro_sub2 = sem("ro_sub2")
        ro_exp2 = sem("ro_exp2")
        ro_tab = sem("ro_tab")
        ro_1h = sem("ro_1h")
        ro_tm = sem("ro_tm")
        ro_tok = sem("ro_tok")
        wg_full0 = sem("wg_full0")
        wg_full1 = sem("wg_full1")
        wd_full0 = sem("wd_full0")
        wd_full1 = sem("wd_full1")
        ic0 = sem("ic0")
        ic1 = sem("ic1")
        xg_in0 = sem("xg_in0")
        xg_in1 = sem("xg_in1")
        xt_mm0 = sem("xt_mm0")
        xt_mm1 = sem("xt_mm1")
        xe_ok0 = sem("xe_ok0")
        xe_ok1 = sem("xe_ok1")
        g_mm0 = sem("g_mm0")
        g_mm1 = sem("g_mm1")
        u_mm0 = sem("u_mm0")
        u_mm1 = sem("u_mm1")
        sg_ok0 = sem("sg_ok0")
        sg_ok1 = sem("sg_ok1")
        he_ok0 = sem("he_ok0")
        he_ok1 = sem("he_ok1")
        y_mm0 = sem("y_mm0")
        y_mm1 = sem("y_mm1")
        ye_a0 = sem("ye_a0")
        ye_a1 = sem("ye_a1")
        ye_d0 = sem("ye_d0")
        ye_d1 = sem("ye_d1")
        y_out0 = sem("y_out0")
        y_out1 = sem("y_out1")
        hc0 = sem("hc0")
        hc1 = sem("hc1")
        pool_nop = sem("pool_nop")
        yc_in0 = sem("yc_in0")
        yc_in1 = sem("yc_in1")
        yc_first = sem("yc_first")
        yc_sum = sem("yc_sum")
        yc_mm = sem("yc_mm")
        x_new = sem("x_new")
        layer_range = range(w_full0.num, x_new.num + 1)
        assert len(layer_range) == 138, "the layer's semaphores lie in one range"
        w_full = [w_full0, w_full1]
        wg_full = [wg_full0, wg_full1]
        wd_full = [wd_full0, wd_full1]
        hs_st = [hs_st0, hs_st1]
        ic = [ic0, ic1]
        xg_in = [xg_in0, xg_in1]
        xt_mm = [xt_mm0, xt_mm1]
        xe_ok = [xe_ok0, xe_ok1]
        g_mm = [g_mm0, g_mm1]
        u_mm = [u_mm0, u_mm1]
        sg_ok = [sg_ok0, sg_ok1]
        he_ok = [he_ok0, he_ok1]
        y_mm = [y_mm0, y_mm1]
        ye_a = [ye_a0, ye_a1]
        ye_d = [ye_d0, ye_d1]
        y_out = [y_out0, y_out1]
        yc_in = [yc_in0, yc_in1]
        ada_in = [ada_in0, ada_in1]

        I_CONV, I_FOUR, I_ATT, I_HY, I_OUT = 8, 9, 10, 11, 12

        def wait_item(eng, i):
            eng.wait_ge(w_full[i % SLOTS], 16 * (i // SLOTS))

        def slot(i, *dims):
            return at(ring[:, i % SLOTS, :], 0, *dims)

        GRP = ((0, LS), (LS, T))

        def tap(m, j):
            r = R_SW + 3 * j + m // 2
            return prmT[:, m % 2, r:r + 1]

        def last_of_layer(eng, name):
            eng.drain().then_inc(arrived, 1)
            eng.wait_ge(go[name], 1)
            eng.sem_clear(go[name])

        block = ctx.enter_context(nc.Block())

        @block.sync
        def _(sp):
            sp.dma_start(work[:, 0:NT * D].rearrange("p (t d) -> p t d", t=NT)[:, 0:4, :],
                         io["x_sample"][0].rearrange("(t p) d -> p t d", p=P)).then_inc(x_in, 16)
            sp.dma_start(work[:, 4 * D:NT * D], io["x_prompt"][0]).then_inc(x_in, 16)
            sp.dma_start(sq[:, :, :], io["c_sq"]).then_inc(x_in, 16)

            def ada_first(l, i):
                sp.dma_start(slot(i, WSLOT), io["ada_w"][l].rearrange("(p k) n -> p k n", k=KC)[:, i, :]).then_inc(ada_in[i], 16)

            def table(dst, name):
                full = dst[:, :] if len(dst.shape) == 2 else dst[:, :, :]
                sp.dma_start(full, io["c_" + name]).then_inc(const_in, 16)

            ada_first(0, 0)
            table(feat, "feat")
            table(win, "win")
            ada_first(0, 1)
            table(dft, "fwd_s")
            for dst, name in ((fwd_p, "fwd_p"), (inv_p, "inv_p"), (mix_p, "mix_p"), (mix_c, "mix_c"), (iota, "iota"),
                              (rope, "rope")):
                table(dst, name)
            with sp.Fori(0, DEPTH) as l:
                ada = io["ada_w"][l].rearrange("(p k) n -> p k n", k=KC)
                win_l = io["w_in"][l].rearrange("(p k) n -> p k n", k=KC)
                wout_l = io["w_out"][l].rearrange("(i p) n -> p i n", p=P)
                for i in range(SLOTS, KC):
                    sp.wait_ge(w_used, i - SLOTS + 1)
                    sp.dma_start(slot(i, WSLOT), ada[:, i, :]).then_inc(w_full[i % SLOTS], 16)
                for i, lo, n, used, count in ((I_CONV, 0, 512, w_used, KC - 1), (I_FOUR, 1280, 256, w_used, KC),
                                              (I_ATT, 1536, 512, cv_mm, 4), (I_HY, 512, 768, fo_x, NT)):
                    sp.wait_ge(used, count)
                    if i == I_FOUR:
                        sp.wait_ge(hy_k, 6)
                        sp.dma_start(dft[:, :, :], io["c_mix_s"]).then_inc(cs_in, 16)
                    sp.dma_start(slot(i, KC, n), win_l[:, :, lo:lo + n]).then_inc(w_full[i % SLOTS], 16)
                sp.wait_ge(fo_a, 6)
                sp.dma_start(dft[:, :, :], io["c_fwd_s"]).then_inc(f_in, 16)
                sp.dma_start(inv_s[:, :, :], io["c_inv_s"]).then_inc(f_in, 16)
                for i, used, count in ((I_OUT, at_mm, 5), (I_OUT + 1, hy_u, 7)):
                    sp.wait_ge(used, count)
                    if used is hy_u:
                        sp.wait_ge(k_out, 32)
                        sp.dma_start(kspec.rearrange("p q t c -> p (q t c)"), K_dram[0]).then_inc(k_in, 16)
                    h = i - I_OUT
                    sp.dma_start(slot(i, 4, D), wout_l[:, 4 * h:4 * h + 4, :]).then_inc(w_full[i % SLOTS], 16)
                sp.wait_ge(hy_y, 5)
                sp.dma_start(kspec.rearrange("p q t c -> p (q t c)"), K_dram[1]).then_inc(k_in, 16)
                for t in range(NT):
                    sp.wait_ge(hs_ev, 2 * t + 2)
                    sp.dma_start(H_dram[t * P:(t + 1) * P, :], htok[:, t % 2, :]).then_inc(hs_st[t % 2], 16)
                sp.wait_ge(wo_mm, KC)
                sp.wait_ge(ro_tab, 1)
                turns = sp.value_load(nturn[0:1, 0:1], min_val=1, max_val=NBLK // 2)
                with sp.Fori(0, turns) as j:
                    for s in range(SLOTS):
                        e = sp.value_load(ebi[0:1, bass.ds(j * SLOTS + s, 1)], min_val=0, max_val=NE - 1)
                        sp.wait_ge(y_mm[s], j * 2 + 1)
                        gw = slot(s, 3, KC * FE)
                        for q, name in ((0, "exp_gate"), (1, "exp_up")):
                            src = io[name].rearrange("l e (p k) f -> (l e) p (k f)", k=KC)
                            sp.dma_start(gw[:, q, :], src[l * NE + e]).then_inc(wg_full[s], 16)
                        if s == 0:
                            sp.wait_ge(xg_in[1], 16)
                        src = io["exp_down"].rearrange("l e (p k) f -> (l e) p (k f)", k=2)
                        sp.dma_start(gw[:, 2, :], src[l * NE + e]).then_inc(wd_full[s], 16)
                for s in range(SLOTS):
                    sp.wait_ge(y_out[s], turns * 16 + 16)
                yrow = Y_dram.rearrange("(t p k) d -> t p (k d)", p=P, k=TOPK)
                for t in range(NT):
                    if t >= 2:
                        sp.wait_ge(yc_sum, t - 1)
                    sp.dma_start(ycomb[:, t % 2, :, :].rearrange("p k d -> p (k d)"), yrow[t]) \
                        .then_inc(yc_in[t % 2], 16)
                for i in range(SLOTS):
                    ada_first(DEPTH - 1, i)
                sp.wait_ge(kv_out, 32)
                sp.wait_ge(arrived, 4)
                sp.sem_clear(layer_range)
                sp.sem_clear(arrived)
                for e in ("pe", "act", "dve", "pool"):
                    sp.sem_inc(go[e])
            for t in range(NT):
                sp.wait_ge(hs_ev, 2 * t + 2)
                dst = out["y_sample"][0, t * P:(t + 1) * P, :] if t < 4 else out["y_prompt"][0]
                sp.dma_start(dst, work[:, t * D:(t + 1) * D]).then_inc(out_st, 16)
            for i in range(SLOTS):
                sp.wait_ge(ada_in[i], 16 * (DEPTH + 1))
            sp.wait_ge(out_st, 16 * NT)

        @block.gpsimd
        def _(pool):
            pool.dma_start(c_raw[:, 0, :], io["c"][0].rearrange("(p k) -> p k", k=KC)).then_inc(cond_in, 16)
            pool.dma_start(c_raw[:, 1, :], io["c_ctx"].rearrange("(p k) -> p k", k=KC)).then_inc(cond_in, 16)
            pool.dma_start(nf[:, :], io["norm_f_g"].rearrange("(p k) -> p k", k=KC)).then_inc(cond_in, 16)
            pool.memset(c_act[:, :, :], 0.0)
            pool.memset(epsc[:, :], EPS).then_inc(set_up, 1)
            def parameters(l):
                for dst, src in (
                        (frow[0:1, :], io["hy_fb1"][l].rearrange("(a c) -> a c", a=1)),
                        (frow[1:2, :], io["hy_freq1"][l].rearrange("(a c) -> a c", a=1)),
                        (frow[2:3, :], io["hy_fb2"][l].rearrange("(a c) -> a c", a=1)),
                        (frow[3:4, :], io["hy_freq2"][l].rearrange("(a c) -> a c", a=1)),
                        (fw1[:, :], io["hy_fw1"][l]),
                        (fw2[:, :], io["hy_fw2"][l]),
                        (fw3_[0:FFN, :], io["hy_fw3"][l]),
                        (fw3_[FFN:FFN + 1, :],
                         io["hy_fb3"][l].rearrange("(a c) -> a c", a=1))):
                    pool.dma_start(dst, src).then_inc(fpar_in, 16)
                for dst, src in (
                        (ada_b[:, :, :], io["ada_b"][l].rearrange("(a p k) -> p a k", a=6, k=KC)),
                        (norms[:, 0, :], io["norm1_g"][l].rearrange("(p k) -> p k", k=KC)),
                        (norms[:, 1, :], io["norm2_g"][l].rearrange("(p k) -> p k", k=KC)),
                        (prm[0:TAPS, :], io["conv_dw_w"][l]),
                        (prm[R_DWB:R_DWB + 1, :], io["conv_dw_b"][l].rearrange("(a c) -> a c", a=1)),
                        (prm[R_LNG:R_LNG + 1, :], io["conv_ln_g"][l].rearrange("(a c) -> a c", a=1)),
                        (prm[R_LNB:R_LNB + 1, :], io["conv_ln_b"][l].rearrange("(a c) -> a c", a=1)),
                        (prm[R_SW:R_SW + 9, :], io["hy_short_w"][l].rearrange("j (g c) -> (j g) c", c=CH)),
                        (prm[R_SB:R_SB + 3, :], io["hy_short_b"][l].rearrange("(g c) -> g c", c=CH)),
                        (prm[R_HD:R_HD + 2, :], io["hy_d"][l]),
                        (brow[:, 0:4], io["attn_sink"][l].rearrange("(a c) -> a c", a=1)),
                        (brow[:, 4:8], io["router_coarse_b"][l].rearrange("(a c) -> a c", a=1)),
                        (brow[:, 8:40], io["router_fine_b"][l].rearrange("(a c) -> a c", a=1)),
                        (ckv[:, 0, :], io["cache_k"][0, l].rearrange("t h d -> t (h d)")),
                        (ckv[:, 1, :], io["cache_v"][0, l].rearrange("t h d -> t (h d)"))):
                    pool.dma_start(dst, src).then_inc(par_in, 16)

            def router_weights(l):
                for n0, n1, name in ((0, NG, "router_coarse_w"), (NG, NG + NE, "router_fine_w")):
                    pool.dma_start(wr[:, :, n0:n1], io[name][l].rearrange("(p k) n -> p k n", k=KC)).then_inc(par_in, 16)

            def modulate_context(n, xn_sem, hc_sem):
                for k in range(KC):
                    pool.wait_ge(xn_sem, k + 1)
                    nc.gpsimd.tensor_scalar(hT[:, k, LS:T], hT[:, k, LS:T], gain[:, n, k, 1:2], mods[:, 3 * n, k, 1:2],
                                            ALU.mult, ALU.add).then_inc(hc_sem, 1)

            parameters(0)
            router_weights(0)
            with pool.Fori(0, DEPTH) as l:
                for o in range(2):
                    for t in range(NT):
                        pool.wait_ge(hy_abs, NT * o + t + 1)
                        g = 0 if t < 4 else 1
                        if t == 0 and o:
                            pool.wait_ge(hy_norm, 1)
                        if t in (0, 4):
                            last = pool.tensor_copy(fsum[:, g, :, :], fabs[:, t % 2, :, :])
                        else:
                            last = pool.tensor_tensor(fsum[:, g, :, :], fsum[:, g, :, :], fabs[:, t % 2, :, :], ALU.add)
                        last.then_inc(hy_sum, 1)
                        pool.wait_ge(hy_sum, 7 * o + t + 1)
                    for g in range(2):
                        pool.tensor_tensor(fsum[:, g, 0, :], fsum[:, g, 0, :], fsum[:, g, 1, :], ALU.add).then_inc(hy_sum, 1)
                pool.wait_ge(mods_ok, 3)
                modulate_context(0, xn0, hc0)
                pool.wait_ge(at_ev, 8)
                for q, name in ((0, "state_k"), (1, "state_v")):
                    pool.dma_start(out[name][0, l].rearrange("t h d -> t (h d)"), kvo[:, q, :]).then_inc(kv_out, 16)
                modulate_context(1, xn1, hc1)
                for s in range(SLOTS):
                    pool.dma_start(xg[:, s, :], io["x_prompt"][0]).then_inc(y_out[s], 16)
                pool.wait_ge(kv_out, 32)
                parameters(DEPTH - 1)
                pool.wait_ge(ro_mm, 1)
                router_weights(DEPTH - 1)
                for s in range(SLOTS):
                    pool.wait_ge(y_out[s], 16)
                for q in range(2):
                    pool.wait_ge(hs_st[q], 16 * ((NT + 1 - q) // 2))
                pool.wait_ge(ro_tok, 1)
                turns = pool.value_load(nturn[0:1, 0:1], min_val=1, max_val=NBLK // 2)

                def gather_rows(s):
                    pool.indirect_dma_start(
                        xg[0:BR, s, :], None, H_dram[:, :],
                        bass.IndirectOffsetOnAxis(ap=icol[0:BR, s, 0:1].bitcast(U32), axis=0),
                        bounds_check=T - 1, oob_is_err=False).then_inc(xg_in[s], 16)

                for s in range(SLOTS):
                    pool.tensor_copy(icol[0:BR, s, 0:1], tabs[0:BR, 0, s:s + 1]).then_inc(ic[s], 1)
                for s in range(SLOTS):
                    pool.wait_ge(ic[s], 1)
                    gather_rows(s)
                with pool.Fori(0, turns) as j:
                    for s in range(SLOTS):
                        pool.wait_ge(xg_in[s], j * 16 + 16)
                        pool.sem_inc(pool_nop)
                        pool.wait_ge(y_out[s], j * 16 + 16)
                        pool.sem_inc(pool_nop)
                        pool.tensor_copy(icol[0:BR, s, 0:1], tabs[0:BR, 0, bass.ds(j * SLOTS + SLOTS + s, 1)])
                        pool.tensor_copy(icol[0:BR, s, 1:2], tabs[0:BR, 1, bass.ds(j * SLOTS + s, 1)]).then_inc(ic[s], 1)
                        pool.wait_ge(ic[s], j + 2)
                        pool.sem_inc(pool_nop)
                        pool.wait_ge(xt_mm[s], j + 1)
                        pool.sem_inc(pool_nop)
                        gather_rows(s)
                        pool.wait_ge(ye_a[s], j + 2)
                        pool.sem_inc(pool_nop)
                        pool.wait_ge(ye_d[s], j + 2)
                        pool.sem_inc(pool_nop)
                        pool.indirect_dma_start(
                            Y_dram[:, :], bass.IndirectOffsetOnAxis(ap=icol[0:BR, s, 1:2].bitcast(U32), axis=0),
                            ye[0:BR, s, :], None,
                            bounds_check=T * TOPK - 1, oob_is_err=False).then_inc(y_out[s], 16)
                for s in range(SLOTS):
                    pool.wait_ge(xg_in[s], turns * 16 + 16)
                    pool.sem_inc(pool_nop)
                    pool.wait_ge(y_out[s], turns * 16 + 16)
                    pool.sem_inc(pool_nop)
                pool.dma_reset(layer_range)
                last_of_layer(pool, "pool")
            pool.wait_ge(par_in, 16 * 17 * (DEPTH + 1))
            pool.wait_ge(fpar_in, 16 * 8 * (DEPTH + 1))

        @block.tensor
        def _(pe):
            mm = nc.tensor.matmul

            def group(k, n, lhsT_of, tile_s, tile_p, rhs=hT):
                mm(tile_s, lhsT_of(k), rhs[:, k, 0:LS], start=(k == 0), stop=(k == n - 1))
                return mm(tile_p, lhsT_of(k), rhs[:, k, LS:T], start=(k == 0), stop=(k == n - 1))

            def mean_square(ss_sem, ms_sem):
                pe.wait_ge(ss_sem, KC - 1)
                mm(ps[:, 0, :], mean_d, hT[:, 0, 0:LS], start=True, stop=True)
                mm(ps[:, 1, 0:LP], mean_d, hT[:, 0, LS:T], start=True, stop=True).then_inc(ms_sem, 1)

            pe.wait_ge(x_in, 48)
            for t in range(NT):
                if t >= 2:
                    pe.wait_ge(xT_in, 2 * (t - 1))
                for k in range(KC):
                    last = nc.tensor.transpose(ps[:, 4 * (t % 2) + k // 4, (k % 4) * P:(k % 4 + 1) * P],
                                               work[:, t * D + k:(t + 1) * D:KC], ident)
                last.then_inc(xT_mm, 1)
            pe.wait_ge(xT_in, 2 * NT)
            pe.wait_ge(c_ready, 1)
            with pe.Fori(0, DEPTH) as l:
                def ada(k):
                    if k < SLOTS:
                        pe.wait_ge(ada_in[k], l * 16 + 16)
                    else:
                        wait_item(pe, k)
                    w = slot(k, 6 * D)
                    for b in range(3):
                        for g in range(4):
                            col = D * g + 512 * b if b < 2 else 4 * D + 512 * g
                            last = mm(ps[32 * g:32 * g + 32, 4 + b, :], c_act[:, k, :], w[:, col:col + 512],
                                      start=(k == 0), stop=(k == KC - 1))
                    last.then_inc(w_used, 1)

                def filter_rows(o):
                    for t in range(NT):
                        n = NT * o + t
                        if t >= 2:
                            pe.wait_ge(hy_raw, n - 1)
                        mm(ps[:, t % 2, :], h2[0:FFN + 1, t * P:(t + 1) * P], fw3[:, :, o, :],
                           start=True, stop=True).then_inc(hy_f, 1)

                def filter_spectrum(o):
                    pe.wait_ge(hy_eo, NT * (o + 1))
                    for q in range(2):
                        for f in range(4):
                            for t in range(4):
                                last = mm(ps[:, 2 * q + f // 2, (f % 2) * CH:(f % 2 + 1) * CH],
                                          dft[:, t, q * LS + f * P:q * LS + (f + 1) * P], evod[:, t, q, :],
                                          start=(t == 0), stop=(t == 3))
                        last.then_inc(hy_k, 1)
                    pe.wait_ge(hy_ke, 4 * o + 1)
                    for q in range(2):
                        last = mm(ps[:, 0, q * CH:(q + 1) * CH], fwd_p[:, 0, q * LP:(q + 1) * LP], evod[:, 4, q, :],
                                  start=True, stop=True)
                    last.then_inc(hy_k, 1)
                    pe.wait_ge(hy_sum, 7 * (o + 1))
                    for g in range(2):
                        for c in range(2):
                            last = mm(ps[:, 1, 2 * g + c:2 * g + c + 1], fsum[:, g, 0, c * P:(c + 1) * P], ones[:, 0:1],
                                      start=True, stop=True)
                    last.then_inc(hy_norm, 1)

                ada(0)
                ada(1)
                pe.wait_ge(fpar_in, l * (16 * 8) + 16 * 8)
                mean_square(ss0, ms0)
                pe.wait_ge(rt0, 2)
                pe.wait_ge(const_in, 16 * 9)
                nc.tensor.transpose(ps[0:FFN, 2, 0:4], frow[:, :], ident[0:4, 0:4]).then_inc(row_mm, 1)
                mm(ps[0:FFN, 0, :], fw1[:, :], feat[:, 0:LS], start=True, stop=True)
                mm(ps[0:FFN, 1, 0:LP], fw1[:, :], feat[:, LS:T], start=True, stop=True).then_inc(hy_m1, 1)
                ada(2)
                pe.wait_ge(hy_s1, 1)
                mm(ps[0:FFN, 0, :], fw2[:, :], h1[0:FFN, 0:LS], start=True, stop=True)
                mm(ps[0:FFN, 1, 0:LP], fw2[:, :], h1[0:FFN, LS:T], start=True, stop=True).then_inc(hy_m2, 1)
                ada(3)
                pe.wait_ge(hy_s2, 1)
                filter_rows(0)
                ada(4)
                filter_spectrum(0)
                ada(5)
                pe.wait_ge(hy_ke, 4)
                pe.wait_ge(hy_rn, 1)
                filter_rows(1)
                ada(6)
                pe.wait_ge(par_in, l * (16 * 17) + 16 * 17)
                filter_spectrum(1)
                pe.wait_ge(hy_ke, 8)
                for c in range(2):
                    nc.tensor.transpose(ps[:, 3, c * ROWS:(c + 1) * ROWS], prm[:, c * P:(c + 1) * P], ident[0:ROWS, 0:ROWS])
                mm(ps[:, 3, 104:144], ones[0:1, :], brow[:, :], start=True, stop=True)
                nc.tensor.transpose(ps[:, 3, 144:272], ckv[:, 0, :], ident).then_inc(par_mm, 1)
                ada(7)
                pe.wait_ge(hy_rn, 2)
                pe.wait_ge(row_ev, 1)
                for q in range(KC):
                    last = nc.tensor.transpose(ps[:, q // 4, (q % 4) * P:(q % 4 + 1) * P], adarow[:, q:D:KC], ident)
                last.then_inc(ada_t, 1)
                pe.wait_ge(row_ev, 3)
                pe.wait_ge(par_ev, 3)
                for q in range(KC):
                    last = nc.tensor.transpose(ps[:, 2 + q // 4, (q % 4) * P:(q % 4 + 1) * P], adarow[:, D + q:2 * D:KC], ident)
                last.then_inc(ada_t, 1)
                wait_item(pe, I_CONV)
                pe.wait_ge(par_ev, 3)
                pe.wait_ge(mods_ok, 9)
                w = slot(I_CONV, KC, 512)
                for c in range(2):
                    for m in (2 + c, c):
                        for k in range(KC):
                            if c == 0 and m == 2:
                                pe.wait_ge(h0, k + 1)
                                pe.wait_ge(hc0, k + 1)
                            last = group(k, KC, lambda k: w[:, k, m * P:(m + 1) * P], ps[:, m, :], ps[:, 4 + m, 0:LP])
                        last.then_inc(cv_mm, 1)
                wait_item(pe, I_FOUR)
                w = slot(I_FOUR, KC, CH)
                pe.wait_ge(cv_glu, 2)
                for t in range(NT):
                    for k in range(KC):
                        last = mm(ps[:, t, 0:CH], hT[:, k, t * P:(t + 1) * P], w[:, k, :], start=(k == 0), stop=(k == KC - 1))
                    last.then_inc(fo_x, 1)
                pe.wait_ge(cs_in, 16)
                pe.wait_ge(fo_xe, 5)
                for c in range(2):
                    for q in range(2):
                        for t in range(4):
                            last = mm(ps[:, (5 + 2 * c + q) % 8, :], fX[:, t, c * P:(c + 1) * P],
                                      dft[:, t, q * LS:(q + 1) * LS], start=(t == 0), stop=(t == 3))
                        last.then_inc(fo_a, 1)
                for c in range(2):
                    mm(ps[:, 1 + c, 0:CH], fX[:, 4, c * P:(c + 1) * P], mix_p[:, 0, :], start=True, stop=True) \
                        .then_inc(fo_a, 1)
                pe.wait_ge(fo_ae, 6)
                for m in range(2):
                    n = 0
                    for c in range(2):
                        for q in range(2):
                            lhs = mix_c[:, c, q * CH + m * P:q * CH + (m + 1) * P]
                            mm(ps[:, 3 + m, :], lhs, fA[:, c, q, 0:LS], start=(n == 0), stop=(n == 3))
                            last = mm(ps[:, 5 + m, 0:LP], lhs, fA[:, c, q, LS:T], start=(n == 0), stop=(n == 3))
                            n += 1
                    last.then_inc(fo_b, 1)
                wait_item(pe, I_ATT)
                w = slot(I_ATT, KC, 512)
                pe.wait_ge(yc_ok, 4)
                for m in range(2):
                    for k in range(KC):
                        last = group(k, KC, lambda k: w[:, k, m * P:(m + 1) * P],
                                     ps[:, m, :], ps[:, 2 + m, 0:LP])
                    last.then_inc(at_mm, 1)
                for k in range(KC):
                    last = group(k, KC, lambda k: w[:, k, 256:384], ps[:, 4, :], ps[:, 5, 0:LP])
                last.then_inc(at_mm, 1)
                for t in range(4):
                    for k in range(KC):
                        last = mm(ps[:, 6, t * P:(t + 1) * P], hT[:, k, t * P:(t + 1) * P], w[:, k, 384:512],
                                  start=(k == 0), stop=(k == KC - 1))
                last.then_inc(at_mm, 1)
                for k in range(KC):
                    last = mm(ps[:, 7, 0:256], hT[:, k, LS:T], w[:, k, 256:512], start=(k == 0), stop=(k == KC - 1))
                last.then_inc(at_mm, 1)
                for m in range(3):
                    pe.wait_ge(at_ev, 4 if m < 2 else 6)
                    src = qraw[:, m, 0:LS] if m < 2 else kraw[:, 0:LS]
                    mm(ps[:, m, :], rot, src, start=True, stop=True).then_inc(at_rot, 1)
                pe.wait_ge(cv_tap, 2 * TAPS)
                for c in range(2):
                    mm(ps[:, 5, :], mean_c, acc[:, c, 0:LS], start=(c == 0), stop=(c == 1))
                    last = mm(ps[:, 4, 0:CONV - LS], mean_c, acc[:, c, LS:CONV], start=(c == 0), stop=(c == 1))
                last.then_inc(ln_mm, 1)
                wait_item(pe, I_HY)
                w_hy = slot(I_HY, KC, 768)

                def hyena_tile(m, k0, k1):
                    if m and k0 == 0:
                        pe.wait_ge(hy_uc, m + 1)
                    for k in range(k0, k1):
                        last = mm(ps[:, 7, :], w_hy[:, k, m * P:(m + 1) * P], hT[:, k, 0:LS],
                                  start=(k == 0), stop=(k == KC - 1))
                    if k1 == KC:
                        last.then_inc(hy_u, 1)

                pe.wait_ge(at_ev, 8)
                for m in range(6):
                    for k in range(KC):
                        last = mm(ps[:, (3, 6)[m // 4], m % 4 * P:(m % 4 + 1) * P], w_hy[:, k, m * P:(m + 1) * P],
                                  hT[:, k, LS:T], start=(k == 0), stop=(k == KC - 1))
                last.then_inc(hy_u, 1)
                pe.wait_ge(ln_sq, 2)
                for c in range(2):
                    mm(ps[:, 5, :], mean_c, csq[:, c, 0:LS], start=(c == 0), stop=(c == 1))
                    last = mm(ps[:, 4, 0:CONV - LS], mean_c, csq[:, c, LS:CONV], start=(c == 0), stop=(c == 1))
                last.then_inc(ln_var, 1)
                hyena_tile(0, 0, 4)
                pe.wait_ge(at_rope, 3)
                pe.wait_ge(hy_uc, 1)

                def score(i, h):
                    if i > 0:
                        pe.wait_ge(at_exp, 4 * (i - 1) + h + 1)
                    p0, m = HD * (h // 2), h % 2
                    if i < 4:
                        lo, hi = max(i - 1, 0), min(i + 2, 4)
                        mm(ps[:, h, 0:P], qraw[p0:p0 + HD, m, i * P:(i + 1) * P], ckT[p0:p0 + HD, :], start=True, stop=True)
                        last = mm(ps[:, h, P:P + (hi - lo) * P], qrope[p0:p0 + HD, m, i * P:(i + 1) * P],
                                  krope[p0:p0 + HD, lo * P:hi * P], start=True, stop=True)
                    else:
                        last = mm(ps[:, h, 0:P], qraw[p0:p0 + HD, m, LS:T], kraw[p0:p0 + HD, LS:T], start=True, stop=True)
                    last.then_inc(at_s, 1)

                for h in range(4):
                    score(0, h)
                hyena_tile(0, 4, KC)
                pe.wait_ge(ln_rt, 2)
                for i in range(NT):
                    lo, hi = max(i - 1, 0), min(i + 2, 4)
                    nk = 1 + hi - lo if i < 4 else 1
                    for h in range(4):
                        pe.wait_ge(at_exp, 4 * i + h + 1)
                        if h == 1 and i > 0:
                            pe.wait_ge(yd_ok, i)
                        if h >= 2:
                            pe.wait_ge(at_te, 4 * i + h - 1)
                        for t in range(nk):
                            last = nc.tensor.transpose(ps[:, 4 + h % 2, t * P:(t + 1) * P], prob[:, h, t * P:(t + 1) * P], ident)
                        last.then_inc(at_t, 1)
                        if i + 1 < NT:
                            score(i + 1, h)
                    hyena_tile(i + 1, 0, 4)
                    for h in range(4):
                        kv = h // 2
                        pe.wait_ge(at_te, 4 * i + h + 1)
                        for t in range(nk):
                            if i == 4:
                                v = vtok[:, 4, kv * HD:(kv + 1) * HD]
                            elif t == 0:
                                v = ckv[:, 1, kv * HD:(kv + 1) * HD]
                            else:
                                v = vtok[:, lo + t - 1, kv * HD:(kv + 1) * HD]
                            last = mm(ps[:, 6, h * HD:(h + 1) * HD], probT[:, h, t * P:(t + 1) * P], v,
                                      start=(t == 0), stop=(t == nk - 1))
                    last.then_inc(at_pv, 1)
                    hyena_tile(i + 1, 4, KC)
                    pe.wait_ge(at_o, i + 1)
                    for q in range(2):
                        last = nc.tensor.transpose(ps[:, 5, q * P:(q + 1) * P], otok[:, q * P:(q + 1) * P], ident)
                    last.then_inc(at_ot, 1)
                pe.wait_ge(yd_ok, NT)
                pe.wait_ge(hy_uc, 6)
                pe.wait_ge(f_in, 32)
                for o in range(2):
                    for c in range(2):
                        if o:
                            pe.wait_ge(hy_zn, c + 1)
                        for t in range(NT):
                            bank, col = (c, t * P) if t < 4 else (2 + c, 0)
                            last = nc.tensor.transpose(ps[:, bank, col:col + P], u[c][:, t * P:(t + 1) * P], ident)
                        last.then_inc(hy_zt, 1)
                    pe.wait_ge(hy_z, 2 * (o + 1))
                    for q in range(2):
                        last = mm(ps[:, 4, q * CH:(q + 1) * CH], fwd_p[:, 0, q * LP:(q + 1) * LP], zs[:, 4, :],
                                  start=True, stop=True)
                    last.then_inc(hy_fz, 1)
                    for f in range(4):
                        for q in range(2):
                            for t in range(4):
                                last = mm(ps[:, f, q * CH:(q + 1) * CH],
                                          dft[:, t, q * LS + f * P:q * LS + (f + 1) * P], zs[:, t, :],
                                          start=(t == 0), stop=(t == 3))
                        last.then_inc(hy_fz, 1)
                    for c in range(2):
                        for f in range(4):
                            if c == 0:
                                pe.wait_ge(hy_y, 5 * o + f + 2)
                            for q in range(2):
                                mm(ps[:, 6 + c, :], yspec[:, q, f, c * P:(c + 1) * P], inv_s[:, 4 * q + f, :],
                                   start=(q + f == 0), stop=(q == 1 and f == 3))
                        for q in range(2):
                            last = mm(ps[:, 4 + c, 0:P], yspec[:, q, 4, c * P:(c + 1) * P], inv_p[:, q, :],
                                      start=(q == 0), stop=(q == 1))
                        last.then_inc(hy_inv, 1)
                wait_item(pe, I_OUT)
                wait_item(pe, I_OUT + 1)
                pe.wait_ge(hy_zn, 4)
                pe.wait_ge(ya_ok, 4)
                w2 = [slot(I_OUT + i, 4, D) for i in range(2)]
                for m in range(KC):
                    if m >= 4:
                        pe.wait_ge(x_mid, 2 * (m - 3))
                    for k in range(KC):
                        last = group(k, KC, lambda k: w2[k // 4][:, k % 4, m:D:KC], ps[:, m % 4, :], ps[:, 4 + m % 4, 0:LP], yT)
                    last.then_inc(wo_mm, 1)
                pe.wait_ge(x_mid, 16)
                mean_square(ss1, ms1)
                for k in range(KC):
                    pe.wait_ge(h1s, k + 1)
                    pe.wait_ge(hc1, k + 1)
                    last = group(k, KC, lambda k: wr[:, k, :], ps[0:36, 2, :], ps[0:36, 3, 0:LP])
                last.then_inc(ro_mm, 1)

                def rows_of_h(t):
                    if t >= 2:
                        pe.wait_ge(hs_ev, 2 * (t - 1))
                    for k in range(KC):
                        last = nc.tensor.transpose(ps[:, 4 + 2 * (t % 2) + k // 4, (k % 4) * P:(k % 4 + 1) * P],
                                                   hT[:, k, t * P:(t + 1) * P], ident)
                    last.then_inc(hs_mm, 1)

                rows_of_h(0)
                pe.wait_ge(ro_lt, 2)
                for t in range(NT):
                    last = nc.tensor.transpose(ps[:, 0, t * 36:(t + 1) * 36], lgT[0:36, t * P:(t + 1) * P], ident[0:36, 0:36])
                last.then_inc(ro_lg, 1)
                rows_of_h(1)
                rows_of_h(2)
                pe.wait_ge(ro_oh, 1)
                mm(ps[:, 3, 0:(NT + 1) * NE], tri, both.rearrange("p t e -> p (t e)"), start=True, stop=False)
                mm(ps[:, 3, 0:(NT + 1) * NE], ones, before.rearrange("p t e -> p (t e)"), start=False, stop=True) \
                    .then_inc(ro_rank, 1)
                rows_of_h(3)
                rows_of_h(4)
                pe.wait_ge(ro_1h, 1)
                for n in range(2 * NT):
                    last = mm(ps[0:BR, 2, 0:NBLK + SLOTS], ohs[:, n, :], ohb[:, n, :], start=(n == 0), stop=(n == 2 * NT - 1))
                last.then_inc(ro_tm, 1)
                def rows_in(s):
                    for k in range(KC):
                        last = nc.tensor.transpose(ps[:, k // 4, (k % 4) * P:(k % 4 + 1) * P],
                                                   xg[:, s, k * P:(k + 1) * P], ident)
                    return last

                for s in range(SLOTS):
                    pe.sem_inc(y_mm[s])
                pe.wait_ge(ro_tab, 1)
                turns = pe.value_load(nturn[0:1, 0:1], min_val=1, max_val=NBLK // 2)
                pe.wait_ge(xg_in[0], 16)
                rows_in(0).then_inc(xt_mm[0], 1)
                with pe.Fori(0, turns) as j:
                    for s in range(SLOTS):
                        w = slot(s, 3, KC, FE)
                        wd = slot(s, 3, 2, D)
                        pe.wait_ge(xe_ok[s], j * 2 + 2)
                        pe.wait_ge(wg_full[s], j * 32 + 32)
                        for q, done in ((0, g_mm[s]), (1, u_mm[s])):
                            for m in range(2):
                                for k in range(KC):
                                    last = mm(ps[:, 2 + q, m * BR:(m + 1) * BR], w[:, q, k, m:FE:2], xe[:, s, k, :],
                                              start=(k == 0), stop=(k == KC - 1))
                            last.then_inc(done, 1)
                        if s == 0:
                            pe.wait_ge(xg_in[1], j * 16 + 16)
                        else:
                            pe.wait_ge(xg_in[0], j * 16 + 32)
                        rows_in(1 - s).then_inc(xt_mm[1 - s], 1)
                        pe.wait_ge(he_ok[s], j + 1)
                        pe.wait_ge(wd_full[s], j * 16 + 16)
                        other = j + 1 if s == 0 else j + 2
                        pe.wait_ge(ye_a[1 - s], other)
                        pe.wait_ge(ye_d[1 - s], other)
                        for n in range(2):
                            for k in range(2):
                                last = mm(ps[0:BR, 6 + n, :], he[:, s, k, :], wd[:, 2, k, n * 512:(n + 1) * 512],
                                          start=(k == 0), stop=(k == 1))
                            last.then_inc(y_mm[s], 1)
                pe.wait_ge(ye_a[1], turns + 1)
                pe.wait_ge(ye_d[1], turns + 1)
                for t in range(NT):
                    pe.wait_ge(yc_sum, t + 1)
                    if t >= 2:
                        pe.wait_ge(x_new, KC * (t - 1))
                    for k in range(KC):
                        last = nc.tensor.transpose(ps[:, 2 * (t % 2) + k // 4, (k % 4) * P:(k % 4 + 1) * P],
                                                   ysum[:, t % 2, k:D:KC], ident)
                    last.then_inc(yc_mm, 1)
                last_of_layer(pe, "pe")
            mean_square(ss0, ms0)
            for t in range(NT):
                if t >= 2:
                    pe.wait_ge(hs_ev, 2 * (t - 1))
                for k in range(KC):
                    if t == 0:
                        pe.wait_ge(h0, k + 1)
                    last = nc.tensor.transpose(ps[:, 2 + 2 * (t % 2) + k // 4, (k % 4) * P:(k % 4 + 1) * P],
                                               hT[:, k, t * P:(t + 1) * P], ident)
                last.then_inc(hs_mm, 1)

        @block.scalar
        def _(act):
            A = nc.scalar.activation

            def squares(ready, step_, base, sq_sem):
                for k in range(KC):
                    act.wait_ge(ready, base + step_ * k)
                    A(hT[:, k, :], xT[:, k, :], ACT.Square).then_inc(sq_sem, 1)

            def root(ms_sem, rt_sem):
                act.wait_ge(ms_sem, 1)
                A(rms[:, 0:LS], ps[:, 0, :], ACT.Sqrt, bias=epsc[:, :]).then_inc(rt_sem, 1)
                A(rms[:, LS:T], ps[:, 1, 0:LP], ACT.Sqrt, bias=epsc[:, :]).then_inc(rt_sem, 1)

            def modulate(n, xn_sem, h_sem):
                for k in range(KC):
                    act.wait_ge(xn_sem, k + 1)
                    A(hT[:, k, 0:LS], hT[:, k, 0:LS], ACT.Identity, scale=gain[:, n, k, 0:1],
                      bias=mods[:, 3 * n, k, 0:1]).then_inc(h_sem, 1)

            for t in range(NT):
                act.wait_ge(xT_mm, t + 1)
                for q in range(2):
                    A(xT[:, 4 * q:4 * q + 4, t * P:(t + 1) * P],
                      ps[:, 4 * (t % 2) + q, :].rearrange("p (k t) -> p k t", k=4), ACT.Copy).then_inc(xT_in, 1)
            act.wait_ge(cond_in, 16 * 3)
            act.wait_ge(set_up, 1)
            for g in range(2):
                last = A(c_act[:, :, g], c_raw[:, g, :], ACT.Silu)
            last.then_inc(c_ready, 1)
            act.wait_ge(xT_in, 2 * NT)
            with act.Fori(0, DEPTH):
                squares(xT_in, 0, 2 * NT, sq0)
                root(ms0, rt0)
                act.wait_ge(hy_a1, 1)
                A(h1[0:FFN, :], fa_[0:FFN, :], ACT.Sin).then_inc(hy_s1, 1)
                act.wait_ge(hy_a2, 1)
                A(h2[0:FFN, :], fa_[0:FFN, :], ACT.Sin).then_inc(hy_s2, 1)
                for o in range(2):
                    for t in range(NT):
                        n = NT * o + t
                        act.wait_ge(hy_eo, n + 1)
                        if n >= 2:
                            act.wait_ge(hy_sum, 7 * ((n - 2) // NT) + (n - 2) % NT + 1)
                        A(fabs[:, t % 2, :, :], ftime[:, t % 2, :, :], ACT.Abs).then_inc(hy_abs, 1)
                    if o:
                        act.wait_ge(k_out, 16)
                    for q in range(2):
                        act.wait_ge(hy_k, 3 * o + q + 1)
                        A(knew[:, q, 0:4, :], ps[:, 2 * q:2 * q + 2, :].rearrange("p b (f c) -> p (b f) c", f=2), ACT.Copy) \
                            .then_inc(hy_ke, 1)
                    act.wait_ge(hy_k, 3 * o + 3)
                    for q in range(2):
                        A(knew[:, q, 4, :], ps[:, 0, q * CH:(q + 1) * CH], ACT.Copy).then_inc(hy_ke, 1)
                    act.wait_ge(hy_ke, 4 * (o + 1))
                    act.dma_start(K_dram[o], knew.rearrange("p q t c -> p (q t c)")).then_inc(k_out, 16)
                act.wait_ge(w_used, KC)
                A(adarow[:, 0:D], ps[:, 4:6, :].rearrange("p b c -> p (b c)"), ACT.Copy).then_inc(row_ev, 1)
                act.wait_ge(mods_ok, 3)
                modulate(0, xn0, h0)
                for c in range(2):
                    act.wait_ge(cv_mm, 2 * c + 1)
                    for (a, b), bank in ((GRP[0], 2 + c), (GRP[1], 6 + c)):
                        last = A(sig[:, c, a:b], ps[:, bank, 0:b - a], ACT.Sigmoid)
                    last.then_inc(cv_sig, 1)
                for t in range(NT):
                    act.wait_ge(fo_x, t + 1)
                    A(fX[:, t, :], ps[:, t, 0:CH], ACT.Copy).then_inc(fo_xe, 1)
                for c in range(2):
                    for q in range(2):
                        act.wait_ge(fo_a, 2 * c + q + 1)
                        A(fA[:, c, q, 0:LS], ps[:, (5 + 2 * c + q) % 8, :], ACT.Copy).then_inc(fo_ae, 1)
                for c in range(2):
                    act.wait_ge(fo_a, 5 + c)
                    A(fA[:, c, :, LS:T], ps[:, 1 + c, 0:CH].rearrange("p (q t) -> p q t", q=2), ACT.Copy) \
                        .then_inc(fo_ae, 1)
                act.wait_ge(k_out, 32)
                for m in range(2):
                    act.wait_ge(fo_b, m + 1)
                    A(yT[:, 4 + m, 0:LS], ps[:, 3 + m, :], ACT.Copy).then_inc(yc_ok, 1)
                    A(yT[:, 4 + m, LS:T], ps[:, 5 + m, 0:LP], ACT.Copy).then_inc(yc_ok, 1)
                for m in range(2):
                    act.wait_ge(at_mm, m + 1)
                    for (a, b), bank in ((GRP[0], m), (GRP[1], 2 + m)):
                        for h in range(2):
                            last = A(qraw[m * HD:(m + 1) * HD, h, a:b], ps[h * HD:(h + 1) * HD, bank, 0:b - a], ACT.Copy)
                        last.then_inc(at_ev, 1)
                act.wait_ge(at_mm, 3)
                A(kraw[:, 0:LS], ps[:, 4, :], ACT.Copy).then_inc(at_ev, 1)
                A(kraw[:, LS:T], ps[:, 5, 0:LP], ACT.Copy).then_inc(at_ev, 1)
                act.wait_ge(at_mm, 4)
                A(vtok[:, 0:4, :], ps[:, 6, :].rearrange("p (t c) -> p t c", t=4), ACT.Copy).then_inc(at_ev, 1)
                act.wait_ge(at_mm, 5)
                A(vtok[:, 4, :], ps[:, 7, P:2 * P], ACT.Copy)
                A(kvo[:, :, :], ps[:, 7, 0:256].rearrange("p (q c) -> p q c", q=2), ACT.Copy).then_inc(at_ev, 1)
                act.wait_ge(ln_ctr, 2)
                for c in range(2):
                    A(csq[:, c, :], acc[:, c, :], ACT.Square).then_inc(ln_sq, 1)
                act.wait_ge(hy_u, 1)
                for m in range(6):
                    last = A(u[m][:, LS:T], ps[:, (3, 6)[m // 4], m % 4 * P:(m % 4 + 1) * P], ACT.Identity,
                             scale=tap(m, 1), bias=tap(m, 3))
                last.then_inc(hy_u1, 1)
                act.wait_ge(ln_var, 1)
                A(crs[:, 0:LS], ps[:, 5, :], ACT.Sqrt, bias=epsc[:, :]).then_inc(ln_rt, 1)
                A(crs[:, LS:CONV], ps[:, 4, 0:CONV - LS], ACT.Sqrt, bias=epsc[:, :]).then_inc(ln_rt, 1)
                for c in range(2):
                    act.wait_ge(ln_out, c + 1)
                    for (a, b), o in ((GRP[0], 0), (GRP[1], PAD)):
                        A(yT[:, c, a:b], acc[:, c, a + o:b + o], ACT.Silu, scale=prmT[:, c, R_LNG:R_LNG + 1],
                          bias=prmT[:, c, R_LNB:R_LNB + 1]).then_inc(ya_ok, 1)
                def exponentials(i):
                    nk = (3, 4, 4, 3, 1)[i]
                    act.wait_ge(at_max, i + 1)
                    A(ast[:, i % 2, 3, :], ast[:, i % 2, 2, :], ACT.Exp)
                    for h in range(4):
                        if i > 0:
                            act.wait_ge(at_t, 4 * (i - 1) + h + 1)
                        A(prob[:, h, 0:nk * P], ps[:, h, 0:nk * P], ACT.Exp, bias=ast[:, i % 2, 1, h:h + 1], scale=HD ** -0.5,
                          accum_out=ast[:, i % 2, 4, h:h + 1]).then_inc(at_exp, 1)

                def middle_tap(m):
                    act.wait_ge(hy_u, m + 2)
                    A(u[m][:, 0:LS], ps[:, 7, :], ACT.Identity, scale=tap(m, 1), bias=tap(m, 3)).then_inc(hy_u1, 1)

                middle_tap(0)
                act.wait_ge(ya_ok, 4)
                exponentials(0)
                for i in range(NT):
                    nk = (3, 4, 4, 3, 1)[i]
                    for h in range(4):
                        act.wait_ge(at_t, 4 * i + h + 1)
                        if i > 0 and h == 0:
                            act.wait_ge(at_pv, i)
                        A(probT[:, h, 0:nk * P], ps[:, 4 + h % 2, 0:nk * P], ACT.Copy).then_inc(at_te, 1)
                    if i + 1 < NT:
                        exponentials(i + 1)
                    middle_tap(i + 1)
                    act.wait_ge(at_ot, i + 1)
                    A(yT[:, 6:8, i * P:(i + 1) * P], ps[:, 5, 0:2 * P].rearrange("p (q t) -> p q t", q=2), ACT.Copy) \
                        .then_inc(yd_ok, 1)
                for o in range(2):
                    for c in range(2):
                        act.wait_ge(hy_zt, 2 * o + c + 1)
                        A(zs[:, 0:4, c * P:(c + 1) * P], ps[:, c, :].rearrange("p (t c) -> p t c", t=4), ACT.Copy)
                        A(zs[:, 4, c * P:(c + 1) * P], ps[:, 2 + c, 0:P], ACT.Copy).then_inc(hy_z, 1)
                squares(x_mid, 2, 2, sq1)
                root(ms1, rt1)
                modulate(1, xn1, h1s)
                act.wait_ge(ro_sub, 1)
                A(gexp[:, :, :], gt[:, :, :], ACT.Exp).then_inc(ro_exp, 1)
                for t in range(NT):
                    act.wait_ge(hs_mm, t + 1)
                    if t >= 2:
                        act.wait_ge(hs_st[t % 2], 16 * (t // 2))
                    for q in range(2):
                        A(htok[:, t % 2, 512 * q:512 * q + 512], ps[:, 4 + 2 * (t % 2) + q, :], ACT.Copy).then_inc(hs_ev, 1)
                act.wait_ge(ro_sub2, 1)
                A(emx[:, :], ediff[:, :], ACT.Exp).then_inc(ro_exp2, 1)
                for s in range(SLOTS):
                    act.sem_inc(ye_a[s])
                act.wait_ge(ro_tab, 1)
                turns = act.value_load(nturn[0:1, 0:1], min_val=1, max_val=NBLK // 2)
                for q in range(2):
                    act.wait_ge(hs_st[q], 16 * ((NT + 1 - q) // 2))

                def rows_out(s):
                    for q in range(2):
                        A(xe[:, s, 4 * q:4 * q + 4, :], ps[:, q, :].rearrange("p (k t) -> p k t", k=4)[:, :, 0:BR], ACT.Copy) \
                            .then_inc(xe_ok[s], 1)

                act.wait_ge(xt_mm[0], 1)
                rows_out(0)
                with act.Fori(0, turns) as j:
                    for s in range(SLOTS):
                        act.wait_ge(g_mm[s], j + 1)
                        A(sg[:, s, :], ps[:, 2, 0:2 * BR], ACT.Silu).then_inc(sg_ok[s], 1)
                        act.wait_ge(xt_mm[1 - s], j + 1 if s == 0 else j + 2)
                        rows_out(1 - s)
                        act.wait_ge(y_mm[s], j * 2 + 2)
                        act.wait_ge(y_out[s], j * 16 + 16)
                        A(ye[0:BR, s, 0:512], ps[0:BR, 6, :], ACT.Copy).then_inc(ye_a[s], 1)
                for s in range(SLOTS):
                    act.wait_ge(y_out[s], turns * 16 + 16)
                for t in range(NT):
                    act.wait_ge(yc_in[t % 2], 16 * (t // 2 + 1))
                    if t >= 2:
                        act.wait_ge(yc_mm, t - 1)
                    A(ysum[:, t % 2, :], ycomb[:, t % 2, 0, :], ACT.Copy, scale=wgt[0][:, t:t + 1]).then_inc(yc_first, 1)
                last_of_layer(act, "act")
            squares(xT_in, 0, 2 * NT, sq0)
            root(ms0, rt0)
            for k in range(KC):
                act.wait_ge(xn0, k + 1)
                A(hT[:, k, :], hT[:, k, :], ACT.Copy, scale=nf[:, k:k + 1]).then_inc(h0, 1)
            for t in range(NT):
                act.wait_ge(hs_mm, t + 1)
                for q in range(2):
                    A(work[:, t * D:(t + 1) * D].rearrange("p (c k) -> p k c", k=KC)[:, 4 * q:4 * q + 4, :],
                      ps[:, 2 + 2 * (t % 2) + q, :].rearrange("p (k c) -> p k c", k=4), ACT.Copy).then_inc(hs_ev, 1)

        @block.vector
        def _(dve):
            V = nc.vector
            chain = [0]

            def step(ins):
                chain[0] += 1
                ins.then_inc(dchain, 1)
                dve.wait_ge(dchain, chain[0])

            def bc(ap, n):
                return ap.rearrange("p (a b) -> p a b", b=1).to_broadcast([P, ap.shape[1], n])

            def row(ap, n):
                return ap.rearrange("p (b a) -> p b a", b=1).to_broadcast([P, n, ap.shape[1]])

            def add_square(k, sq_sem, ss_sem):
                dve.wait_ge(sq_sem, k + 1)
                if k >= 2:
                    dve.wait_ge(ss_sem, k - 1)
                V.tensor_tensor(hT[:, 0, :], hT[:, 0, :], hT[:, k, :], ALU.add).then_inc(ss_sem, 1)

            def normalise(rt_sem, xn_sem):
                dve.wait_ge(rt_sem, 2)
                step(V.reciprocal(rinv[:, :], rms[:, :]))
                for k in range(KC):
                    V.tensor_tensor(hT[:, k, :], xT[:, k, :], rinv[:, :], ALU.mult).then_inc(xn_sem, 1)

            def residual(t):
                dve.wait_ge(yc_mm, t + 1)
                for k in range(KC):
                    x = xT[:, k, t * P:(t + 1) * P]
                    g = 0 if t < 4 else 1
                    V.scalar_tensor_tensor(out=x, in0=ps[:, 2 * (t % 2) + k // 4, (k % 4) * P:(k % 4 + 1) * P],
                                           scalar=mods[:, 5, k, g:g + 1], in1=x, op0=ALU.mult, op1=ALU.add) \
                        .then_inc(x_new, 1)

            with dve.Fori(0, DEPTH):
                chain[0] = 0
                for k in range(1, KC):
                    add_square(k, sq0, ss0)

                def sine_argument(done):
                    a, k = fa_[0:FFN, :], fk_[0:FFN, :]
                    step(V.tensor_scalar(k, a, 1 / (2 * np.pi), MAGIC, ALU.mult, ALU.add))
                    step(V.tensor_scalar(k, k, -MAGIC, None, ALU.add))
                    step(V.scalar_tensor_tensor(out=a, in0=k, scalar=-TWO_PI_HI, in1=a, op0=ALU.mult, op1=ALU.add))
                    step(V.scalar_tensor_tensor(out=a, in0=k, scalar=-float(TWO_PI_LO), in1=a, op0=ALU.mult, op1=ALU.add))
                    V.tensor_scalar(a, a, 3.1415925, -3.1415925, ALU.min, ALU.max).then_inc(done, 1)

                dve.wait_ge(row_mm, 1)
                V.memset(h2[FFN:FFN + 1, :], 1.0)
                step(V.tensor_copy(frowT[:, :], ps[0:FFN, 2, 0:4]))
                for n, (mm_sem, done, fb) in enumerate(((hy_m1, hy_a1, 0), (hy_m2, hy_a2, 2))):
                    dve.wait_ge(mm_sem, 1)
                    for (a, b), bank in ((GRP[0], 0), (GRP[1], 1)):
                        last = V.tensor_scalar(fa_[0:FFN, a:b], ps[0:FFN, bank, 0:b - a], frowT[:, fb:fb + 1],
                                               frowT[:, fb + 1:fb + 2], ALU.add, ALU.mult)
                    step(last)
                    sine_argument(done)
                for o in range(2):
                    for t in range(NT):
                        n = NT * o + t
                        dve.wait_ge(hy_f, n + 1)
                        if n == 0:
                            dve.wait_ge(hy_s2, 1)
                        if n >= 2:
                            dve.wait_ge(hy_abs, n - 1)
                        f = ftime[:, t % 2, :, :]
                        V.tensor_tensor(f, ps[:, t % 2, :].rearrange("p (q c) -> p q c", q=2), row(win[:, t, :], 2),
                                        ALU.mult).then_inc(hy_raw, 1)
                        dve.wait_ge(hy_raw, n + 1)
                        V.tensor_tensor(evod[:, t, 1, :], f[:, 0, :], f[:, 1, :], ALU.subtract)
                        if t in (0, 4):
                            step(V.tensor_tensor(evod[:, t, 0, :], f[:, 0, :], f[:, 1, :], ALU.add))
                            step(V.tensor_copy(f[0:1, 0, :], evod[0:1, t, 0, :]))
                            V.memset(f[0:1, 1, :], 0.0).then_inc(hy_eo, 1)
                        else:
                            V.tensor_tensor(evod[:, t, 0, :], f[:, 0, :], f[:, 1, :], ALU.add).then_inc(hy_eo, 1)
                    if o == 0:
                        normalise(rt0, xn0)
                    dve.wait_ge(hy_norm, o + 1)
                    step(V.tensor_scalar(rnorm[:, o, :], ps[:, 1, 0:4], EPS, None, ALU.add))
                    V.reciprocal(rnorm[:, o, :], rnorm[:, o, :]).then_inc(hy_rn, 1)
                dve.wait_ge(par_mm, 1)
                V.tensor_copy(prmT[:, :, :], ps[:, 3, 0:2 * ROWS].rearrange("p (c r) -> p c r", c=2)).then_inc(par_ev, 1)
                V.tensor_copy(bcast[:, :], ps[:, 3, 104:144]).then_inc(par_ev, 1)
                V.tensor_copy(ckT[:, :], ps[:, 3, 144:272]).then_inc(par_ev, 1)

                def add_bias(part, p0, p1, bank, r):
                    src = ps[p0:p1, bank:bank + 2, :].rearrange("p b (q r) -> p (b q) r", r=P)[:, :, r:r + 2]
                    bias = ada_b[p0:p1, part, :].rearrange("p (k a) -> p k a", a=1).to_broadcast([p1 - p0, KC, 2])
                    V.tensor_tensor(mods[p0:p1, part, :, :], src, bias, ALU.add).then_inc(mods_ok, 1)

                def norm_gain(n, ready):
                    dve.wait_ge(mods_ok, ready)
                    V.scalar_tensor_tensor(out=gain[:, n, :, :], in0=mods[:, 3 * n + 1, :, :], scalar=1.0,
                                           in1=bc(norms[:, n, :], 2), op0=ALU.add, op1=ALU.mult).then_inc(mods_ok, 1)

                dve.wait_ge(row_ev, 1)
                for i in range(2):
                    V.tensor_copy(adarow[:, D + 512 * i:D + 512 * (i + 1)], ps[:, 6, :]).then_inc(row_ev, 1)
                dve.wait_ge(ada_t, 1)
                add_bias(0, 0, P, 0, 0)
                add_bias(1, 0, P, 0, 32)
                norm_gain(0, 2)
                add_bias(2, 0, P, 0, 64)
                add_bias(3, 0, P, 0, 96)
                dve.wait_ge(ada_t, 2)
                for part in (4, 5):
                    for i in range(2):
                        add_bias(part, 64 * i, 64 * i + 64, 2, 32 * (2 * (part - 4) + i))
                norm_gain(1, 9)
                dve.wait_ge(xn0, KC)
                for c in range(2):
                    V.memset(glu[:, c, 0:PAD], 0.0)
                    V.memset(glu[:, c, PAD + LS:2 * PAD + LS], 0.0)
                    last = V.memset(glu[:, c, GW - PAD:GW], 0.0)
                step(last)
                for c in range(2):
                    dve.wait_ge(cv_sig, c + 1)
                    dve.wait_ge(cv_mm, 2 * c + 2)
                    V.tensor_tensor(glu[:, c, PAD:PAD + LS], ps[:, c, :], sig[:, c, 0:LS], ALU.mult)
                    V.tensor_tensor(glu[:, c, 2 * PAD + LS:2 * PAD + T], ps[:, 4 + c, 0:LP], sig[:, c, LS:T],
                                    ALU.mult).then_inc(cv_glu, 1)
                dve.wait_ge(cv_glu, 2)
                for j in range(TAPS):
                    for c in range(2):
                        if j == 0:
                            V.tensor_scalar(acc[:, c, :], glu[:, c, j:j + CONV], prmT[:, c, j:j + 1],
                                            prmT[:, c, R_DWB:R_DWB + 1], ALU.mult, ALU.add).then_inc(cv_tap, 1)
                        else:
                            dve.wait_ge(cv_tap, 2 * j + c - 1)
                            V.scalar_tensor_tensor(out=acc[:, c, :], in0=glu[:, c, j:j + CONV], scalar=prmT[:, c, j:j + 1],
                                                   in1=acc[:, c, :], op0=ALU.mult, op1=ALU.add).then_inc(cv_tap, 1)
                for m in range(3):
                    src, dst = (qraw[:, m, 0:LS], qrope[:, m, :]) if m < 2 else (kraw[:, 0:LS], krope[:, :])
                    dve.wait_ge(at_rot, m + 1)
                    V.tensor_tensor(ps[:, m, :], ps[:, m, :], rope[:, 1, :], ALU.mult)
                    step(V.tensor_tensor(dst, src, rope[:, 0, :], ALU.mult))
                    V.tensor_tensor(dst, dst, ps[:, m, :], ALU.add).then_inc(at_rope, 1)
                def outer_tap(m, which, src, dst):
                    n = src.shape[-1]
                    a, b = (1, 0) if which == 0 else (0, 1)
                    return V.scalar_tensor_tensor(out=dst[:, a:n - b], in0=src[:, b:n - a], scalar=tap(m, which),
                                                  in1=dst[:, a:n - b], op0=ALU.mult, op1=ALU.add)

                def outer_taps(m):
                    dve.wait_ge(hy_u1, m + 2)
                    step(outer_tap(m, 0, ps[:, 7, :], u[m][:, 0:LS]))
                    outer_tap(m, 2, ps[:, 7, :], u[m][:, 0:LS]).then_inc(hy_uc, 1)

                dve.wait_ge(ln_mm, 1)
                for c in range(2):
                    V.tensor_tensor(acc[:, c, 0:LS], acc[:, c, 0:LS], ps[:, 5, :], ALU.subtract)
                    V.tensor_tensor(acc[:, c, LS:CONV], acc[:, c, LS:CONV], ps[:, 4, 0:CONV - LS],
                                    ALU.subtract).then_inc(ln_ctr, 1)
                dve.wait_ge(hy_u1, 1)
                for which in (0, 2):
                    for m in range(6):
                        last = outer_tap(m, which, ps[:, (3, 6)[m // 4], m % 4 * P:(m % 4 + 1) * P], u[m][:, LS:T])
                    if which == 0:
                        step(last)
                last.then_inc(hy_uc, 1)
                dve.wait_ge(ln_rt, 2)
                step(V.reciprocal(crn[:, :], crs[:, :]))
                for c in range(2):
                    V.tensor_tensor(acc[:, c, :], acc[:, c, :], crn[:, :], ALU.mult).then_inc(ln_out, 1)
                sink = bcast[:, 0:4]

                def divide(i):
                    dve.wait_ge(at_exp, 4 * i + 4)
                    step(V.tensor_tensor(ast[:, i % 2, 6, :], ast[:, i % 2, 3, :], ast[:, i % 2, 4, :], ALU.add))
                    step(V.reciprocal(ast[:, i % 2, 7, :], ast[:, i % 2, 6, :]))
                    dve.wait_ge(at_pv, i + 1)
                    V.tensor_tensor(otok.rearrange("p (h c) -> p h c", h=4), ps[:, 6, 0:256].rearrange("p (h c) -> p h c", h=4),
                                    bc(ast[:, i % 2, 7, :], HD), ALU.mult).then_inc(at_o, 1)

                def maximum(i):
                    nk = (3, 4, 4, 3, 1)[i]
                    dve.wait_ge(at_s, 4 * (i + 1))
                    if 1 <= i < 4:
                        step(V.tensor_tensor(ps[:, 0:4, P:2 * P], ps[:, 0:4, P:2 * P], row(mask_l, 4), ALU.add))
                    if i < 3:
                        step(V.tensor_tensor(ps[:, 0:4, (nk - 1) * P:nk * P], ps[:, 0:4, (nk - 1) * P:nk * P],
                                             row(mask_r, 4), ALU.add))
                    step(V.tensor_reduce(ast[:, i % 2, 0, :], ps[:, 0:4, 0:nk * P], AX.X, ALU.max))
                    step(V.scalar_tensor_tensor(out=ast[:, i % 2, 5, :], in0=ast[:, i % 2, 0, :], scalar=HD ** -0.5, in1=sink,
                                                op0=ALU.mult, op1=ALU.max))
                    V.tensor_scalar(ast[:, i % 2, 1, :], ast[:, i % 2, 5, :], -1.0, None, ALU.mult)
                    V.tensor_tensor(ast[:, i % 2, 2, :], sink, ast[:, i % 2, 5, :], ALU.subtract).then_inc(at_max, 1)

                maximum(0)
                outer_taps(0)
                for i in range(NT):
                    if i + 1 < NT:
                        maximum(i + 1)
                    divide(i)
                    outer_taps(i + 1)
                dve.wait_ge(yd_ok, NT)
                for o in range(2):
                    for c in range(2):
                        dve.wait_ge(hy_zt, 2 * o + c + 1)
                        V.tensor_scalar(u[c], u[c], prmT[:, c, R_HD + o:R_HD + o + 1], None, ALU.mult) \
                            .then_inc(hy_dz, 1)
                    dve.wait_ge(k_in, 16 * (o + 1))
                    for n, f in enumerate((4, 0, 1, 2, 3)):
                        dve.wait_ge(hy_fz, 5 * o + n + 1)
                        z = ps[:, f, :].rearrange("p (q c) -> p q c", q=2)
                        by_r, by_i = ctmp[:, n % 2, 0, :, :], ctmp[:, n % 2, 1, :, :]
                        V.tensor_tensor(by_r, z, row(kspec[:, 0, f, :], 2), ALU.mult)
                        step(V.tensor_tensor(by_i, z, row(kspec[:, 1, f, :], 2), ALU.mult))
                        V.tensor_tensor(yspec[:, 0, f, :], by_r[:, 0, :], by_i[:, 1, :], ALU.subtract)
                        V.tensor_tensor(yspec[:, 1, f, :], by_r[:, 1, :], by_i[:, 0, :], ALU.add).then_inc(hy_y, 1)
                    dve.wait_ge(hy_dz, 2 * (o + 1))
                    dve.wait_ge(hy_rn, o + 1)
                    for c in range(2):
                        dve.wait_ge(hy_inv, 2 * o + c + 1)
                        for g, (a, b) in enumerate(GRP):
                            src = ps[:, 6 + c, :] if g == 0 else ps[:, 4 + c, 0:P]
                            last = V.scalar_tensor_tensor(out=u[c][:, a:b], in0=src, scalar=rnorm[:, o, 2 * g + c:2 * g + c + 1],
                                                          in1=u[c][:, a:b], op0=ALU.mult, op1=ALU.add)
                        step(last)
                        V.tensor_tensor(u[c], u[c], u[2 + 2 * o + c], ALU.mult).then_inc(hy_zn, 1)
                for m in range(KC):
                    if m >= 2:
                        add_square(m - 1, sq1, ss1)
                    dve.wait_ge(wo_mm, m + 1)
                    for g, (a, b) in enumerate(GRP):
                        bank = m % 4 + 4 * g
                        V.scalar_tensor_tensor(out=xT[:, m, a:b], in0=ps[:, bank, 0:b - a], scalar=mods[:, 2, m, g:g + 1],
                                               in1=xT[:, m, a:b], op0=ALU.mult, op1=ALU.add).then_inc(x_mid, 1)
                add_square(KC - 1, sq1, ss1)
                normalise(rt1, xn1)
                V.memset(both[:, NT, :], 0.0)
                V.memset(before[:, 0, :], 0.0)
                dve.wait_ge(ro_mm, 1)
                V.tensor_copy(lgT[0:36, 0:LS], ps[0:36, 2, :]).then_inc(ro_lt, 1)
                V.tensor_copy(lgT[0:36, LS:T], ps[0:36, 3, 0:LP]).then_inc(ro_lt, 1)
                dve.wait_ge(ro_lg, 1)
                step(V.tensor_tensor(lg[:, :, :], ps[:, 0, 0:NT * 36].rearrange("p (t n) -> p t n", t=NT),
                                     row(bcast[:, 4:40], NT), ALU.add))
                lc, lf = lg[:, :, 0:NG], lg[:, :, NG:36]
                step(V.tensor_reduce(gmax[:, :], lc, AX.X, ALU.max))
                V.tensor_tensor(gt[:, :, :], lc, bc(gmax[:, :], NG), ALU.subtract).then_inc(ro_sub, 1)
                step(V.tensor_tensor(goh[:, :, :], lc, bc(gmax[:, :], NG), ALU.is_lt))
                step(V.scalar_tensor_tensor(out=goh[:, :, :], in0=goh[:, :, :], scalar=1000.0, in1=row(iota[:, 0:NG], NT),
                                            op0=ALU.mult, op1=ALU.add))
                step(V.tensor_reduce(gidx[:, :], goh[:, :, :], AX.X, ALU.min))
                step(V.tensor_tensor(goh[:, :, :], row(iota[:, 0:NG], NT), bc(gidx[:, :], NG), ALU.is_equal))
                step(V.tensor_scalar(goh[:, :, :], goh[:, :, :], -1.0, 1e30, ALU.add, ALU.mult))
                for g in range(NG):
                    last = V.tensor_tensor(lfm[:, :, g * EPG:(g + 1) * EPG], lf[:, :, g * EPG:(g + 1) * EPG],
                                           goh[:, :, g:g + 1].to_broadcast([P, NT, EPG]), ALU.add)
                step(last)
                for q in range(2):
                    step(V.tensor_reduce(top[q][:, :], lfm[:, :, :], AX.X, ALU.max))
                    step(V.tensor_tensor(lt[:, :, :], lfm[:, :, :], bc(top[q][:, :], NE), ALU.is_lt))
                    step(V.scalar_tensor_tensor(out=lt[:, :, :], in0=lt[:, :, :], scalar=1000.0, in1=row(iota[:, 0:NE], NT),
                                                op0=ALU.mult, op1=ALU.add))
                    step(V.tensor_reduce(tidx[:, :], lt[:, :, :], AX.X, ALU.min))
                    step(V.tensor_tensor(oh[q][:, :, :], row(iota[:, 0:NE], NT), bc(tidx[:, :], NE), ALU.is_equal))
                    if q == 0:
                        step(V.scalar_tensor_tensor(out=lfm[:, :, :], in0=oh[0][:, :, :], scalar=-3e30, in1=lfm[:, :, :],
                                                    op0=ALU.mult, op1=ALU.add))
                step(V.tensor_tensor(both[:, 0:NT, :], oh[0][:, :, :], oh[1][:, :, :], ALU.add))
                V.tensor_copy(before[:, 1, :], both[:, 0, :])
                step(V.tensor_tensor(before[:, 2, :], both[:, 0, :], both[:, 1, :], ALU.add))
                for t in range(2, NT - 1):
                    step(V.tensor_tensor(before[:, t + 1, :], before[:, t, :], both[:, t, :], ALU.add))
                V.tensor_tensor(before[:, NT, :], before[:, NT - 1, :], both[:, NT - 1, :], ALU.add).then_inc(ro_oh, 1)
                V.tensor_tensor(ediff[:, :], top[1][:, :], top[0][:, :], ALU.subtract).then_inc(ro_sub2, 1)
                V.tensor_scalar(thr[:, :], iota[:, 0:NTHR], float(BR), None, ALU.mult)
                dve.wait_ge(ro_rank, 1)
                V.tensor_copy(rank[:, :, :], ps[:, 3, 0:NT * NE].rearrange("p (t n) -> p t n", t=NT))
                step(V.tensor_copy(cnt[:, :], ps[:, 3, NT * NE:(NT + 1) * NE]))
                step(V.tensor_tensor(ebt[:, 0:NE, 0:NTHR], bc(cnt[:, :], NTHR), row(thr[:, :], NE), ALU.is_gt))
                step(V.tensor_reduce(nbl[:, :], ebt[:, 0:NE, 0:NTHR], AX.X, ALU.add))
                step(V.tensor_tensor_scan(out=cum[:, :], data0=ones[:, 0:NE], data1=nbl[:, :], initial=0.0,
                                          op0=ALU.mult, op1=ALU.add))
                step(V.tensor_tensor(exc[:, :], cum[:, :], nbl[:, :], ALU.subtract))
                step(V.tensor_tensor(ebt[:, :, :], row(cum[:, :], NBLK), bc(iota[:, 0:NBLK], NE), ALU.is_le))
                step(V.tensor_reduce(ebf[:, :], ebt[:, :, :], AX.X, ALU.add))
                V.tensor_scalar(ebi[:, :], ebf[:, :], float(NE - 1), None, ALU.min)
                step(V.tensor_scalar(nturn[:, 1:2], cum[:, NE - 1:NE], 1.0, None, ALU.add))
                V.tensor_scalar(nturn[:, 0:1], nturn[:, 1:2], 1, None, ALU.arith_shift_right).then_inc(ro_tab, 1)
                for q in range(2):
                    step(V.tensor_tensor(lt[:, :, :], oh[q][:, :, :], rank[:, :, :], ALU.mult))
                    step(V.tensor_reduce(selr[:, q, :], lt[:, :, :], AX.X, ALU.add))
                    step(V.tensor_tensor(lt[:, :, :], oh[q][:, :, :], row(exc[:, :], NT), ALU.mult))
                    step(V.tensor_reduce(sele[:, q, :], lt[:, :, :], AX.X, ALU.add))
                sr = selr[:, :, :].rearrange("p a b -> p (a b)")
                se = sele[:, :, :].rearrange("p a b -> p (a b)")
                fl = flo[:, :, :].rearrange("p a b -> p (a b)")
                ft = flt[:, :, :, :].rearrange("p a b c -> p (a b) c")
                step(V.tensor_tensor(ft, bc(sr, NTHR - 1), row(thr[:, 1:NTHR], 2 * NT), ALU.is_ge))
                step(V.tensor_reduce(fl, ft, AX.X, ALU.add))
                V.scalar_tensor_tensor(out=sr, in0=fl, scalar=-float(BR), in1=sr, op0=ALU.mult, op1=ALU.add)
                step(V.tensor_tensor(se, se, fl, ALU.add))
                V.tensor_tensor(ohb[:, :, :], row(iota[:, 0:NBLK + SLOTS], 2 * NT), bc(se, NBLK + SLOTS), ALU.is_equal)
                step(V.tensor_tensor(ohs[:, :, :], row(iota[:, 0:BR], 2 * NT), bc(sr, BR), ALU.is_equal))
                V.tensor_tensor(ohb[:, :, :], ohb[:, :, :], bc(iota[:, P:P + 2 * NT], NBLK + SLOTS), ALU.mult).then_inc(ro_1h, 1)
                dve.wait_ge(ro_tm, 1)
                step(V.tensor_scalar(tabz[0:BR, :], ps[0:BR, 2, 0:NBLK + SLOTS], 0.0, 8192.0, ALU.is_equal, ALU.mult))
                step(V.scalar_tensor_tensor(out=tabf[0:BR, :], in0=ps[0:BR, 2, 0:NBLK + SLOTS], scalar=-1.0, in1=tabz[0:BR, :],
                                            op0=ALU.add, op1=ALU.add))
                step(V.tensor_copy(tabs[0:BR, 1, :], tabf[0:BR, :]))
                V.tensor_scalar(tabs[0:BR, 0, :], tabs[0:BR, 1, :], 1, None, ALU.arith_shift_right).then_inc(ro_tok, 1)
                dve.wait_ge(ro_exp, 1)
                step(V.tensor_reduce(gsum[:, :], gexp[:, :, :], AX.X, ALU.add))
                dve.wait_ge(ro_exp2, 1)
                step(V.scalar_tensor_tensor(out=eden[:, :], in0=emx[:, :], scalar=1.0, in1=gsum[:, :], op0=ALU.add, op1=ALU.mult))
                step(V.reciprocal(wgt[0][:, :], eden[:, :]))
                step(V.tensor_tensor(wgt[1][:, :], wgt[0][:, :], emx[:, :], ALU.mult))
                for s in range(SLOTS):
                    dve.sem_inc(ye_d[s])
                turns = dve.value_load(nturn[0:1, 0:1], min_val=1, max_val=NBLK // 2)
                with dve.Fori(0, turns) as j:
                    for s in range(SLOTS):
                        dve.wait_ge(sg_ok[s], j + 1)
                        dve.wait_ge(u_mm[s], j + 1)
                        V.tensor_tensor(he[:, s, :, :].rearrange("p k t -> p (k t)"), sg[:, s, :], ps[:, 3, 0:2 * BR],
                                        ALU.mult).then_inc(he_ok[s], 1)
                        dve.wait_ge(y_mm[s], j * 2 + 3)
                        dve.wait_ge(y_out[s], j * 16 + 16)
                        V.tensor_copy(ye[0:BR, s, 512:1024], ps[0:BR, 7, :]).then_inc(ye_d[s], 1)
                for t in range(NT):
                    dve.wait_ge(yc_first, t + 1)
                    V.scalar_tensor_tensor(out=ysum[:, t % 2, :], in0=ycomb[:, t % 2, 1, :], scalar=wgt[1][:, t:t + 1],
                                           in1=ysum[:, t % 2, :], op0=ALU.mult, op1=ALU.add).then_inc(yc_sum, 1)
                    if t >= 1:
                        residual(t - 1)
                residual(NT - 1)
                last_of_layer(dve, "dve")
            for k in range(1, KC):
                add_square(k, sq0, ss0)
            chain[0] = 0
            normalise(rt0, xn0)


INPUTS = ("x_prompt x_sample cache_k cache_v c c_ctx ada_w ada_b norm1_g norm2_g w_in conv_dw_w conv_dw_b "
          "conv_ln_g conv_ln_b hy_short_w hy_short_b hy_fw1 hy_fb1 hy_freq1 hy_fw2 hy_fb2 hy_freq2 hy_fw3 hy_fb3 "
          "hy_d attn_sink w_out router_coarse_w router_coarse_b router_fine_w router_fine_b exp_gate exp_up "
          "exp_down norm_f_g").split()
OUTPUTS = {"y_prompt": (1, LP, D), "y_sample": (1, LS, D), "state_k": (1, DEPTH, LP, 2, HD),
           "state_v": (1, DEPTH, LP, 2, HD)}


def program(nc, arrays):
    io = {}
    for name, a in arrays.items():
        io[name] = nc.dram_tensor("in_" + name, a.shape, mybir.dt.from_np(a.dtype), kind="ExternalInput").ap()
    out = {n: nc.dram_tensor("out_" + n, s, F32, kind="ExternalOutput").ap() for n, s in OUTPUTS.items()}
    trunk(nc, io, out)


def kernel(**inputs):
    import concourse.bacc as bacc
    from concourse.bass_utils import run_bass_kernel_spmd

    arrays = {n: np.ascontiguousarray(inputs[n]) for n in INPUTS}
    arrays.update({"c_" + n: a for n, a in constants().items()})
    nc = bacc.Bacc("TRN2", target_bir_lowering=False, num_devices=1)
    program(nc, arrays)
    r = run_bass_kernel_spmd(nc, [{"in_" + n: a for n, a in arrays.items()}], core_ids=[0])
    return tuple(r.results[0]["out_" + n] for n in OUTPUTS)
```
